# Optimizing a Trainium2 kernel written in Bass

```python
import jax, jax.numpy as jnp
from jax import lax
import numpy as np

D_MODEL = 1024
BATCH = 1
SEQ = 1024
DEPTH = 2
DEC_BATCH = 8
DEC_SEQ = 1
PAST_LEN = 4096
PAGE_SIZE = 128

N_MIXERS = 2
N_CONV_LAYERS = (DEPTH + 1) // 2
N_ATTN_LAYERS = DEPTH // 2
CONV_WIDTH = 3
N_HEADS = 8
QK_NOPE_DIM = 128
QK_ROPE_DIM = 64
V_HEAD_DIM = 128
Q_LORA_RANK = 384
KV_LORA_RANK = 256
D_FF = 2816
ROPE_THETA = 10000.0
RMS_EPS = 1e-6
Q_BLOCK = 128
N_MOD = 6
ATTN_SCALE = (QK_NOPE_DIM + QK_ROPE_DIM) ** -0.5

kernel_name = 'hybrid_shortconv_mla_convffn_step'

def rmsnorm(x, g):
    xf = x.astype(jnp.float32)
    y = xf * lax.rsqrt(jnp.mean(xf * xf, axis=-1, keepdims=True) + RMS_EPS)
    return (y * g.astype(jnp.float32)).astype(x.dtype)

def rope(x, pos):
    half = QK_ROPE_DIM // 2
    inv = ROPE_THETA ** (-jnp.arange(half, dtype=jnp.float32) * 2.0 / QK_ROPE_DIM)
    ang = pos.astype(jnp.float32)[:, None] * inv[None, :]
    ang = ang.reshape((ang.shape[0],) + (1,) * (x.ndim - 3) + (half,))
    cos, sin = jnp.cos(ang), jnp.sin(ang)
    xf = x.astype(jnp.float32)
    x1, x2 = xf[..., :half], xf[..., half:]
    return jnp.concatenate([x1 * cos - x2 * sin, x2 * cos + x1 * sin], axis=-1).astype(x.dtype)

def causal_dwconv(x, prev, w):
    T = x.shape[1]
    xp = jnp.concatenate([prev.astype(x.dtype), x], axis=1)
    y = xp[:, 0:T] * w[0]
    for k in range(1, CONV_WIDTH):
        y = y + xp[:, k:k + T] * w[k]
    return y, xp[:, T:]

def short_conv_mixer(h, prev, w_in, conv_w, w_out):
    b_gate, c_gate, v = jnp.split(h @ w_in, 3, axis=-1)
    y, buf = causal_dwconv(c_gate * v, prev, conv_w)
    return (b_gate * y) @ w_out, buf

def conv_ffn(h, prev, w_in, conv_w, conv_b, w_out):
    a, v = jnp.split(h @ w_in, 2, axis=-1)
    a, buf = causal_dwconv(a, prev, conv_w)
    return (jax.nn.silu(a + conv_b) * v) @ w_out, buf

def mla_attend_block(q_lat, q_pe, kv_lat, k_pe, q_pos, k_pos):
    s = (jnp.einsum('bthc,bsc->bhts', q_lat, kv_lat, preferred_element_type=jnp.float32)
         + jnp.einsum('bthr,bsr->bhts', q_pe, k_pe, preferred_element_type=jnp.float32)) * ATTN_SCALE
    mask = k_pos[None, :] <= q_pos[:, None]
    s = jnp.where(mask[None, None], s, jnp.finfo(jnp.float32).min)
    p = jax.nn.softmax(s, axis=-1).astype(kv_lat.dtype)
    return jnp.einsum('bhts,bsc->bthc', p, kv_lat)

def mla_attend(q_lat, q_pe, kv_lat, k_pe, q_pos, k_pos):
    B, T = q_lat.shape[0], q_lat.shape[1]
    qb = Q_BLOCK if T % Q_BLOCK == 0 else T
    nb = T // qb
    if nb == 1:
        return mla_attend_block(q_lat, q_pe, kv_lat, k_pe, q_pos, k_pos)

    def split(a):
        return a.reshape((B, nb, qb) + a.shape[2:]).swapaxes(0, 1)

    out = lax.map(lambda a: mla_attend_block(a[0], a[1], kv_lat, k_pe, a[2], k_pos),
                  (split(q_lat), split(q_pe), q_pos.reshape(nb, qb)))
    return out.swapaxes(0, 1).reshape((B, T) + out.shape[3:])

def mla_mixer(h, pos, past_lat, past_pe, w_qa, qa_norm, w_qb, w_kva, kv_norm, w_kvb, w_o):
    B, T, _ = h.shape
    q = (rmsnorm(h @ w_qa, qa_norm) @ w_qb).reshape(B, T, N_HEADS, QK_NOPE_DIM + QK_ROPE_DIM)
    q_nope, q_pe = q[..., :QK_NOPE_DIM], rope(q[..., QK_NOPE_DIM:], pos)
    kv = h @ w_kva
    lat = rmsnorm(kv[..., :KV_LORA_RANK], kv_norm)
    pe = rope(kv[..., KV_LORA_RANK:], pos)
    w_kvb_h = w_kvb.reshape(KV_LORA_RANK, N_HEADS, QK_NOPE_DIM + V_HEAD_DIM)
    q_lat = jnp.einsum('bthn,chn->bthc', q_nope, w_kvb_h[..., :QK_NOPE_DIM])
    if past_lat is None:
        keys_lat, keys_pe = lat, pe
    else:
        keys_lat = jnp.concatenate([past_lat.astype(lat.dtype), lat], axis=1)
        keys_pe = jnp.concatenate([past_pe.astype(pe.dtype), pe], axis=1)
    k_pos = jnp.arange(keys_lat.shape[1], dtype=jnp.int32)
    o_lat = mla_attend(q_lat, q_pe, keys_lat, keys_pe, pos, k_pos)
    o = jnp.einsum('bthc,chv->bthv', o_lat, w_kvb_h[..., QK_NOPE_DIM:]).reshape(B, T, N_HEADS * V_HEAD_DIM)
    return o @ w_o, lat, pe

def trunk(x, c, pos, mix_prev, ffn_prev, attn_past, p):
    B = x.shape[0]
    new_lat, new_pe, new_mix, new_ffn = [], [], [], []
    for i in range(DEPTH):
        j = i // N_MIXERS
        m = (jax.nn.silu(c) @ p['mod_w'][i] + p['mod_b'][i]).reshape(B, 1, N_MOD, D_MODEL)
        sh1, sc1, g1, sh2, sc2, g2 = (m[:, :, k] for k in range(N_MOD))
        h = rmsnorm(x, p['norm_mix_pre'][i]) * (1 + sc1) + sh1
        if i % N_MIXERS == 0:
            o, buf = short_conv_mixer(h, mix_prev[j], p['sc_w_in'][j], p['sc_conv_w'][j], p['sc_w_out'][j])
            new_mix.append(buf)
        else:
            if attn_past is None:
                past_lat, past_pe = None, None
            else:
                cache_lat, cache_pe, page_table = attn_past
                past_lat = cache_lat[j, page_table].reshape(B, -1, KV_LORA_RANK)
                past_pe = cache_pe[j, page_table].reshape(B, -1, QK_ROPE_DIM)
            o, lat, pe = mla_mixer(h, pos, past_lat, past_pe, p['mla_w_qa'][j], p['mla_qa_norm'][j],
                                   p['mla_w_qb'][j], p['mla_w_kva'][j], p['mla_kv_norm'][j],
                                   p['mla_w_kvb'][j], p['mla_w_o'][j])
            new_lat.append(lat)
            new_pe.append(pe)
        x = x + g1 * rmsnorm(o, p['norm_mix_post'][i])
        h = rmsnorm(x, p['norm_ffn_pre'][i]) * (1 + sc2) + sh2
        o, buf = conv_ffn(h, ffn_prev[i], p['ffn_w_in'][i], p['ffn_conv_w'][i], p['ffn_conv_b'][i], p['ffn_w_out'][i])
        new_ffn.append(buf)
        x = x + g2 * rmsnorm(o, p['norm_ffn_post'][i])
    return x, jnp.stack(new_lat), jnp.stack(new_pe), jnp.stack(new_mix), jnp.stack(new_ffn)

def setup_inputs(seed: int = 0) -> dict:
    key = jax.random.key(seed)
    ks = iter(jax.random.split(key, 40))
    f32 = jnp.float32

    def nrm(shape, scale=1.0):
        return jax.random.normal(next(ks), shape, f32) * scale

    n_pages = PAST_LEN // PAGE_SIZE
    n_used = DEC_BATCH * n_pages
    n_pool = n_used + n_used // 4
    page_table = jax.random.permutation(next(ks), n_pool)[:n_used].reshape(DEC_BATCH, n_pages).astype(jnp.int32)
    dq = N_HEADS * (QK_NOPE_DIM + QK_ROPE_DIM)
    dkv = N_HEADS * (QK_NOPE_DIM + V_HEAD_DIM)
    return {
        'x_prompt': nrm((BATCH, SEQ, D_MODEL)),
        'x_sample': nrm((DEC_BATCH, DEC_SEQ, D_MODEL)),
        'cache_kv_latent': nrm((N_ATTN_LAYERS, n_pool, PAGE_SIZE, KV_LORA_RANK)),
        'cache_k_rope': nrm((N_ATTN_LAYERS, n_pool, PAGE_SIZE, QK_ROPE_DIM)),
        'state_mixconv': nrm((N_CONV_LAYERS, DEC_BATCH, CONV_WIDTH - 1, D_MODEL)),
        'state_ffnconv': nrm((DEPTH, DEC_BATCH, CONV_WIDTH - 1, D_FF)),
        'page_table': page_table,
        'c_prompt': nrm((BATCH, D_MODEL)),
        'c_sample': nrm((DEC_BATCH, D_MODEL)),
        'mod_w': nrm((DEPTH, D_MODEL, N_MOD * D_MODEL), 0.5 * D_MODEL ** -0.5),
        'mod_b': nrm((DEPTH, N_MOD * D_MODEL), 0.02),
        'norm_mix_pre': 1.0 + nrm((DEPTH, D_MODEL), 0.02),
        'norm_mix_post': 1.0 + nrm((DEPTH, D_MODEL), 0.02),
        'norm_ffn_pre': 1.0 + nrm((DEPTH, D_MODEL), 0.02),
        'norm_ffn_post': 1.0 + nrm((DEPTH, D_MODEL), 0.02),
        'sc_w_in': nrm((N_CONV_LAYERS, D_MODEL, 3 * D_MODEL), D_MODEL ** -0.5),
        'sc_conv_w': nrm((N_CONV_LAYERS, CONV_WIDTH, D_MODEL), CONV_WIDTH ** -0.5),
        'sc_w_out': nrm((N_CONV_LAYERS, D_MODEL, D_MODEL), D_MODEL ** -0.5),
        'mla_w_qa': nrm((N_ATTN_LAYERS, D_MODEL, Q_LORA_RANK), D_MODEL ** -0.5),
        'mla_qa_norm': 1.0 + nrm((N_ATTN_LAYERS, Q_LORA_RANK), 0.02),
        'mla_w_qb': nrm((N_ATTN_LAYERS, Q_LORA_RANK, dq), Q_LORA_RANK ** -0.5),
        'mla_w_kva': nrm((N_ATTN_LAYERS, D_MODEL, KV_LORA_RANK + QK_ROPE_DIM), D_MODEL ** -0.5),
        'mla_kv_norm': 1.0 + nrm((N_ATTN_LAYERS, KV_LORA_RANK), 0.02),
        'mla_w_kvb': nrm((N_ATTN_LAYERS, KV_LORA_RANK, dkv), KV_LORA_RANK ** -0.5),
        'mla_w_o': nrm((N_ATTN_LAYERS, N_HEADS * V_HEAD_DIM, D_MODEL), (N_HEADS * V_HEAD_DIM) ** -0.5),
        'ffn_w_in': nrm((DEPTH, D_MODEL, 2 * D_FF), D_MODEL ** -0.5),
        'ffn_conv_w': nrm((DEPTH, CONV_WIDTH, D_FF), CONV_WIDTH ** -0.5),
        'ffn_conv_b': nrm((DEPTH, D_FF), 0.02),
        'ffn_w_out': nrm((DEPTH, D_FF, D_MODEL), D_FF ** -0.5),
    }

def reference(x_prompt, x_sample, cache_kv_latent, cache_k_rope, state_mixconv, state_ffnconv, page_table,
              c_prompt, c_sample, mod_w, mod_b, norm_mix_pre, norm_mix_post, norm_ffn_pre, norm_ffn_post,
              sc_w_in, sc_conv_w, sc_w_out, mla_w_qa, mla_qa_norm, mla_w_qb, mla_w_kva, mla_kv_norm,
              mla_w_kvb, mla_w_o, ffn_w_in, ffn_conv_w, ffn_conv_b, ffn_w_out):
    p = {'mod_w': mod_w, 'mod_b': mod_b, 'norm_mix_pre': norm_mix_pre, 'norm_mix_post': norm_mix_post,
         'norm_ffn_pre': norm_ffn_pre, 'norm_ffn_post': norm_ffn_post, 'sc_w_in': sc_w_in,
         'sc_conv_w': sc_conv_w, 'sc_w_out': sc_w_out, 'mla_w_qa': mla_w_qa, 'mla_qa_norm': mla_qa_norm,
         'mla_w_qb': mla_w_qb, 'mla_w_kva': mla_w_kva, 'mla_kv_norm': mla_kv_norm, 'mla_w_kvb': mla_w_kvb,
         'mla_w_o': mla_w_o, 'ffn_w_in': ffn_w_in, 'ffn_conv_w': ffn_conv_w, 'ffn_conv_b': ffn_conv_b,
         'ffn_w_out': ffn_w_out}
    B, S = x_prompt.shape[0], x_prompt.shape[1]
    pos_p = jnp.arange(S, dtype=jnp.int32)
    mix0 = jnp.zeros((N_CONV_LAYERS, B, CONV_WIDTH - 1, D_MODEL), x_prompt.dtype)
    ffn0 = jnp.zeros((DEPTH, B, CONV_WIDTH - 1, D_FF), x_prompt.dtype)
    y_prompt, lat_p, pe_p, mix_p, ffn_p = trunk(x_prompt, c_prompt, pos_p, mix0, ffn0, None, p)
    past_len = page_table.shape[1] * cache_kv_latent.shape[2]
    pos_s = past_len + jnp.arange(x_sample.shape[1], dtype=jnp.int32)
    y_sample, lat_s, pe_s, mix_s, ffn_s = trunk(x_sample, c_sample, pos_s, state_mixconv, state_ffnconv,
                                                (cache_kv_latent, cache_k_rope, page_table), p)
    return (y_prompt, y_sample, lat_p, pe_p, lat_s, pe_s, mix_p, mix_s, ffn_p, ffn_s)


_drawn_inputs = setup_inputs


def setup_inputs(seed=0):
    import zlib

    import numpy as np

    out = dict(_drawn_inputs(seed))
    spreads = {}
    factors = {'norm_mix_post': 7.378,
     'norm_ffn_pre': 2.897,
     'norm_ffn_post': 7.589,
     'mla_qa_norm': 8.0,
     'mla_kv_norm': 3.154,
     'ffn_conv_b': 7.785}
    for name, (base, spread) in spreads.items():
        noise = np.random.default_rng([zlib.crc32(name.encode()), seed]).standard_normal(out[name].shape)
        drawn = base * np.exp(spread * noise) if base else spread * noise
        out[name] = __import__('jax').numpy.asarray(drawn.astype(out[name].dtype))
    for name, factor in factors.items():
        out[name] = (out[name] * factor).astype(out[name].dtype)
    return out
```

```python
from contextlib import ExitStack, contextmanager

import numpy as np

import concourse.bass as bass
from concourse import mybir

F32 = mybir.dt.float32
F32R = mybir.dt.float32r
BF16 = mybir.dt.bfloat16
I32 = mybir.dt.int32
ALU = mybir.AluOpType
ACT = mybir.ActivationFunctionType
AX = mybir.AxisListType

P = 128
D = 1024
KD = D // P
TP = 1024
NS = 8
T = TP + NS
KT_TOK = TP // P
F = 2816
KF = F // P
UC, NU = T // 3, 3
DC, ND = T // 4, 4
PL = TP - (ND - 1) * DC
H = 8
DN, DR, DV = 128, 64, 128
QR, KR = 384, 256
KQ, KC = QR // P, KR // P
PAGE = 128
NPG = 32
PAST = PAGE * NPG
EPS = 1e-6
SCALE = float(DN + DR) ** -0.5
NEG = -1e30
TAIL = 2 + NS
MODS = 6
MLANES = 1 + NS
MB = 512


class Tally:

    def __init__(self, n=0):
        self.n, self.loops = n, []

    def __call__(self, more=0):
        value = self.n + more
        for i, per in self.loops:
            value = i * per + value
        return value

    def add(self, k=1):
        self.n += k


def wait(eng, sem, value):
    if isinstance(value, int) and value <= 0:
        return
    eng.wait_ge(sem, value)


@contextmanager
def loop(eng, trips, per):
    entry = {t: t.n for t in per}
    with eng.Fori(0, trips) as i:
        for t, k in per.items():
            t.loops.append((i, k))
        yield i
    for t, k in per.items():
        assert t.n - entry[t] == k, (t.n - entry[t], k)
        t.n += (trips - 1) * k
        t.loops.pop()


def build(nc, ins, outs):
    (x_prompt, x_sample, cache_lat, cache_pe, state_mix, state_ffn, page_table, c_prompt, c_sample, mod_w, mod_b,
     n_mix_pre, n_mix_post, n_ffn_pre, n_ffn_post, sc_w_in, sc_conv_w, sc_w_out, w_qa, qa_norm, w_qb, w_kva,
     kv_norm, w_kvb, w_o, ffn_w_in, ffn_conv_w, ffn_conv_b, ffn_w_out, rope_tab) = ins
    (y_prompt, y_sample, lat_p, pe_p, lat_s, pe_s, mix_p, mix_s, ffn_p, ffn_s) = outs

    mid_d = nc.dram_tensor("mid_d", (F, T), F32).ap()
    snew_d = nc.dram_tensor("snew_d", (NS, NS * H), F32).ap()

    base = (nc.sbuf_base + 63) // 64 * 64
    room = [base]

    def arena(size):
        at = room[0]
        room[0] += (size + 31) // 32 * 32
        return at

    names = set()

    def at(name, shape, off, dt=F32):
        assert name not in names
        names.add(name)
        return nc.alloc_sbuf_tensor_at(name, shape, dt, offset=off, align_bytes=8)

    T4, D4 = T * 4, DC * 4
    A_X = arena(KD * T4)
    A_H = arena(2 * KD * T4)
    A_W = arena(9 * KD * P * 4)
    A_A = arena(2 * KF * D4)
    A_O = arena(2 * KD * D4)
    A_S = arena(2 * D4)
    A_C = arena(12 * 1024)
    assert room[0] <= nc.sbuf_usable_end, (room[0], nc.sbuf_usable_end)

    xT = at("xT", [P, KD, T], A_X)
    h_hi = at("h_hi", [P, KD, T], A_H, F32R)
    h_lo = at("h_lo", [P, KD, T], A_H + KD * T4, F32R)
    WB = KD * P * 4
    w_raw = [at(f"w_raw{s}", [P, KD, P], A_W + s * WB) for s in range(3)]
    w_hi = [at(f"w_hi{s}", [P, KD, P], A_W + (3 + s) * WB, F32R) for s in range(3)]
    w_lo = [at(f"w_lo{s}", [P, KD, P], A_W + (6 + s) * WB, F32R) for s in range(3)]
    act_hi = at("act_hi", [P, KF, DC], A_A, F32R)
    act_lo = at("act_lo", [P, KF, DC], A_A + KF * D4, F32R)
    stage = [at(f"stage{i}", [P, DC], A_S + i * D4) for i in range(2)]
    o_sb = at("o_sb", [P, KD, DC], A_O)
    sq = at("sq", [P, KD, DC], A_O + KD * D4)
    c0 = [A_C]

    def small(name, shape, dt=F32):
        n = int(np.prod(shape[1:])) * (2 if dt == BF16 else 4)
        off = c0[0]
        c0[0] += (n + 31) // 32 * 32
        assert c0[0] <= A_C + 12 * 1024, name
        return at(name, shape, off, dt)

    modv = small("modv", [P, 2 * MODS * KD, MLANES])
    vec = small("vec", [P, 4, P])
    ident = small("ident", [P, P])
    ones = small("ones", [P, P])
    ident_b = small("ident_b", [P, P], BF16)
    mask_b = small("mask_b", [P, P], BF16)
    prev_mix = small("prev_mix", [P, KD, NS])
    prev_ffn = small("prev_ffn", [P, 2, KF, NS])
    rs = small("rs", [P, DC])
    var, root_b = small("var", [P, DC]), small("root_b", [P, DC])
    tmp_s = small("tmp_s", [P, KD, NS])
    VA, VB = vec[:, 0, :], vec[:, 1, :]
    v_modb, v_scw, v_qan, v_kvn = VA[:, 0:96], VA[:, 96:120], VA[:, 120:123], VA[:, 123:125]
    v_norm = VB[:, 0:64]
    v_cb = VB[:, 64:108]

    x_in = at("x_in", [P, KT_TOK, D], A_H)
    mod_raw = [at(f"mod_raw{b}", [P, KD, MB], A_H + KT_TOK * D * 4 + b * KD * MB * 4) for b in range(2)]
    off = A_A
    xs_in = at("xs_in", [NS, D], off); off += D * 4
    c_in = at("c_in", [MLANES, D], off); off += D * 4
    packs = at("packs", [P, 4, P], off); off += 4 * P * 4
    mix_in = at("mix_in", [2 * NS, D], off); off += D * 4
    ffn_in = at("ffn_in", [2 * NS, 2, F], off); off += 2 * F * 4
    assert off <= A_S
    csil = at("csil", [MLANES, D], A_O)
    csT = at("csT", [P, KD, MLANES], A_O + D * 4)
    ptmp = at("ptmp", [P, KF, NS], A_O + D * 4 + 512)
    off = A_A
    a_sb = at("a_sb", [P, 2 + T], off); off += (2 + T) * 4 + 24
    y_sb = at("y_sb", [P, T], off); off += T4
    g_sb = at("g_sb", [P, T], off); off += T4
    tail = at("tail", [P, KF, TAIL], off); off += KF * TAIL * 4 + 16
    tail_t = at("tail_t", [TAIL, F], off); off += F * 4
    assert off <= A_S
    off = A_A
    q_raw = at("q_raw", [P, KQ, T], off); off += KQ * T4
    l_raw = at("l_raw", [P, KC, T], off); off += KC * T4
    tab = at("tab", [P, T], off); off += T4
    p_t = at("p_t", [P, KT_TOK, 512], off); off += KT_TOK * 2048
    kvb = at("kvb", [P, KC, DN + DV], off); off += KC * (DN + DV) * 4
    assert off <= A_S
    tok = [at(f"tok{i}", [P, KR + DR], A_A + i * 1280) for i in range(2)]
    off = A_H
    qn_hi = at("qn_hi", [P, KQ, T], off, F32R); off += KQ * T4
    qn_lo = at("qn_lo", [P, KQ, T], off, F32R); off += KQ * T4
    latn = at("latn", [P, KC, T], off); off += KC * T4
    kpe = at("kpe", [DR, T], off); off += T4
    qno = at("qno", [P, T], off); off += T4
    qpe = at("qpe", [DR, T], off); off += T4
    kno = at("kno", [P, TP], off); off += TP * 4
    v_sb = at("v_sb", [P, KT_TOK, P], off); off += KT_TOK * P * 4
    p_sb = [at(f"p_sb{i}", [P, TP], off + i * TP * 4) for i in range(2)]; off += 2 * TP * 4
    wkT = at("wkT", [P, KC, P], off); off += KC * P * 4
    assert off <= A_W
    sqm = at("sqm", [P, KQ, T], A_O)
    rsm = at("rsm", [P, T], A_O + KQ * T4)
    varm = at("varm", [P, T], A_H + 2 * KQ * T4 + KC * T4 + T4)
    rootm = at("rootm", [P, T], A_H + 2 * KQ * T4 + KC * T4 + 2 * T4)
    off = A_O
    oh = [at(f"oh{i}", [P, 512], off + i * 2048) for i in range(2)]; off += 4096
    rope1 = at("rope1", [DR, T], off); off += T4
    st = at("st", [P, 8, 2], off); off += 64
    qlat = at("qlat", [P, KC, NS, H], off); off += KC * 256
    qpes = at("qpes", [DR, NS, H], off); off += 256
    lats = at("lats", [P, KC, NS], off); off += KC * 32
    kpes = at("kpes", [DR, NS], off); off += 32
    sx = at("sx", [NS, NS * H], off); off += 256
    olat = at("olat", [P, KC, H, NS], off); off += KC * 256
    ovs = at("ovs", [P, H, NS], off); off += 256
    dm = at("dm", [P, 8 * 6], off); off += 192
    ptab = at("ptab", [1, NS * NPG], off, I32); off += NS * NPG * 4
    assert off <= A_S
    pg = [at(f"pg{i}", [P, NPG, KR], A_H + i * NPG * KR * 4) for i in range(2)]
    off = A_A
    pgr = [at(f"pgr{i}", [P, NPG, DR], off + i * NPG * DR * 4) for i in range(2)]; off += 2 * NPG * DR * 4
    kT = [at(f"kT{i}", [P, 3, 512], off + i * 6144) for i in range(2)]; off += 2 * 6144
    s_sb = [at(f"s_sb{i}", [P, NPG + 1, H], off + i * 1056) for i in range(2)]; off += 2112
    e_sb = [at(f"e_sb{i}", [P, NPG + 1, H], off + i * 1056) for i in range(2)]; off += 2112
    vnew = [at(f"vnew{i}", [1, KR], off + i * 1024) for i in range(2)]; off += 2048
    assert off <= A_S
    y_tok = [at(f"y_tok{i}", [P, D], A_H + i * D * 4) for i in range(2)]
    wv = at("wv", [P, KC, H, DV], A_A)

    with ExitStack() as ctx:
        ps = ctx.enter_context(nc.psum_tensor("ps", [P, 8, 512], F32))

        def bank(b):
            return ps[:, b, :]

        def upset(s):
            return ps[:, 3 * s:3 * s + NU, 0:UC]

        def chunked(ap):
            return ap.rearrange("p (c n) -> p c n", c=NU)

        def sem(name):
            return ctx.enter_context(nc.semaphore(name))

        const_ready = sem("const_ready")
        vec_in, c_loaded, mix_loaded, ffn_loaded = sem("vec_in"), sem("c_loaded"), sem("mix_loaded"), sem("ffn_loaded")
        x_loaded, xs_loaded, state_out = sem("x_loaded"), sem("xs_loaded"), sem("state_out")
        csil_ready = sem("csil_ready")
        setup_t, setup_e = sem("setup_t"), sem("setup_e")
        xt_t, xt_e = sem("xt_t"), sem("xt_e")
        mod_loaded = [sem("mod_loaded0"), sem("mod_loaded1")]
        mod_mm, mod_done = sem("mod_mm"), sem("mod_done")
        raw_ready = [sem(f"raw_ready{s}") for s in range(3)]
        hi_ready = [sem(f"hi_ready{s}") for s in range(3)]
        w_ready = [sem(f"w_ready{s}") for s in range(3)]
        w_done = [sem(f"w_done{s}") for s in range(3)]
        set_free = [sem("set_free0"), sem("set_free1")]
        conv_done, act_done, g_ready, g_out = sem("conv_done"), sem("act_done"), sem("g_ready"), sem("g_out")
        tail_ready, tail_t_done, tail_e, tail_out = sem("tail_ready"), sem("tail_t_done"), sem("tail_e"), sem("tail_out")
        st_ready = [sem("st_ready0"), sem("st_ready1")]
        ah_ready, act_ready = sem("ah_ready"), sem("act_ready")
        var_ready, root_ready = sem("var_ready"), sem("root_ready")
        sq_ready, ss_ready, stat_ready = sem("sq_ready"), sem("ss_ready"), sem("stat_ready")
        x_done, t_ready, hh_ready, h_ready = sem("x_done"), sem("t_ready"), sem("hh_ready"), sem("h_ready")
        dve_step, act_step = sem("dve_step"), sem("act_step")
        tab_in, kvb_in = sem("tab_in"), sem("kvb_in")
        qn_r, lat_r, kpe_r = sem("qn_r"), sem("lat_r"), sem("kpe_r")
        qn_t = sem("qn_t")
        tok_t, tok_e, tok_out = sem("tok_t"), sem("tok_e"), [sem("tok_out0"), sem("tok_out1")]
        qpe_r, qlat_r = sem("qpe_r"), sem("qlat_r")
        kv_mm, kv_e = sem("kv_mm"), sem("kv_e")
        s_mm, nm_ready, e_ready, p_ready = sem("s_mm"), sem("nm_ready"), sem("e_ready"), sem("p_ready")
        p_t_mm, p_t_e, pv_mm, pv_e = sem("p_t_mm"), sem("p_t_e"), sem("pv_mm"), sem("pv_e")
        head_out = [sem("head_out0"), sem("head_out1")]
        sn_c, sn_mm, sn_e, sn_out, pt_in = sem("sn_c"), sem("sn_mm"), sem("sn_e"), sem("sn_out"), sem("pt_in")
        pg_in, vn_in = [sem("pg_in0"), sem("pg_in1")], [sem("vn_in0"), sem("vn_in1")]
        kt_mm, kt_ea, kt_ed, sc_mm = sem("kt_mm"), sem("kt_ea"), sem("kt_ed"), sem("sc_mm")
        ch_pe, ch_dve, ch_act, dpv, olat_r = sem("ch_pe"), sem("ch_dve"), sem("ch_act"), sem("dpv"), sem("olat_r")
        neg_ready, wv_in, ov_mm, ov_e, ov_out = (sem("neg_ready"), sem("wv_in"), sem("ov_mm"), sem("ov_e"),
                                                 sem("ov_out"))
        yt_mm, yt_e, y_out = sem("yt_mm"), sem("yt_e"), [sem("y_out0"), sem("y_out1")]

        SETS = 3 * KD // 2 + KF
        NORMS = ND + 4 * ND
        PARTS8 = [(0, 0, 4), (1, 4, 8)]
        PARTS22 = [(0, 0, 8), (1, 8, 16), (2, 16, 22)]

        def block_cols(w, c):
            return w[:, bass.ds(c, P)].rearrange("(k p) m -> p k m", p=P)

        block = ctx.enter_context(nc.Block())

        @block.sync
        def _(sp):
            raws = [Tally() for _ in range(3)]

            def load(slot, dst, src):
                wait(sp, w_ready[slot], raws[slot]())
                sp.dma_start(dst, src).then_inc(raw_ready[slot], 16)
                raws[slot].add()

            def load_block(slot, w, c):
                load(slot, w_raw[slot][:], block_cols(w, c))

            def vrows(t, r0, src):
                sp.dma_start(packs[r0:r0 + src.shape[0], t, :], src).then_inc(vec_in, 16)

            sp.dma_start(c_in[0:1, :], c_prompt).then_inc(c_loaded, 16)
            sp.dma_start(c_in[1:MLANES, :], c_sample).then_inc(c_loaded, 16)
            vrows(0, 0, mod_b.rearrange("l (m p) -> (l m) p", p=P))
            vrows(0, 96, sc_conv_w.rearrange("k (m p) -> (k m) p", p=P))
            vrows(0, 120, qa_norm.rearrange("l (m p) -> (l m) p", p=P))
            vrows(0, 123, kv_norm.rearrange("l (m p) -> (l m) p", p=P))
            for n, v in enumerate((n_mix_pre, n_mix_post, n_ffn_pre, n_ffn_post)):
                vrows(1, 16 * n, v.rearrange("l (m p) -> (l m) p", p=P))
            vrows(1, 64, ffn_conv_b.rearrange("l (m p) -> (l m) p", p=P))
            for l in range(2):
                vrows(2 + l, 0, ffn_conv_w[l].rearrange("k (m p) -> (k m) p", p=P))
            sp.dma_start(mix_in[:], state_mix.rearrange("b k d -> (b k) d")).then_inc(mix_loaded, 16)
            sp.dma_start(ffn_in[:], state_ffn.rearrange("l b k d -> (b k) l d")).then_inc(ffn_loaded, 16)
            sp.dma_start(x_in[:], x_prompt.rearrange("(t p) d -> p t d", p=P)).then_inc(x_loaded, 16)
            sp.dma_start(xs_in[:], x_sample).then_inc(xs_loaded, 16)
            mods = Tally(1)
            for l in range(2):
                with loop(sp, MODS, {mods: 2}) as i:
                    for b in range(2):
                        c = sp.snap(i * (2 * MB) + b * MB)
                        sp.wait_ge(mod_mm, mods())
                        mods.add()
                        sp.dma_start(mod_raw[b][:], mod_w[l][:, bass.ds(c, MB)].rearrange("(k p) m -> p k m", p=P)
                                     ).then_inc(mod_loaded[b], 16)
            for s, c in ((0, D), (1, 2 * D), (2, 0)):
                load(s, w_raw[s][:], block_cols(sc_w_in, c))
            with loop(sp, KD - 1, {raws[0]: 1, raws[1]: 1, raws[2]: 1}) as i:
                for s, c in ((0, D), (1, 2 * D), (2, 0)):
                    cc = sp.snap(i * P + (c + P))
                    load_block(s, sc_w_in, cc)

            def loads_down(w, parts):
                src = w.rearrange("(k p) m -> p k m", p=P)
                with loop(sp, ND, {raws[s]: KD for s, _, _ in parts}):
                    for m in range(KD):
                        for s, k0, k1 in parts:
                            load(s, w_raw[s][:, 0:k1 - k0, :], src[:, k0:k1, m * P:(m + 1) * P])

            def loads_ffn(l):
                with loop(sp, KF, {raws[0]: 1, raws[1]: 1}) as i:
                    for s in range(2):
                        cc = sp.snap(i * P + s * F)
                        load_block(s, ffn_w_in[l], cc)
                loads_down(ffn_w_out[l], PARTS22)

            loads_down(sc_w_out, PARTS8)
            loads_ffn(0)
            for m in range(KQ):
                load(m, w_raw[m][:], block_cols(w_qa, m * P))
            for m in range(KC):
                load(m, w_raw[m][:], block_cols(w_kva, m * P))
            src = w_kva.rearrange("(k p) m -> p k m", p=P)
            wait(sp, w_ready[2], raws[2]())
            for d0, c, n in ((0, KR, DR), (DR, KR + DR // 2, DR // 2), (DR + DR // 2, KR, DR // 2)):
                sp.dma_start(w_raw[2][:, :, d0:d0 + n], src[:, :, c:c + n]).then_inc(raw_ready[2], 16)
            raws[2].add()
            wait(sp, w_done[2], raws[2](-2))
            sp.dma_start(tab[:], rope_tab).then_inc(tab_in, 16)
            qsrc = w_qb.rearrange("(k p) m -> p k m", p=P)
            ksrc = w_kvb.rearrange("(k p) m -> p k m", p=P)

            def head_loads(h, first):
                cols = [h * (DN + DR), h * (DN + DR) + DN, h * (DN + DR) + (DN + DR // 2), h * (DN + DV)]
                if not first:
                    cols = [sp.snap(c) for c in cols]
                load(0, w_raw[0][:, 0:KQ, :], qsrc[:, :, bass.ds(cols[0], P)])
                wait(sp, w_ready[1], raws[1]())
                for d0, c, n in ((0, cols[1], DR), (DR, cols[2], DR // 2), (DR + DR // 2, cols[1], DR // 2)):
                    sp.dma_start(w_raw[1][:, 0:KQ, d0:d0 + n], qsrc[:, :, bass.ds(c, n)]).then_inc(raw_ready[1], 16)
                raws[1].add()
                if not first:
                    sp.wait_ge(kv_mm, kvs())
                    kvs.add(4)
                sp.dma_start(kvb[:], ksrc[:, :, bass.ds(cols[3], DN + DV)]).then_inc(kvb_in, 16)

            kvs = Tally(3)
            head_loads(0, True)
            with loop(sp, H - 1, {raws[0]: 1, raws[1]: 1, kvs: 4}) as h:
                head_loads(h + 1, False)
            sp.dma_start(ptab[:], page_table.rearrange("(a b) n -> a (b n)", a=1)).then_inc(pt_in, 16)
            sp.wait_ge(pt_in, 16)
            sp.wait_ge(pv_mm, 2 * H)
            sp.wait_ge(qlat_r, H)
            sp.wait_ge(sn_out, 16)
            sp.wait_ge(neg_ready, 2)
            sp.wait_ge(tok_out[0], 16 * 10)
            seqs = Tally(1)
            with loop(sp, NS // 2, {seqs: 2}) as i:
                for u in range(2):
                    nb = i * 2 + u
                    e0 = sp.snap(nb * NPG)
                    r1 = sp.snap(nb)
                    r2 = sp.snap(nb * (NS * H + H))
                    sp.wait_ge(dpv, seqs())
                    seqs.add()
                    sp.dma_start(vnew[u][:], lat_s[bass.ds(r1, 1), :]).then_inc(vn_in[u], 16)
                    sp.dma_start(s_sb[u][0:1, NPG, :],
                                 snew_d.rearrange("(a b) n -> a (b n)", a=1)[:, bass.ds(r2, H)]).then_inc(vn_in[u], 16)
                    with sp.Fori(0, NPG) as j:
                        page = sp.value_load(ptab[0:1, bass.ds(e0 + j, 1)], min_val=0, max_val=cache_lat.shape[0] - 1)
                        sp.dma_start(pg[u][:, bass.ds(j, 1), :],
                                     cache_lat[bass.ds(page, 1)].rearrange("a p c -> p a c")).then_inc(pg_in[u], 16)
                        sp.dma_start(pgr[u][:, bass.ds(j, 1), :],
                                     cache_pe[bass.ds(page, 1)].rearrange("a p c -> p a c")).then_inc(pg_in[u], 16)
            sp.wait_ge(dpv, NS + 2)
            for c in range(KC):
                sp.dma_start(wv[:, c], w_kvb[c * P:(c + 1) * P, :].rearrange("p (h n) -> p h n", h=H)[:, :, DN:DN + DV]
                             ).then_inc(wv_in, 16)
            sp.wait_ge(ov_e, 1)
            sp.dma_start(mid_d[0:H * DV, TP:T].rearrange("(h p) b -> p h b", p=P), ovs[:]).then_inc(ov_out, 16)
            loads_down(w_o, PARTS8)
            loads_ffn(1)
            for t in range(KT_TOK + 1):
                sp.wait_ge(yt_e, 2 * (t + 1))
                if t < KT_TOK:
                    sp.dma_start(y_prompt[t * P:(t + 1) * P, :], y_tok[t % 2][:]).then_inc(y_out[t % 2], 16)
                else:
                    sp.dma_start(y_sample, y_tok[t % 2][0:NS, :]).then_inc(y_out[t % 2], 16)
            sp.wait_ge(y_out[0], 16 * 5)
            sp.wait_ge(y_out[1], 16 * 4)

        @block.gpsimd
        def _(pool):
            pool.memset(ones[:], 1.0)
            pool.memset(ident[:], 0.0).then_inc(const_ready, 1)
            pool.memset(mask_b[:], 0.0).then_inc(const_ready, 1)
            pool.wait_ge(const_ready, 2)
            pool.affine_select(out=ident[:], in_=ident[:], compare_op=ALU.not_equal, fill=1.0, base=0,
                               pattern=[[-1, P]], channel_multiplier=1).then_inc(const_ready, 1)
            pool.affine_select(out=mask_b[:], in_=mask_b[:], compare_op=ALU.is_ge, fill=NEG, base=0,
                               pattern=[[-1, P]], channel_multiplier=1).then_inc(const_ready, 1)
            pool.wait_ge(const_ready, 4)
            pool.tensor_copy(ident_b[:], ident[:]).then_inc(const_ready, 1)
            stores, staged, used = Tally(), [Tally(), Tally()], Tally()

            pool.dma_start(mix_s[:, 0:1, :], state_mix[:, 1:2, :]).then_inc(state_out, 16)
            for l in range(2):
                pool.dma_start(ffn_s[l, :, 0:1, :], state_ffn[l, :, 1:2, :]).then_inc(state_out, 16)

            def store_g(n):
                with loop(pool, n, {stores: 1}) as i:
                    r = pool.snap(i * P)
                    pool.wait_ge(g_ready, stores(1))
                    pool.dma_start(mid_d[bass.ds(r, P), :], g_sb[:]).then_inc(g_out, 16)
                    stores.add()

            def store_tail(f, dst_p, dst_s, n):
                pool.wait_ge(tail_e, n)
                pool.dma_start(dst_p, tail_t[0:2, 0:f]).then_inc(tail_out, 16)
                pool.dma_start(dst_s, tail_t[2:TAIL, 0:f]).then_inc(tail_out, 16)

            def stage_in(kt):
                with loop(pool, ND, {used: kt}) as d:
                    col = pool.snap(d * DC)
                    with loop(pool, kt // 2, {used: 2}) as i:
                        for u in range(2):
                            row = pool.snap(i * (2 * P) + u * P)
                            pool.wait_ge(act_ready, used(1))
                            pool.dma_start(stage[u][:], mid_d[bass.ds(row, P), bass.ds(col, DC)]
                                           ).then_inc(st_ready[u], 16)
                            used.add()

            store_g(KD)
            store_tail(D, mix_p, mix_s[:, 1, :], 2)
            pool.wait_ge(g_out, 16 * KD)
            stage_in(KD)
            store_g(KF)
            store_tail(F, ffn_p[0], ffn_s[0, :, 1, :], 8)
            pool.wait_ge(g_out, 16 * (KD + KF))
            stage_in(KF)
            for t in range(KT_TOK + 1):
                pool.wait_ge(tok_e, t + 1)
                n = P if t < KT_TOK else NS
                dl = lat_p[t * P:(t + 1) * P, :] if t < KT_TOK else lat_s
                dp = pe_p[t * P:(t + 1) * P, :] if t < KT_TOK else pe_s
                pool.dma_start(dl, tok[t % 2][0:n, 0:KR]).then_inc(tok_out[t % 2], 16)
                pool.dma_start(dp, tok[t % 2][0:n, KR:KR + DR]).then_inc(tok_out[t % 2], 16)
            with loop(pool, H, {}) as h:
                r = pool.snap(h * DV)
                for half in range(2):
                    pool.wait_ge(pv_e, h * 2 + (half + 1))
                    pool.dma_start(mid_d[bass.ds(r, DV), half * 512:(half + 1) * 512], oh[half][:]
                                   ).then_inc(head_out[half], 16)
            pool.wait_ge(sn_e, 1)
            pool.dma_start(snew_d, sx[:]).then_inc(sn_out, 16)
            for half in range(2):
                pool.wait_ge(head_out[half], 16 * H)
            pool.wait_ge(ov_out, 16)
            stage_in(KD)
            store_g(KF)
            store_tail(F, ffn_p[1], ffn_s[1, :, 1, :], 14)
            pool.wait_ge(g_out, 16 * (KD + 2 * KF))
            stage_in(KF)
            pool.wait_ge(tail_out, 16 * 6)
            pool.wait_ge(state_out, 16 * 3)
            pool.wait_ge(tok_out[0], 16 * 10)
            pool.wait_ge(tok_out[1], 16 * 8)

        @block.scalar
        def _(act):
            splits = [Tally() for _ in range(3)]
            raw_n = [Tally() for _ in range(3)]
            pres, steps, roots = Tally(), Tally(), Tally()

            def hi_split(s, k, dmas=1):
                raw_n[s].add(16 * dmas)
                act.wait_ge(raw_ready[s], raw_n[s]())
                wait(act, w_done[s], splits[s]())
                act.activation(w_hi[s][:, 0:k, :], w_raw[s][:, 0:k, :], ACT.Copy).then_inc(hi_ready[s], 1)
                splits[s].add()

            def split_next(blocks):
                for b in blocks:
                    hi_split(*b)

            act.preload_act_table(ACT.Silu)
            act.wait_ge(c_loaded, 32)
            act.activation(csil[:], c_in[:], ACT.Silu).then_inc(csil_ready, 1)
            n = 0
            for t in range(KT_TOK + 1):
                w = P if t < KT_TOK else NS
                for half in range(2):
                    act.wait_ge(xt_t, n + 1)
                    act.activation(xT[:, 4 * half:4 * half + 4, t * P:t * P + w],
                                   bank(5 + n % 3).rearrange("p (k t) -> p k t", k=4)[:, :, 0:w], ACT.Copy
                                   ).then_inc(xt_e, 1)
                    n += 1

            def pre_squares(cols):
                act.wait_ge(x_done, pres(1))
                act.activation(sq[:], xT[:, :, cols], ACT.Square).then_inc(sq_ready, 1)

            def pre_round(cols):
                act.wait_ge(t_ready, pres(1))
                act.activation(h_hi[:, :, cols], sq[:], ACT.Copy).then_inc(hh_ready, 1)
                pres.add()

            def square_root(v=var, w=root_b):
                act.wait_ge(var_ready, roots(1))
                roots.add()
                act.activation(w[:], v[:], ACT.Sqrt).then_inc(root_ready, 1)

            def post_squares():
                act.wait_ge(act_step, steps())
                act.activation(sq[:], o_sb[:], ACT.Square).then_inc(sq_ready, 1)

            act.wait_ge(xt_e, 2 * (KT_TOK + 1))
            for d in range(ND):
                if d:
                    act.wait_ge(h_ready, d)
                pre_squares(slice(d * DC, (d + 1) * DC))
                square_root()
                pre_round(slice(d * DC, (d + 1) * DC))

            def round_act(k):
                u = k % 2
                sts[u].add(16)
                act.wait_ge(st_ready[u], sts[u]())
                act.activation(act_hi[:, k, :], stage[u][:], ACT.Copy).then_inc(ah_ready, 1)

            sts = [Tally(), Tally()]

            def down(kt, parts, nxt, last_norm, tails):
                own = [(s, k1 - k0) for s, k0, k1 in parts]
                wait(act, tail_out, 32 * tails)
                for k in range(kt):
                    round_act(k)

                def tiles(m0, m1, nxt_blocks=None, more_acts=False):
                    for m in range(m0, m1):
                        last = m == KD - 1
                        for (s, k0, k1), b in zip(parts, own):
                            if last:
                                wait(act, w_done[s], splits[s]())
                            if not (last and nxt_blocks is not None):
                                hi_split(*b)
                            if last and more_acts:
                                for k in range(k0, k1):
                                    round_act(k)
                        if last and nxt_blocks is not None:
                            split_next(nxt_blocks)

                def evac(m0, m1):
                    for m in range(m0, m1):
                        act.wait_ge(w_done[parts[-1][0]], done())
                        done.add()
                        act.activation(o_sb[:, m, :], bank(m % 6)[:, 0:DC], ACT.Copy).then_inc(act_step, 1)
                        steps.add()

                def chunk(more, prev_cols, nxt_blocks=None):
                    tiles(0, 2)
                    if prev_cols is not None:
                        square_root()
                        act.wait_ge(x_done, pres(1))
                    evac(0, 2)
                    if prev_cols is not None and not last_norm:
                        pre_squares(prev_cols)
                    tiles(2, 4)
                    evac(2, 4)
                    tiles(4, 6)
                    evac(4, 6)
                    if prev_cols is not None:
                        if last_norm:
                            pres.add()
                        else:
                            square_root()
                            pre_round(prev_cols)
                    tiles(6, 8, nxt_blocks, more)
                    evac(6, 8)
                    if prev_cols is not None and not last_norm:
                        act.wait_ge(h_ready, pres())
                    post_squares()

                done = Tally(splits[parts[-1][0]].n)
                S = {splits[s]: KD for s, _, _ in parts}
                S.update({raw_n[s]: 16 * KD for s, _, _ in parts})
                act.preload_act_table(ACT.Sqrt)
                chunk(True, None)
                per = dict(S)
                per.update({done: KD, steps: KD, sts[0]: 16 * kt // 2, sts[1]: 16 * kt // 2, pres: 1,
                            roots: 1 if last_norm else 2})
                with loop(act, ND - 2, per) as i:
                    c = act.snap(i * DC)
                    chunk(True, bass.ds(c, DC))
                chunk(False, slice((ND - 2) * DC, (ND - 1) * DC), nxt)
                cols = slice((ND - 1) * DC, T)
                square_root()
                if last_norm:
                    pres.add()
                else:
                    pre_squares(cols)
                    square_root()
                    pre_round(cols)

            conv_base = [0]

            def up_run(n, n_slots, ffn_layer, nxt):
                own = [(s, KD) for s in range(n_slots)]
                convs = Tally(conv_base[0])

                def body(j, blocks, parity):
                    for s in range(n_slots):
                        if s == 0:
                            act.wait_ge(w_done[0], splits[0]())
                        if blocks is own:
                            hi_split(s, KD)
                        if s == 0:
                            wait(act, conv_done, convs())
                            act.activation(chunked(a_sb[:, 2:2 + T]), upset(parity), ACT.Copy
                                           ).then_inc(set_free[parity], 1)
                            convs.add()
                            if ffn_layer is not None:
                                act.wait_ge(conv_done, convs())
                                act.activation(y_sb[:], y_sb[:], ACT.Silu,
                                               bias=v_cb[:, bass.ds(j + ffn_layer * KF, 1)]).then_inc(act_done, 1)
                    if blocks is not own:
                        split_next(blocks)

                per = {splits[s]: 1 for s in range(n_slots)}
                per.update({raw_n[s]: 16 for s in range(n_slots)})
                per[convs] = 1
                if n_slots == 2:
                    with loop(act, n - 1, per) as i:
                        body(i, own, 0)
                    body(n - 1, nxt, 0)
                else:
                    with loop(act, n // 2 - 1, {t: 2 * k for t, k in per.items()}) as i:
                        body(None, own, 0)
                        body(None, own, 1)
                    body(None, own, 0)
                    body(None, nxt, 1)
                conv_base[0] = convs.n

            split_next([(0, KD), (1, KD), (2, KD)])
            P8, P22 = [(s, k1 - k0) for s, k0, k1 in PARTS8], [(s, k1 - k0) for s, k0, k1 in PARTS22]
            up_run(KD, 3, None, P8)
            down(KD, PARTS8, [(0, KD), (1, KD)], False, 1)
            act.preload_act_table(ACT.Silu)
            up_run(KF, 2, 0, P22)
            down(KF, PARTS22, [(0, KD), (1, KD), (2, KD)], False, 2)

            for m in range(KQ + KC):
                s = m % 3
                act.wait_ge(w_done[s], splits[s]())
                if m < 3:
                    hi_split(s, KD, 3 if m == 2 else 1)
                dst = q_raw[:, m, :] if m < KQ else l_raw[:, m - KQ, :]
                act.activation(chunked(dst), upset(m % 2), ACT.Copy).then_inc(set_free[m % 2], 1)
            act.wait_ge(set_free[0], SETS + 2)
            act.wait_ge(set_free[1], SETS + 1)
            act.activation(sqm[:], q_raw[:], ACT.Square).then_inc(sq_ready, 1)
            act.wait_ge(ss_ready, NORMS + 1)
            act.wait_ge(set_free[1], SETS + 2)
            act.wait_ge(set_free[0], SETS + 3)
            act.activation(sqm[:, 0:KC, :], l_raw[:], ACT.Square).then_inc(sq_ready, 1)
            act.wait_ge(w_done[2], splits[2]())
            square_root(varm, rootm)
            act.wait_ge(qn_t, 1)
            act.activation(qn_hi[:], q_raw[:], ACT.Copy).then_inc(hh_ready, 1)
            square_root(varm, rootm)

            act.preload_act_table(ACT.Exp)
            hi_split(0, KQ)
            hi_split(1, KQ, 3)

            def head(more):
                act.wait_ge(w_done[0], splits[0]())
                if more:
                    hi_split(0, KQ)
                act.activation(chunked(qno[:]), upset(0), ACT.Copy).then_inc(set_free[0], 1)
                act.wait_ge(w_done[1], splits[1]())
                if more:
                    hi_split(1, KQ, 3)
                act.wait_ge(kv_mm, h4(1))
                act.activation(kno[:].rearrange("p (c n) -> p c n", c=2), ps[:, 6:8, :], ACT.Copy).then_inc(kv_e, 1)
                act.wait_ge(kv_mm, h4(2))
                act.activation(v_sb[:].rearrange("p (c t) v -> p c (t v)", c=2), ps[:, 0:2, :], ACT.Copy
                               ).then_inc(kv_e, 1)
                act.wait_ge(kv_mm, h4(3))
                act.activation(wkT[:].rearrange("p c n -> p (c n)"), bank(2)[:, 0:KC * P], ACT.Copy
                               ).then_inc(kv_e, 1)
                h4.add(4)

                def exp(q):
                    nk = (q + 1) * P
                    act.wait_ge(nm_ready, h8(q + 1))
                    wait(act, p_t_mm, h8(q - 1))
                    act.activation(p_sb[q % 2][:, 0:nk], ps[:, 2 * (q % 2):2 * (q % 2) + 2, :].rearrange(
                        "p b n -> p (b n)")[:, 0:nk], ACT.Exp, bias=st[:, 2 + q % 2, 0:1], scale=SCALE,
                        accum_out=st[:, 4 + q % 2, 0:1]).then_inc(e_ready, 1)

                def evac_t(q):
                    act.wait_ge(p_t_mm, h8(q + 1))
                    if q in (0, 4):
                        wait(act, pv_mm, h2(q // 4))
                    ins = None
                    for b in range(q // 4 + 1):
                        k0, k1 = 4 * b, min(4 * b + 4, q + 1)
                        ins = act.activation(p_t[:, k0:k1, (q % 4) * P:(q % 4 + 1) * P],
                                             bank(4 + b)[:, 0:(k1 - k0) * P].rearrange("p (k n) -> p k n", n=P),
                                             ACT.Copy)
                    ins.then_inc(p_t_e, 1)

                def evac_o(half):
                    act.wait_ge(pv_mm, h2(half + 1))
                    wait(act, head_out[half], h16())
                    act.activation(oh[half][:], bank(6 + half), ACT.Copy).then_inc(pv_e, 1)

                exp(0)
                for q in range(1, KT_TOK):
                    exp(q)
                    if q == 5:
                        evac_o(0)
                    evac_t(q - 1)
                evac_t(KT_TOK - 1)
                evac_o(1)
                h8.add(8)
                h2.add(2)
                h16.add(16)

            h4, h8, h2, h16 = Tally(), Tally(), Tally(), Tally()
            head(True)
            with loop(act, H - 2, {splits[0]: 1, splits[1]: 1, raw_n[0]: 16, raw_n[1]: 48, h4: 4, h8: 8, h2: 2,
                                   h16: 16}):
                head(True)
            head(False)

            groups = Tally()
            seqs = Tally()
            act.wait_ge(neg_ready, 2)

            def decode_seq(u):
                for g in range(8):
                    b0 = 3 * (g % 2)
                    act.wait_ge(kt_mm, groups(1))
                    wait(act, sc_mm, groups(-1))
                    act.activation(kT[g % 2][:, 0, :], bank(b0), ACT.Copy)
                    act.activation(kT[g % 2][0:DR, 2, :], bank(b0 + 2)[0:DR, :], ACT.Copy).then_inc(kt_ea, 1)
                    groups.add()
                act.wait_ge(ch_dve, seqs(4))
                seqs.add(6)
                act.activation(e_sb[u][:], e_sb[u][:], ACT.Exp, scale=SCALE).then_inc(ch_act, 1)

            decode_seq(0)
            decode_seq(1)
            with loop(act, NS // 2 - 1, {groups: 16, seqs: 12}):
                decode_seq(0)
                decode_seq(1)
            split_next(P8)
            down(KD, PARTS8, [(0, KD), (1, KD)], False, 0)
            act.preload_act_table(ACT.Silu)
            up_run(KF, 2, 1, P22)
            down(KF, PARTS22, [], True, 3)
            for n in range(2 * (KT_TOK + 1)):
                t, half = n // 2, n % 2
                w = P if t < KT_TOK else NS
                act.wait_ge(yt_mm, n + 1)
                if t >= 2:
                    act.wait_ge(y_out[t % 2], 16 * (t // 2))
                act.activation(y_tok[t % 2][0:w, half * 512:(half + 1) * 512], bank(n % 4)[0:w, :], ACT.Copy
                               ).then_inc(yt_e, 1)

        @block.vector
        def _(dve):
            steps = Tally()
            splits = [Tally() for _ in range(3)]
            stats, pres = Tally(), Tally()
            spl_act = Tally(2)

            def step(ins):
                ins.then_inc(dve_step, 1)
                steps.add()

            def settle():
                dve.wait_ge(dve_step, steps())

            def lo_split(s, k, dmas=1):
                dve.wait_ge(hi_ready[s], splits[s](1))
                dve.tensor_tensor(w_lo[s][:, 0:k, :], w_raw[s][:, 0:k, :], w_hi[s][:, 0:k, :].bitcast(F32),
                                  ALU.subtract).then_inc(w_ready[s], 1)
                splits[s].add()

            def split_next(blocks):
                for b in blocks:
                    lo_split(*b)

            dve.sem_inc(act_ready, 2)
            dve.wait_ge(setup_t, 1)
            for t, r in enumerate((125, 108, 66, 66)):
                step(dve.tensor_copy(vec[:, t, 0:r], bank(0)[:, t * P:t * P + r]))
            dve.wait_ge(setup_t, 2)
            dve.tensor_copy(csT[:], bank(1)[:, 0:KD * MLANES].rearrange("p (k c) -> p k c", k=KD)).then_inc(setup_e, 1)
            settle()

            def taps(b, kt, w, dst):
                state = bank(b)[:, 0:kt * 2 * NS].rearrange("p (m b k) -> p m b k", m=kt, b=NS)
                for k, out in ((0, dst), (1, ptmp[:, 0:kt, :])):
                    step(dve.tensor_tensor(out, state[:, :, :, k],
                                           w[:, k * kt:(k + 1) * kt].unsqueeze(2).to_broadcast([P, kt, NS]), ALU.mult))
                settle()
                step(dve.tensor_tensor(dst, dst, ptmp[:, 0:kt, :], ALU.add))
                settle()

            dve.wait_ge(setup_t, 3)
            taps(2, KD, v_scw, prev_mix[:])
            for l in range(2):
                dve.wait_ge(setup_t, 4 + l)
                taps(3 + l, KF, vec[:, 2 + l, :], prev_ffn[:, l])
            dve.sem_inc(setup_e, 1)

            mods = Tally(2)
            with loop(dve, MODS, {mods: 4}) as i:
                for b in range(4):
                    mods.add()
                    dve.wait_ge(mod_mm, mods())
                    m0 = i * 16 + 4 * b
                    dve.tensor_tensor(modv[:, bass.ds(m0, 4), :],
                                      bank(b % 2)[:, 0:4 * MLANES].rearrange("p (m c) -> p m c", m=4),
                                      v_modb[:, bass.ds(m0, 4)].unsqueeze(2).to_broadcast([P, 4, MLANES]),
                                      ALU.add).then_inc(mod_done, 1)
            dve.wait_ge(mod_done, 4 * MODS)

            def mod(l, kind):
                return modv[:, (l * MODS + kind) * KD:(l * MODS + kind + 1) * KD, :]

            def gain(n, l):
                return v_norm[:, (2 * n + l) * KD:(2 * n + l + 1) * KD].unsqueeze(2).to_broadcast([P, KD, MLANES])

            for l in range(2):
                for s in range(2):
                    step(dve.scalar_tensor_tensor(mod(l, 3 * s + 1), mod(l, 3 * s + 1), 1.0, gain(2 * s, l),
                                                  ALU.add, ALU.mult))
                    step(dve.tensor_tensor(mod(l, 3 * s + 2), mod(l, 3 * s + 2), gain(2 * s + 1, l), ALU.mult))
            settle()

            def rsqrt(dst, v, w, src, n):
                dve.wait_ge(stat_ready, stats(1))
                stats.add()
                dve.tensor_scalar(v, src, 1.0 / n, EPS, ALU.mult, ALU.add).then_inc(var_ready, 1)
                dve.wait_ge(root_ready, stats())
                newton(dst, v, w)

            def newton(dst, v, w):
                step(dve.reciprocal(dst, w))
                settle()
                step(dve.tensor_tensor(w, dst, v, ALU.mult))
                settle()
                step(dve.scalar_tensor_tensor(w, w, -0.5, dst, ALU.mult, ALU.mult))
                settle()
                step(dve.scalar_tensor_tensor(dst, w, 1.5, dst, ALU.add, ALU.mult))
                settle()

            def sum_squares(src, dst):
                dve.wait_ge(sq_ready, stats(1))
                dve.tensor_reduce(dst, src.rearrange("p k t -> p t k"), AX.X, ALU.add).then_inc(ss_ready, 1)

            def root(n):
                rsqrt(rs[:], var[:], root_b[:], bank(6)[:, 0:DC], n)

            def pre_norm(l, s, cols, last):
                root(D)
                step(dve.tensor_tensor(sq[:], xT[:, :, cols], rs[:].unsqueeze(1).to_broadcast([P, KD, DC]), ALU.mult))
                settle()
                n = PL if last else DC
                A, B = mod(l, 3 * s + 1), mod(l, 3 * s)
                ins = None
                if last:
                    step(dve.tensor_tensor(tmp_s[:], sq[:, :, PL:DC], A[:, :, 1:MLANES], ALU.mult))
                    settle()
                    dve.tensor_tensor(sq[:, :, PL:DC], tmp_s[:], B[:, :, 1:MLANES], ALU.add)
                for k in range(KD):
                    ins = dve.tensor_scalar(sq[:, k, 0:n], sq[:, k, 0:n], A[:, k, 0:1], B[:, k, 0:1], ALU.mult, ALU.add)
                ins.then_inc(t_ready, 1)
                pres.add()
                dve.wait_ge(hh_ready, pres(hh_more[0]))
                dve.tensor_tensor(h_lo[:, :, cols], sq[:], h_hi[:, :, cols].bitcast(F32), ALU.subtract
                                  ).then_inc(h_ready, 1)

            hh_more = [0]

            def post_norm(l, s, cols, last):
                root(D)
                step(dve.tensor_tensor(o_sb[:], o_sb[:], rs[:].unsqueeze(1).to_broadcast([P, KD, DC]), ALU.mult))
                settle()
                n = PL if last else DC
                G = mod(l, 3 * s + 2)
                if last:
                    step(dve.tensor_tensor(tmp_s[:], o_sb[:, :, PL:DC], G[:, :, 1:MLANES], ALU.mult))
                    settle()
                    dve.tensor_tensor(xT[:, :, TP:T], xT[:, :, TP:T], tmp_s[:], ALU.add)
                    cols = slice((ND - 1) * DC, TP)
                for k in range(KD):
                    ins = dve.scalar_tensor_tensor(xT[:, k, cols], o_sb[:, k, 0:n], G[:, k, 0:1], xT[:, k, cols],
                                                   ALU.mult, ALU.add)
                ins.then_inc(x_done, 1)

            dve.wait_ge(xt_e, 2 * (KT_TOK + 1))
            dve.sem_inc(x_done, ND)
            for d in range(ND):
                sum_squares(sq[:], rs[:])
                pre_norm(0, 0, slice(d * DC, (d + 1) * DC), d == ND - 1)

            def low_act(k):
                dve.wait_ge(ah_ready, spl_act(-1))
                dve.tensor_tensor(act_lo[:, k, :], stage[k % 2][:], act_hi[:, k, :].bitcast(F32), ALU.subtract
                                  ).then_inc(act_ready, 1)
                spl_act.add()

            def down(kt, parts, nxt, norm, nxt_norm):
                own = [(s, k1 - k0) for s, k0, k1 in parts]
                for k in range(kt):
                    low_act(k)

                def tiles(m0, m1, nxt_blocks=None, more_acts=False):
                    for m in range(m0, m1):
                        last = m == KD - 1
                        for (s, k0, k1), b in zip(parts, own):
                            if not (last and nxt_blocks is not None):
                                lo_split(*b)
                            if last and more_acts:
                                for k in range(k0, k1):
                                    low_act(k)
                        if last and nxt_blocks is not None:
                            split_next(nxt_blocks)

                def chunk(more, prev, nxt_blocks=None):
                    tiles(0, 2)
                    if prev is not None:
                        post_norm(*norm, prev, False)
                        if nxt_norm is not None:
                            sum_squares(sq[:], rs[:])
                    tiles(2, 6)
                    if prev is not None and nxt_norm is not None:
                        pre_norm(*nxt_norm, prev, False)
                    tiles(6, 8, nxt_blocks, more)
                    sum_squares(sq[:], rs[:])

                per_norm = 1 if nxt_norm is None else 2
                chunk(True, None)
                n0 = steps.n
                per = {splits[s]: KD for s, _, _ in parts}
                per.update({spl_act: kt, stats: per_norm, steps: STEP_POST + (per_norm - 1) * STEP_PRE})
                if nxt_norm is not None:
                    per[pres] = 1
                with loop(dve, ND - 2, per) as i:
                    c = dve.snap(i * DC)
                    chunk(True, bass.ds(c, DC))
                chunk(False, slice((ND - 2) * DC, (ND - 1) * DC), nxt)
                cols = slice((ND - 1) * DC, T)
                post_norm(*norm, cols, True)
                if nxt_norm is not None:
                    sum_squares(sq[:], rs[:])
                    pre_norm(*nxt_norm, cols, True)

            STEP_POST, STEP_PRE = 5, 5

            def conv(j, taps_w, kt, prev):
                w = [taps_w[:, bass.ds(j + k * kt, 1)] for k in range(3)]
                step(dve.tensor_copy(tail[:, bass.ds(j, 1), :], a_sb[:, 2 + TP - 2:2 + T].unsqueeze(1)))
                step(dve.tensor_scalar(y_sb[:, 0:TP], a_sb[:, 0:TP], w[0], None, ALU.mult))
                step(dve.tensor_copy(y_sb[:, TP:T].unsqueeze(1), prev[:, bass.ds(j, 1), :]))
                settle()
                step(dve.scalar_tensor_tensor(y_sb[:, 0:TP], a_sb[:, 1:1 + TP], w[1], y_sb[:, 0:TP],
                                              ALU.mult, ALU.add))
                settle()
                dve.scalar_tensor_tensor(y_sb[:], a_sb[:, 2:2 + T], w[2], y_sb[:], ALU.mult, ALU.add
                                         ).then_inc(conv_done, 1)

            def tails_out(kt, t0):
                for g in range(-(-kt // 4)):
                    n = min(4, kt - 4 * g)
                    dve.wait_ge(tail_t_done, t0 + g + 1)
                    dve.tensor_copy(tail_t[:, g * 4 * P:(g * 4 + n) * P], bank(6 + g % 2)[0:TAIL, 0:n * P]
                                    ).then_inc(tail_e, 1)

            conv_n, g_n, set0 = Tally(), Tally(), Tally()

            def gate_out(src, parity):
                wait(dve, g_out, g_n())
                g_n.add(16)
                dve.tensor_tensor(chunked(g_sb[:]), chunked(y_sb[:]), upset(parity), ALU.mult)

            split_next([(0, KD), (1, KD), (2, KD)])
            step(dve.memset(a_sb[:, 0:2], 0.0))
            settle()
            f0, f1 = Tally(), Tally()

            def mixer(j, parity, own):
                if own:
                    lo_split(0, KD)
                f = (f0, f1)
                f[parity].add()
                dve.wait_ge(set_free[parity], f[parity]())
                if own:
                    lo_split(1, KD)
                else:
                    dve.wait_ge(w_done[1], splits[1]())
                f[1 - parity].add()
                step(dve.tensor_tensor(chunked(a_sb[:, 2:2 + T]), chunked(a_sb[:, 2:2 + T]), upset(1 - parity),
                                       ALU.mult))
                settle()
                dve.sem_inc(set_free[1 - parity], 1)
                conv(j, v_scw, KD, prev_mix[:])
                conv_n.add()
                dve.wait_ge(conv_done, conv_n())
                if own:
                    lo_split(2, KD)
                else:
                    dve.wait_ge(w_done[2], splits[2]())
                f[parity].add()
                wait(dve, g_out, g_n())
                g_n.add(16)
                dve.tensor_tensor(chunked(g_sb[:]), chunked(y_sb[:]), upset(parity), ALU.mult).then_inc(g_ready, 1)
                gs.add()
                dve.wait_ge(g_ready, gs())
                dve.sem_inc(set_free[parity], 1)

            gs = Tally()
            mixer(0, 0, True)
            mixer(1, 1, True)
            with loop(dve, KD // 2 - 2, {splits[0]: 2, splits[1]: 2, splits[2]: 2, f0: 3, f1: 3, conv_n: 2,
                                         g_n: 32, gs: 2, steps: 10}) as i:
                j = dve.snap(i * 2)
                mixer(j + 2, 0, True)
                mixer(j + 3, 1, True)
            mixer(KD - 2, 0, True)
            mixer(KD - 1, 1, False)
            P8, P22 = [(s, k1 - k0) for s, k0, k1 in PARTS8], [(s, k1 - k0) for s, k0, k1 in PARTS22]
            split_next(P8)
            settle()
            dve.sem_inc(tail_ready, 1)
            tails_out(KD, 0)
            down(KD, PARTS8, [(0, KD), (1, KD)], (0, 0), (0, 1))

            def ffn(l, nxt, t0):
                step(dve.memset(a_sb[:, 0:2], 0.0))
                settle()

                def body(j, own):
                    lo_split(0, KD) if own else dve.wait_ge(w_done[0], splits[0]())
                    f0.add()
                    dve.wait_ge(set_free[0], f0())
                    conv(j, vec[:, 2 + l, :], KF, prev_ffn[:, l])
                    lo_split(1, KD) if own else dve.wait_ge(w_done[1], splits[1]())
                    silus.add()
                    dve.wait_ge(act_done, silus())
                    dve.wait_ge(g_out, g_n())
                    g_n.add(16)
                    f1.add()
                    dve.tensor_tensor(chunked(g_sb[:]), chunked(y_sb[:]), upset(1), ALU.mult).then_inc(g_ready, 1)
                    gs.add()
                    dve.wait_ge(g_ready, gs())
                    dve.sem_inc(set_free[1], 1)

                with loop(dve, KF - 1, {splits[0]: 1, splits[1]: 1, f0: 1, f1: 1, silus: 1, g_n: 16, gs: 1,
                                        steps: 4}) as i:
                    body(i, True)
                body(KF - 1, False)
                split_next(nxt)
                settle()
                dve.sem_inc(tail_ready, 1)
                tails_out(KF, t0)

            silus = Tally()
            ffn(0, P22, 2)
            down(KF, PARTS22, [(0, KD), (1, KD), (2, KD)], (0, 1), (1, 0))

            lo_split(0, KD)
            lo_split(1, KD)
            lo_split(2, KD)
            dve.wait_ge(w_done[2], splits[2]())

            def rope(u, dst, ready):
                step(dve.tensor_tensor(chunked(rope1[:]), upset(u)[0:DR], chunked(tab[0:DR, :]), ALU.mult))
                step(dve.tensor_tensor(chunked(dst[:]), upset(u)[DR:P], chunked(tab[DR:P, :]), ALU.mult))
                settle()
                dve.sem_inc(set_free[u], 1)
                dve.tensor_tensor(dst[:], dst[:], rope1[:], ALU.add).then_inc(ready, 1)

            dve.wait_ge(tab_in, 16)

            def root_all(n):
                dve.wait_ge(stat_ready, stats(1))
                stats.add()
                dve.tensor_scalar(chunked(varm[:]), upset(0), 1.0 / n, EPS, ALU.mult, ALU.add).then_inc(var_ready, 1)
                dve.wait_ge(root_ready, stats())
                newton(rsm[:], varm[:], rootm[:])

            sum_squares(sqm[:], rsm[:])
            root_all(QR)
            step(dve.tensor_tensor(q_raw[:], q_raw[:], rsm[:].unsqueeze(1).to_broadcast([P, KQ, T]), ALU.mult))
            settle()
            for k in range(KQ):
                ins = dve.tensor_scalar(q_raw[:, k, :], q_raw[:, k, :], v_qan[:, k:k + 1], None, ALU.mult)
            ins.then_inc(qn_t, 1)
            sum_squares(sqm[:, 0:KC, :], rsm[:])
            dve.wait_ge(hh_ready, pres(1))
            hh_more[0] = 1
            dve.tensor_tensor(qn_lo[:], q_raw[:], qn_hi[:].bitcast(F32), ALU.subtract).then_inc(qn_r, 1)
            root_all(KR)
            step(dve.tensor_tensor(l_raw[:], l_raw[:], rsm[:].unsqueeze(1).to_broadcast([P, KC, T]), ALU.mult))
            settle()
            for k in range(KC):
                ins = dve.tensor_scalar(latn[:, k, :], l_raw[:, k, :], v_kvn[:, k:k + 1], None, ALU.mult)
            ins.then_inc(lat_r, 1)
            rope(1, kpe, kpe_r)
            lo_split(0, KQ)
            lo_split(1, KQ)
            dve.wait_ge(kpe_r, 1)
            dve.wait_ge(lat_r, 1)
            dve.wait_ge(qn_r, 1)
            step(dve.tensor_copy(lats[:], latn[:, :, TP:T]))
            step(dve.tensor_copy(kpes[:], kpe[:, TP:T]))
            for t in range(KT_TOK + 1):
                n = P if t < KT_TOK else NS
                dve.wait_ge(tok_t, t + 1)
                if t >= 2:
                    dve.wait_ge(tok_out[t % 2], 32 * (t // 2))
                dve.tensor_copy(tok[t % 2][0:n, :], bank(6 + t % 2)[0:n, 0:KR + DR]).then_inc(tok_e, 1)
            h1, h4, h8 = Tally(), Tally(), Tally()

            def head(h, more):
                if more:
                    lo_split(0, KQ)
                    lo_split(1, KQ)
                else:
                    dve.wait_ge(w_done[1], splits[1]())
                step(dve.tensor_tensor(chunked(rope1[:]), upset(1)[0:DR], chunked(tab[0:DR, :]), ALU.mult))
                step(dve.tensor_tensor(chunked(qpe[:]), upset(1)[DR:P], chunked(tab[DR:P, :]), ALU.mult))
                settle()
                step(dve.tensor_tensor(qpe[:], qpe[:], rope1[:], ALU.add))
                settle()
                dve.sem_inc(qpe_r, 1)
                step(dve.tensor_copy(qpes[:, :, bass.ds(h, 1)], qpe[:, TP:T].unsqueeze(2)))
                dve.wait_ge(kv_mm, h4(4))
                h4.add(4)
                dve.tensor_copy(qlat[:, :, :, bass.ds(h, 1)], bank(5)[:, 0:KC * NS].rearrange(
                    "p (c b o) -> p c b o", c=KC, o=1)).then_inc(qlat_r, 1)

                def top(q):
                    u = q % 2
                    dve.wait_ge(s_mm, h8(q + 1))
                    step(dve.tensor_reduce(st[:, u, 0:1], ps[:, 2 * u:2 * u + 2, :].rearrange("p b n -> p (b n)")
                                           [:, 0:(q + 1) * P], AX.X, ALU.max))
                    settle()
                    dve.tensor_scalar(st[:, 2 + u, 0:1], st[:, u, 0:1], -SCALE, None, ALU.mult).then_inc(nm_ready, 1)

                def norm(q):
                    u = q % 2
                    dve.wait_ge(e_ready, h8(q + 1))
                    step(dve.reciprocal(st[:, 6 + u, 0:1], st[:, 4 + u, 0:1]))
                    settle()
                    dve.tensor_scalar(p_sb[u][:, 0:(q + 1) * P], p_sb[u][:, 0:(q + 1) * P], st[:, 6 + u, 0:1], None,
                                      ALU.mult).then_inc(p_ready, 1)

                top(0)
                for q in range(1, KT_TOK):
                    top(q)
                    norm(q - 1)
                norm(KT_TOK - 1)
                h8.add(8)

            with loop(dve, H - 1, {splits[0]: 1, splits[1]: 1, h4: 4, h8: 8, steps: 20}) as h:
                head(h, True)
            head(H - 1, False)
            settle()
            dve.wait_ge(sn_mm, 1)
            dve.wait_ge(qlat_r, H)
            dve.tensor_copy(sx[:], bank(0)[0:NS, 0:NS * H]).then_inc(sn_e, 1)
            for u in range(2):
                dve.memset(s_sb[u][:, NPG, :], NEG).then_inc(neg_ready, 1)

            groups, seqs, olats, dpvs = Tally(), Tally(), Tally(), Tally(2)

            def decode_seq(b, u):
                for g in range(8):
                    dve.wait_ge(kt_mm, groups(1))
                    wait(dve, sc_mm, groups(-1))
                    dve.tensor_copy(kT[g % 2][:, 1, :], bank(3 * (g % 2) + 1)).then_inc(kt_ed, 1)
                    groups.add()
                dve.wait_ge(sc_mm, groups())
                dve.tensor_copy(s_sb[u][:, 0:NPG, :], bank(6)[:, 0:NPG * H].rearrange("p (n h) -> p n h", h=H)
                                ).then_inc(ch_dve, 1)
                dve.wait_ge(ch_dve, seqs(1))
                dve.wait_ge(vn_in[u], vns[u](32))
                vns[u].add(32)
                dve.tensor_reduce(dm[:, 0:H], s_sb[u][:].rearrange("p n h -> p h n"), AX.X, ALU.max
                                  ).then_inc(ch_dve, 1)
                dve.wait_ge(ch_pe, seqs3(1))
                step(dve.tensor_reduce(dm[0:H, 8:9], bank(7)[0:H, 0:P], AX.X, ALU.max))
                settle()
                dve.tensor_scalar(dm[0:H, 16:16 + H], ident[0:H, 0:H], dm[0:H, 8:9], None, ALU.mult
                                  ).then_inc(ch_dve, 1)
                dve.wait_ge(ch_pe, seqs3(2))
                dve.tensor_tensor(e_sb[u][:], s_sb[u][:], bank(7)[:, P:P + H].unsqueeze(1).to_broadcast(
                    [P, NPG + 1, H]), ALU.subtract).then_inc(ch_dve, 1)
                dve.wait_ge(ch_act, acts_n(1))
                acts_n.add()
                dve.tensor_reduce(dm[:, 24:24 + H], e_sb[u][:].rearrange("p n h -> p h n"), AX.X, ALU.add
                                  ).then_inc(ch_dve, 1)
                dve.wait_ge(ch_pe, seqs3(3))
                dve.reciprocal(dm[:, 32:32 + H], bank(7)[:, P + H:P + 2 * H]).then_inc(ch_dve, 1)
                seqs.add(6)
                seqs3.add(3)
                dve.wait_ge(ch_dve, seqs())
                dve.wait_ge(dpv, dpvs(1))
                dpvs.add()
                dve.tensor_tensor(olat[:, :, :, bass.ds(b, 1)],
                                  bank(7)[:, 256:256 + KC * H].rearrange("p (c h o) -> p c h o", c=KC, o=1),
                                  dm[:, 32:32 + H].unsqueeze(1).unsqueeze(3).to_broadcast([P, KC, H, 1]),
                                  ALU.mult).then_inc(olat_r, 1)

            vns, acts_n, seqs3 = [Tally(), Tally()], Tally(), Tally()
            decode_seq(0, 0)
            decode_seq(1, 1)
            with loop(dve, NS // 2 - 1, {groups: 16, seqs: 12, seqs3: 6, dpvs: 2, acts_n: 2, steps: 2,
                                         vns[0]: 32, vns[1]: 32}) as i:
                b = dve.snap(i * 2)
                decode_seq(b + 2, 0)
                decode_seq(b + 3, 1)
            dve.wait_ge(ov_mm, 1)
            dve.tensor_copy(ovs[:], bank(0)[:, 0:H * NS].rearrange("p (h b) -> p h b", h=H)).then_inc(ov_e, 1)
            split_next(P8)
            down(KD, PARTS8, [(0, KD), (1, KD)], (1, 0), (1, 1))
            f0.add(KQ + H)
            f1.add(KQ)
            ffn(1, P22, 8)
            down(KF, PARTS22, [], (1, 1), None)

        @block.tensor
        def _(pe):
            uses = [Tally() for _ in range(3)]
            f = [Tally(), Tally()]
            stats, acts_b = Tally(), Tally(2)

            def trans(out, in_):
                r = in_.shape[0]
                return pe.transpose(out, in_, ident[0:r, 0:r])

            pe.sem_inc(mod_mm, 2)
            pe.sem_inc(dpv, 2)
            pe.wait_ge(const_ready, 5)
            pe.wait_ge(vec_in, 16 * 11)
            for t, r in enumerate((125, 108, 66, 66)):
                ins = trans(bank(0)[:, t * P:t * P + r], packs[0:r, t, :])
            ins.then_inc(setup_t, 1)
            pe.wait_ge(csil_ready, 1)
            for k in range(KD):
                ins = trans(bank(1)[:, k * MLANES:(k + 1) * MLANES], csil[:, k * P:(k + 1) * P])
            ins.then_inc(setup_t, 1)
            pe.wait_ge(mix_loaded, 16)
            for k in range(KD):
                ins = trans(bank(2)[:, k * 2 * NS:(k + 1) * 2 * NS], mix_in[:, k * P:(k + 1) * P])
            ins.then_inc(setup_t, 1)
            pe.wait_ge(ffn_loaded, 16)
            for l in range(2):
                for k in range(KF):
                    ins = trans(bank(3 + l)[:, k * 2 * NS:(k + 1) * 2 * NS], ffn_in[:, l, k * P:(k + 1) * P])
                ins.then_inc(setup_t, 1)
            pe.wait_ge(x_loaded, 16)
            pe.wait_ge(xs_loaded, 16)
            for n in range(2 * (KT_TOK + 1)):
                t, half = n // 2, n % 2
                wait(pe, xt_e, n - 2)
                for k in range(4):
                    c = (4 * half + k) * P
                    src = x_in[:, t, c:c + P] if t < KT_TOK else xs_in[:, c:c + P]
                    w = P if t < KT_TOK else NS
                    ins = trans(bank(5 + n % 3)[:, k * P:k * P + w], src)
                ins.then_inc(xt_t, 1)
            pe.wait_ge(setup_e, 2)
            mods = [Tally(), Tally()]
            md = Tally(-1)

            def mod_pair():
                for b in range(2):
                    mods[b].add(16)
                    pe.wait_ge(mod_loaded[b], mods[b]())
                    wait(pe, mod_done, md())
                    md.add()
                    for m in range(4):
                        for k in range(KD):
                            ins = pe.matmul(bank(b)[:, m * MLANES:(m + 1) * MLANES],
                                            mod_raw[b][:, k, m * P:(m + 1) * P], csT[:, k, :],
                                            start=k == 0, stop=k == KD - 1)
                    ins.then_inc(mod_mm, 1)

            mod_pair()
            with loop(pe, 2 * MODS - 1, {mods[0]: 16, mods[1]: 16, md: 2}):
                mod_pair()

            def stat(src, out):
                pe.wait_ge(ss_ready, stats(1))
                stats.add()
                for o, r in zip(out, src):
                    ins = pe.matmul(o, ones[:], r, start=True, stop=True)
                ins.then_inc(stat_ready, 1)

            def stat_chunk():
                stat([rs[:]], [bank(6)[:, 0:DC]])

            for d in range(ND):
                stat_chunk()

            def product(slot, ks, rhs, outs_, first=True, last=True):
                pe.wait_ge(w_ready[slot], uses[slot](1))
                uses[slot].add()
                for o, (hi, lo) in zip(outs_, rhs):
                    for n, k in enumerate(ks):
                        f_, l_ = first and n == 0, last and n == len(ks) - 1
                        pe.matmul(o, w_hi[slot][:, n, :], hi(k), start=f_, stop=False)
                        pe.matmul(o, w_hi[slot][:, n, :], lo(k), start=False, stop=False)
                        ins = pe.matmul(o, w_lo[slot][:, n, :], hi(k), start=False, stop=l_)
                ins.then_inc(w_done[slot], 1)

            def wide(hi, lo):
                return [(lambda k, c=c: hi[:, k, c * UC:(c + 1) * UC], lambda k, c=c: lo[:, k, c * UC:(c + 1) * UC])
                        for c in range(NU)]

            def up_product(slot, s, kt=KD, hi=None, lo=None):
                wait(pe, set_free[s], f[s]())
                f[s].add()
                product(slot, range(kt), wide(hi or h_hi, lo or h_lo), [upset(s)[:, c, :] for c in range(NU)])

            def down(kt, parts, norm_next):
                def tile(m, first_chunk_tile):
                    ago = 2 if m < 2 else 6 if m >= 6 else KD
                    wait(pe, act_step, evs(1 - ago))
                    evs.add()
                    for n, (s, k0, k1) in enumerate(parts):
                        if first_chunk_tile:
                            pe.wait_ge(act_ready, acts_b(k1))
                        product(s, range(k0, k1), [(lambda k: act_hi[:, k, :], lambda k: act_lo[:, k, :])],
                                [bank(m % 6)[:, 0:DC]], n == 0, n == len(parts) - 1)

                def chunk(prev):
                    tile(0, True)
                    acts_b.add(kt)
                    tile(1, False)
                    if prev:
                        stat_chunk()
                    for m in range(2, 4):
                        tile(m, False)
                    if prev and norm_next:
                        stat_chunk()
                    for m in range(4, 8):
                        tile(m, False)

                chunk(False)
                per = {uses[s]: KD for s, _, _ in parts}
                per.update({evs: KD, acts_b: kt, stats: 2 if norm_next else 1})
                with loop(pe, ND - 1, per):
                    chunk(True)
                stat_chunk()
                if norm_next:
                    stat_chunk()

            evs = Tally()

            def tails(kt, n):
                pe.wait_ge(tail_ready, n)
                for g in range(-(-kt // 4)):
                    if g >= 2:
                        pe.wait_ge(tail_e, te[0] + g - 1)
                    for k in range(4 * g, min(kt, 4 * g + 4)):
                        ins = trans(bank(6 + g % 2)[0:TAIL, (k % 4) * P:(k % 4 + 1) * P], tail[:, k, :])
                    ins.then_inc(tail_t_done, 1)
                te[0] += -(-kt // 4)

            te = [0]

            pe.wait_ge(h_ready, ND)

            def triple(par):
                up_product(0, par)
                up_product(1, 1 - par)
                up_product(2, par)

            triple(0)
            triple(1)
            with loop(pe, KD // 2 - 1, {uses[0]: 2, uses[1]: 2, uses[2]: 2, f[0]: 3, f[1]: 3}):
                triple(0)
                triple(1)
            tails(KD, 1)
            down(KD, PARTS8, True)

            def ffn(n):
                pe.wait_ge(h_ready, n)
                with loop(pe, KF, {uses[0]: 1, uses[1]: 1, f[0]: 1, f[1]: 1}):
                    up_product(0, 0)
                    up_product(1, 1)

            ffn(2 * ND)
            tails(KF, 2)
            down(KF, PARTS22, True)
            pe.wait_ge(h_ready, 3 * ND)
            for m in range(KQ + KC + 1):
                up_product(m % 3, m % 2)
            pe.wait_ge(set_free[0], f[0]())
            for _ in range(2):
                stat([rsm[:, c * UC:(c + 1) * UC] for c in range(NU)], [upset(0)[:, c, :] for c in range(NU)])
            pe.wait_ge(lat_r, 1)
            pe.wait_ge(kpe_r, 1)
            for t in range(KT_TOK + 1):
                n = P if t < KT_TOK else NS
                wait(pe, tok_e, t - 1)
                for c in range(KC):
                    trans(bank(6 + t % 2)[0:n, c * P:(c + 1) * P], latn[:, c, t * P:t * P + n])
                trans(bank(6 + t % 2)[0:n, KR:KR + DR], kpe[:, t * P:t * P + n]).then_inc(tok_t, 1)

            pe.wait_ge(tok_e, KT_TOK + 1)
            pe.wait_ge(qn_r, 1)
            hq, h1, h2, h3, h8 = Tally(), Tally(), Tally(), Tally(), Tally()

            def head(first):
                if not first:
                    pe.wait_ge(e_ready, h8())
                    pe.wait_ge(p_t_e, h8())
                product(0, range(KQ), wide(qn_hi, qn_lo), [upset(0)[:, c, :] for c in range(NU)])
                product(1, range(KQ), wide(qn_hi, qn_lo), [upset(1)[:, c, :] for c in range(NU)])
                hq.add(16)
                pe.wait_ge(kvb_in, hq())
                if not first:
                    pe.wait_ge(pv_e, h2())
                for c in range(2):
                    for k in range(KC):
                        ins = pe.matmul(bank(6 + c), kvb[:, k, 0:DN], latn[:, k, c * 512:(c + 1) * 512],
                                        start=k == 0, stop=k == KC - 1)
                ins.then_inc(kv_mm, 1)
                fq.add()
                pe.wait_ge(set_free[0], fq())
                for t in range(KT_TOK):
                    for k in range(KC):
                        ins = pe.matmul(bank(t // 4)[:, (t % 4) * P:(t % 4 + 1) * P], latn[:, k, t * P:(t + 1) * P],
                                        kvb[:, k, DN:DN + DV], start=k == 0, stop=k == KC - 1)
                ins.then_inc(kv_mm, 1)
                for k in range(KC):
                    ins = trans(bank(2)[:, k * P:(k + 1) * P], kvb[:, k, 0:DN])
                ins.then_inc(kv_mm, 1)
                h1.add()
                pe.wait_ge(qpe_r, h1())
                pe.wait_ge(kv_e, h3(3))
                for k in range(KC):
                    ins = pe.matmul(bank(5)[:, k * NS:(k + 1) * NS], wkT[:, k, :], qno[:, TP:T], start=True, stop=True)
                ins.then_inc(kv_mm, 1)
                h3.add(3)

                def scores(q):
                    u = q % 2
                    if q >= 2:
                        pe.wait_ge(e_ready, h8(q - 1))
                    for b in range(q // 4 + 1):
                        n = min(512, (q + 1) * P - b * 512)
                        keys = slice(b * 512, b * 512 + n)
                        diag = b == q // 4
                        pe.matmul(bank(2 * u + b)[:, 0:n], qno[:, q * P:(q + 1) * P], kno[:, keys],
                                  start=True, stop=False)
                        if diag:
                            pe.matmul(bank(2 * u + b)[:, n - P:n], ident_b[:], mask_b[:], start=False, stop=False,
                                      skip_group_check=True)
                        ins = pe.matmul(bank(2 * u + b)[:, 0:n], qpe[:, q * P:(q + 1) * P], kpe[:, keys],
                                        start=False, stop=True)
                    ins.then_inc(s_mm, 1)

                def turn(q):
                    pe.wait_ge(p_ready, h8(q + 1))
                    if q == 0:
                        pe.wait_ge(qlat_r, h1())
                    else:
                        pe.wait_ge(p_t_e, h8(q))
                    for k in range(q + 1):
                        ins = trans(bank(4 + k // 4)[:, (k % 4) * P:(k % 4 + 1) * P], p_sb[q % 2][:, k * P:(k + 1) * P])
                    ins.then_inc(p_t_mm, 1)

                def values(half):
                    pe.wait_ge(p_t_e, h8(4 * half + 4))
                    n = 4 * half + 4
                    for k in range(n):
                        c = max(0, k - 4 * half) * P
                        ins = pe.matmul(bank(6 + half)[:, c:512], v_sb[:, k, :], p_t[:, k, c:512], start=k == 0,
                                        stop=k >= 4 * half, skip_group_check=True)
                    ins.then_inc(pv_mm, 1)

                scores(0)
                for q in range(1, KT_TOK):
                    scores(q)
                    turn(q - 1)
                    if q == 4:
                        values(0)
                turn(KT_TOK - 1)
                values(1)
                h8.add(8)
                h2.add(2)

            fq = Tally(SETS + 3)
            head(True)
            with loop(pe, H - 1, {uses[0]: 1, uses[1]: 1, hq: 16, h1: 1, h2: 2, h3: 3, h8: 8, fq: 1}):
                head(False)
            pe.wait_ge(qlat_r, H)
            for k in range(KC):
                pe.matmul(bank(0)[0:NS, 0:NS * H], lats[:, k, :], qlat[:, k].rearrange("p b h -> p (b h)"),
                          start=k == 0, stop=False)
            pe.matmul(bank(0)[0:NS, 0:NS * H], kpes[:], qpes[:].rearrange("p b h -> p (b h)"),
                      start=False, stop=True).then_inc(sn_mm, 1)

            pe.wait_ge(sn_e, 1)
            pe.wait_ge(pv_e, 2 * H)
            groups, seqs, seqs6, acts_n, pgs, vns = Tally(), Tally(), Tally(), Tally(), [Tally(), Tally()], [Tally(), Tally()]

            def decode_seq(b, u):
                pgs[u].add(2 * 16 * NPG)
                pe.wait_ge(pg_in[u], pgs[u]())
                wait(pe, ch_dve, seqs6(-5))

                def scores(g):
                    pe.wait_ge(kt_ea, groups())
                    pe.wait_ge(kt_ed, groups())
                    for n in range(4):
                        out = bank(6)[:, (4 * g + n) * H:(4 * g + n + 1) * H]
                        for k in range(KC):
                            pe.matmul(out, kT[g % 2][:, k, n * P:(n + 1) * P], qlat[:, k, bass.ds(b, 1), :].rearrange(
                                "p b h -> p (b h)"), start=k == 0, stop=False)
                        ins = pe.matmul(out, kT[g % 2][0:DR, 2, n * P:(n + 1) * P],
                                        qpes[:, bass.ds(b, 1), :].rearrange("p b h -> p (b h)"), start=False, stop=True)
                    ins.then_inc(sc_mm, 1)

                for g in range(8):
                    wait(pe, kt_ea, groups(-1))
                    wait(pe, kt_ed, groups(-1))
                    b0 = 3 * (g % 2)
                    for n in range(4):
                        for k in range(KC):
                            trans(bank(b0 + k)[:, n * P:(n + 1) * P], pg[u][:, 4 * g + n, k * P:(k + 1) * P])
                        ins = trans(bank(b0 + 2)[0:DR, n * P:(n + 1) * P], pgr[u][:, 4 * g + n, :])
                    ins.then_inc(kt_mm, 1)
                    if g:
                        scores(g - 1)
                    groups.add()
                scores(7)
                pe.wait_ge(ch_dve, seqs6(2))
                wait(pe, olat_r, seqs())
                seqs.add()
                trans(bank(7)[0:H, 0:P], dm[:, 0:H]).then_inc(ch_pe, 1)
                pe.wait_ge(ch_dve, seqs6(3))
                pe.matmul(bank(7)[:, P:P + H], ones[0:H, :], dm[0:H, 16:16 + H], start=True, stop=True
                          ).then_inc(ch_pe, 1)
                pe.wait_ge(ch_dve, seqs6(5))
                pe.matmul(bank(7)[:, P + H:P + 2 * H], ones[:], dm[:, 24:24 + H], start=True, stop=True
                          ).then_inc(ch_pe, 1)
                pe.wait_ge(ch_dve, seqs6(6))
                seqs6.add(6)
                for k in range(KC):
                    out = bank(7)[:, 256 + k * H:256 + (k + 1) * H]
                    for n in range(NPG):
                        pe.matmul(out, pg[u][:, n, k * P:(k + 1) * P], e_sb[u][:, n, :], start=n == 0, stop=False)
                    ins = pe.matmul(out, vnew[u][:, k * P:(k + 1) * P], e_sb[u][0:1, NPG, :], start=False, stop=True)
                ins.then_inc(dpv, 1)

            decode_seq(0, 0)
            decode_seq(1, 1)
            with loop(pe, NS // 2 - 1, {groups: 16, seqs: 2, seqs6: 12, pgs[0]: 1024, pgs[1]: 1024}) as i:
                b = pe.snap(i * 2)
                decode_seq(b + 2, 0)
                decode_seq(b + 3, 1)
            pe.wait_ge(wv_in, 32)
            pe.wait_ge(olat_r, NS)
            for h in range(H):
                for k in range(KC):
                    ins = pe.matmul(bank(0)[:, h * NS:(h + 1) * NS], wv[:, k, h, :], olat[:, k, h, :],
                                    start=k == 0, stop=k == KC - 1)
            ins.then_inc(ov_mm, 1)
            down(KD, PARTS8, True)
            f[0].add(H)
            ffn(4 * ND)
            tails(KF, 3)
            down(KF, PARTS22, False)
            pe.wait_ge(x_done, 5 * ND)
            for n in range(2 * (KT_TOK + 1)):
                t, half = n // 2, n % 2
                wait(pe, yt_e, n - 3)
                w = P if t < KT_TOK else NS
                for k in range(4):
                    ins = trans(bank(n % 4)[0:w, k * P:(k + 1) * P], xT[:, 4 * half + k, t * P:t * P + w])
                ins.then_inc(yt_mm, 1)


_INS = ["x_prompt", "x_sample", "cache_kv_latent", "cache_k_rope", "state_mixconv", "state_ffnconv", "page_table",
        "c_prompt", "c_sample", "mod_w", "mod_b", "norm_mix_pre", "norm_mix_post", "norm_ffn_pre", "norm_ffn_post",
        "sc_w_in", "sc_conv_w", "sc_w_out", "mla_w_qa", "mla_qa_norm", "mla_w_qb", "mla_w_kva", "mla_kv_norm",
        "mla_w_kvb", "mla_w_o", "ffn_w_in", "ffn_conv_w", "ffn_conv_b", "ffn_w_out"]
_FLAT = {"x_prompt", "cache_kv_latent", "cache_k_rope", "state_mixconv", "sc_w_in", "sc_conv_w", "sc_w_out",
         "mla_w_qa", "mla_w_qb", "mla_w_kva", "mla_w_kvb", "mla_w_o"}
_OUTS = [("y_prompt", (TP, D)), ("y_sample", (NS, D)), ("lat_p", (TP, KR)), ("pe_p", (TP, DR)), ("lat_s", (NS, KR)),
         ("pe_s", (NS, DR)), ("mix_p", (2, D)), ("mix_s", (NS, 2, D)), ("ffn_p", (2, 2, F)), ("ffn_s", (2, NS, 2, F))]
_SHAPES = [(1, TP, D), (NS, 1, D), (1, 1, TP, KR), (1, 1, TP, DR), (1, NS, 1, KR), (1, NS, 1, DR), (1, 1, 2, D),
           (1, NS, 2, D), (2, 1, 2, F), (2, NS, 2, F)]


def rope_table():
    half = DR // 2
    inv = np.float32(10000.0) ** (-np.arange(half, dtype=np.float32) * np.float32(2.0) / np.float32(DR))
    pos = np.concatenate([np.arange(TP), np.full(NS, PAST)]).astype(np.float32)
    ang = (inv[:, None] * pos[None, :]).astype(np.float32)
    cos, sin = np.cos(ang), np.sin(ang)
    return np.ascontiguousarray(np.concatenate([cos, cos, -sin, sin]).astype(np.float32))


def kernel(**inputs):
    import concourse.bacc as bacc
    from concourse.bass_utils import run_bass_kernel_spmd

    nc = bacc.Bacc("TRN2", target_bir_lowering=False, num_devices=1)
    arrays, ins, outs = {}, [], []
    for name in _INS:
        a = np.ascontiguousarray(inputs[name])
        if name in _FLAT:
            a = a[0]
        elif name == "x_sample":
            a = a[:, 0]
        arrays[f"in_{name}"] = a
        ins.append(nc.dram_tensor(f"in_{name}", a.shape, mybir.dt.from_np(a.dtype), kind="ExternalInput").ap())
    arrays["in_rope"] = rope_table()
    ins.append(nc.dram_tensor("in_rope", (P, T), F32, kind="ExternalInput").ap())
    for name, shape in _OUTS:
        outs.append(nc.dram_tensor(f"out_{name}", shape, F32, kind="ExternalOutput").ap())
    build(nc, ins, outs)
    r = run_bass_kernel_spmd(nc, [arrays], core_ids=[0])
    return tuple(r.results[0][f"out_{name}"].reshape(s) for (name, _), s in zip(_OUTS, _SHAPES))
```

```python
from contextlib import ExitStack, contextmanager

import numpy as np

import concourse.bass as bass
from concourse import mybir

F32 = mybir.dt.float32
F32R = mybir.dt.float32r
BF16 = mybir.dt.bfloat16
I32 = mybir.dt.int32
ALU = mybir.AluOpType
ACT = mybir.ActivationFunctionType
AX = mybir.AxisListType

P = 128
D = 1024
KD = D // P
TP = 1024
NS = 8
T = TP + NS
KT_TOK = TP // P
F = 2816
KF = F // P
UC, NU = T // 3, 3
DC, ND = T // 4, 4
PL = TP - (ND - 1) * DC
H = 8
DN, DR, DV = 128, 64, 128
QR, KR = 384, 256
KQ, KC = QR // P, KR // P
PAGE = 128
NPG = 32
PAST = PAGE * NPG
EPS = 1e-6
SCALE = float(DN + DR) ** -0.5
NEG = -1e30
TAIL = 2 + NS
MODS = 6
MLANES = 1 + NS
MB = 512


class Tally:

    def __init__(self, n=0):
        self.n, self.loops = n, []

    def __call__(self, more=0):
        value = self.n + more
        for i, per in self.loops:
            value = i * per + value
        return value

    def add(self, k=1):
        self.n += k


def wait(eng, sem, value):
    if isinstance(value, int) and value <= 0:
        return
    eng.wait_ge(sem, value)


@contextmanager
def loop(eng, trips, per):
    entry = {t: t.n for t in per}
    with eng.Fori(0, trips) as i:
        for t, k in per.items():
            t.loops.append((i, k))
        yield i
    for t, k in per.items():
        assert t.n - entry[t] == k, (t.n - entry[t], k)
        t.n += (trips - 1) * k
        t.loops.pop()


def build(nc, ins, outs):
    (x_prompt, x_sample, cache_lat, cache_pe, state_mix, state_ffn, page_table, c_prompt, c_sample, mod_w, mod_b,
     n_mix_pre, n_mix_post, n_ffn_pre, n_ffn_post, sc_w_in, sc_conv_w, sc_w_out, w_qa, qa_norm, w_qb, w_kva,
     kv_norm, w_kvb, w_o, ffn_w_in, ffn_conv_w, ffn_conv_b, ffn_w_out, rope_tab) = ins
    (y_prompt, y_sample, lat_p, pe_p, lat_s, pe_s, mix_p, mix_s, ffn_p, ffn_s) = outs

    mid_d = nc.dram_tensor("mid_d", (2, F, T), F32).ap()
    snew_d = nc.dram_tensor("snew_d", (NS, NS * H), F32).ap()

    base = (nc.sbuf_base + 63) // 64 * 64
    room = [base]

    def arena(size):
        at = room[0]
        room[0] += (size + 31) // 32 * 32
        return at

    names = set()

    def at(name, shape, off, dt=F32):
        assert name not in names
        names.add(name)
        return nc.alloc_sbuf_tensor_at(name, shape, dt, offset=off, align_bytes=8)

    T4, D4 = T * 4, DC * 4
    A_X = arena(KD * T4)
    A_H = arena(2 * KD * T4)
    A_W = arena(9 * KD * P * 4)
    A_A = arena(2 * KF * D4)
    A_O = arena(2 * KD * D4)
    A_C = arena(12 * 1024)
    assert room[0] <= nc.sbuf_usable_end, (room[0], nc.sbuf_usable_end)

    xT = at("xT", [P, KD, T], A_X)
    h_hi = at("h_hi", [P, KD, T], A_H, F32R)
    h_lo = at("h_lo", [P, KD, T], A_H + KD * T4, F32R)
    WB = KD * P * 4
    w_raw = [at(f"w_raw{s}", [P, KD, P], A_W + s * WB) for s in range(3)]
    w_hi = [at(f"w_hi{s}", [P, KD, P], A_W + (3 + s) * WB, F32R) for s in range(3)]
    w_lo = [at(f"w_lo{s}", [P, KD, P], A_W + (6 + s) * WB, F32R) for s in range(3)]
    act_hi = at("act_hi", [P, KF, DC], A_A, F32R)
    act_lo = at("act_lo", [P, KF, DC], A_A + KF * D4, F32R)
    o_sb = at("o_sb", [P, KD, DC], A_O)
    sq = at("sq", [P, KD, DC], A_O + KD * D4)
    c0 = [A_C]

    def small(name, shape, dt=F32):
        n = int(np.prod(shape[1:])) * (2 if dt == BF16 else 4)
        off = c0[0]
        c0[0] += (n + 31) // 32 * 32
        assert c0[0] <= A_C + 12 * 1024, name
        return at(name, shape, off, dt)

    modv = small("modv", [P, 2 * MODS * KD, MLANES])
    vec = small("vec", [P, 4, P])
    ident = small("ident", [P, P])
    ones = small("ones", [P, P])
    ident_b = small("ident_b", [P, P], BF16)
    mask_b = small("mask_b", [P, P], BF16)
    prev_mix = small("prev_mix", [P, KD, NS])
    prev_ffn = small("prev_ffn", [P, 2, KF, NS])
    rs = small("rs", [P, DC])
    var, root_b = small("var", [P, DC]), small("root_b", [P, DC])
    tmp_s = small("tmp_s", [P, KD, NS])
    VA, VB = vec[:, 0, :], vec[:, 1, :]
    v_modb, v_scw, v_qan, v_kvn = VA[:, 0:96], VA[:, 96:120], VA[:, 120:123], VA[:, 123:125]
    v_norm = VB[:, 0:64]
    v_cb = VB[:, 64:108]

    x_in = at("x_in", [P, KT_TOK, D], A_H)
    mod_raw = [at(f"mod_raw{b}", [P, KD, MB], A_H + KT_TOK * D * 4 + b * KD * MB * 4) for b in range(2)]
    off = A_A
    xs_in = at("xs_in", [NS, D], off); off += D * 4
    c_in = at("c_in", [MLANES, D], off); off += D * 4
    packs = at("packs", [P, 4, P], off); off += 4 * P * 4
    mix_in = at("mix_in", [2 * NS, D], off); off += D * 4
    ffn_in = at("ffn_in", [2 * NS, 2, F], off); off += 2 * F * 4
    assert off <= A_O
    csil = at("csil", [MLANES, D], A_O)
    csT = at("csT", [P, KD, MLANES], A_O + D * 4)
    ptmp = at("ptmp", [P, KF, NS], A_O + D * 4 + 512)
    off = A_A
    a_sb = at("a_sb", [P, 2 + T], off); off += (2 + T) * 4 + 24
    y_sb = at("y_sb", [P, T], off); off += T4
    g_sb = at("g_sb", [P, T], off); off += T4
    g_parts = at("g_parts", [P, 2, T], off, F32R); off += 2 * T4
    tail = at("tail", [P, KF, TAIL], off); off += KF * TAIL * 4 + 16
    tail_t = at("tail_t", [TAIL, F], off); off += F * 4
    assert off <= A_O
    off = A_A
    q_raw = at("q_raw", [P, KQ, T], off); off += KQ * T4
    l_raw = at("l_raw", [P, KC, T], off); off += KC * T4
    tab = at("tab", [P, T], off); off += T4
    p_t = at("p_t", [P, KT_TOK, 512], off); off += KT_TOK * 2048
    kvb = at("kvb", [P, KC, DN + DV], off); off += KC * (DN + DV) * 4
    assert off <= A_O
    tok = [at(f"tok{i}", [P, KR + DR], A_A + i * 1280) for i in range(2)]
    off = A_H
    qn_hi = at("qn_hi", [P, KQ, T], off, F32R); off += KQ * T4
    qn_lo = at("qn_lo", [P, KQ, T], off, F32R); off += KQ * T4
    latn = at("latn", [P, KC, T], off); off += KC * T4
    kpe = at("kpe", [DR, T], off); off += T4
    qno = at("qno", [P, T], off); off += T4
    qpe = at("qpe", [DR, T], off); off += T4
    kno = at("kno", [P, TP], off); off += TP * 4
    v_sb = at("v_sb", [P, KT_TOK, P], off); off += KT_TOK * P * 4
    p_sb = [at(f"p_sb{i}", [P, TP], off + i * TP * 4) for i in range(2)]; off += 2 * TP * 4
    wkT = at("wkT", [P, KC, P], off); off += KC * P * 4
    assert off <= A_W
    sqm = at("sqm", [P, KQ, T], A_O)
    rsm = at("rsm", [P, T], A_O + KQ * T4)
    varm = at("varm", [P, T], A_H + 2 * KQ * T4 + KC * T4 + T4)
    rootm = at("rootm", [P, T], A_H + 2 * KQ * T4 + KC * T4 + 2 * T4)
    off = A_O
    oh = [at(f"oh{i}", [P, 2, 512], off + i * 4096, F32R) for i in range(2)]; off += 8192
    rope1 = at("rope1", [DR, T], off); off += T4
    st = at("st", [P, 8, 2], off); off += 64
    qlat = at("qlat", [P, KC, NS, H], off); off += KC * 256
    qpes = at("qpes", [DR, NS, H], off); off += 256
    lats = at("lats", [P, KC, NS], off); off += KC * 32
    kpes = at("kpes", [DR, NS], off); off += 32
    sx = at("sx", [NS, NS * H], off); off += 256
    olat = at("olat", [P, KC, H, NS], off); off += KC * 256
    ovs = at("ovs", [P, 2, H, NS], off, F32R); off += 512
    dm = at("dm", [P, 8 * 6], off); off += 192
    ptab = at("ptab", [1, NS * NPG], off, I32); off += NS * NPG * 4
    assert off <= A_C
    pg = [at(f"pg{i}", [P, NPG, KR], A_H + i * NPG * KR * 4) for i in range(2)]
    off = A_A
    pgr = [at(f"pgr{i}", [P, NPG, DR], off + i * NPG * DR * 4) for i in range(2)]; off += 2 * NPG * DR * 4
    kT = [at(f"kT{i}", [P, 3, 512], off + i * 6144) for i in range(2)]; off += 2 * 6144
    s_sb = [at(f"s_sb{i}", [P, NPG + 1, H], off + i * 1056) for i in range(2)]; off += 2112
    e_sb = [at(f"e_sb{i}", [P, NPG + 1, H], off + i * 1056) for i in range(2)]; off += 2112
    vnew = [at(f"vnew{i}", [1, KR], off + i * 1024) for i in range(2)]; off += 2048
    assert off <= A_O
    y_tok = [at(f"y_tok{i}", [P, D], A_H + i * D * 4) for i in range(2)]
    wv = at("wv", [P, KC, H, DV], A_A)

    with ExitStack() as ctx:
        ps = ctx.enter_context(nc.psum_tensor("ps", [P, 8, 512], F32))

        def bank(b):
            return ps[:, b, :]

        def upset(s):
            return ps[:, 3 * s:3 * s + NU, 0:UC]

        def chunked(ap):
            return ap.rearrange("p (c n) -> p c n", c=NU)

        def sem(name):
            return ctx.enter_context(nc.semaphore(name))

        const_ready = sem("const_ready")
        vec_in, c_loaded, mix_loaded, ffn_loaded = sem("vec_in"), sem("c_loaded"), sem("mix_loaded"), sem("ffn_loaded")
        x_loaded, xs_loaded, state_out = sem("x_loaded"), sem("xs_loaded"), sem("state_out")
        csil_ready = sem("csil_ready")
        setup_t, setup_e = sem("setup_t"), sem("setup_e")
        xt_t, xt_e = sem("xt_t"), sem("xt_e")
        mod_loaded = [sem("mod_loaded0"), sem("mod_loaded1")]
        mod_mm, mod_done = sem("mod_mm"), sem("mod_done")
        raw_ready = [sem(f"raw_ready{s}") for s in range(3)]
        hi_ready = [sem(f"hi_ready{s}") for s in range(3)]
        w_ready = [sem(f"w_ready{s}") for s in range(3)]
        w_done = [sem(f"w_done{s}") for s in range(3)]
        set_free = [sem("set_free0"), sem("set_free1")]
        conv_done, act_done, g_ready, g_out = sem("conv_done"), sem("act_done"), sem("g_ready"), sem("g_out")
        gh_ready, gl_ready = sem("gh_ready"), sem("gl_ready")
        tail_ready, tail_t_done, tail_e, tail_out = sem("tail_ready"), sem("tail_t_done"), sem("tail_e"), sem("tail_out")
        act_in = [sem(f"act_in{n}") for n in range(3)]
        var_ready, root_ready = sem("var_ready"), sem("root_ready")
        sq_ready, ss_ready, stat_ready = sem("sq_ready"), sem("ss_ready"), sem("stat_ready")
        x_done, t_ready, hh_ready, h_ready = sem("x_done"), sem("t_ready"), sem("hh_ready"), sem("h_ready")
        dve_step, act_step = sem("dve_step"), sem("act_step")
        tab_in, kvb_in = sem("tab_in"), sem("kvb_in")
        qn_r, lat_r, kpe_r = sem("qn_r"), sem("lat_r"), sem("kpe_r")
        qn_t = sem("qn_t")
        tok_t, tok_e, tok_out = sem("tok_t"), sem("tok_e"), [sem("tok_out0"), sem("tok_out1")]
        qpe_r, qlat_r = sem("qpe_r"), sem("qlat_r")
        kv_mm, kv_e = sem("kv_mm"), sem("kv_e")
        s_mm, nm_ready, e_ready, p_ready = sem("s_mm"), sem("nm_ready"), sem("e_ready"), sem("p_ready")
        p_t_mm, p_t_e, pv_mm, pv_e = sem("p_t_mm"), sem("p_t_e"), sem("pv_mm"), sem("pv_e")
        pv_h, ov_h = sem("pv_h"), sem("ov_h")
        head_out = [sem("head_out0"), sem("head_out1")]
        sn_c, sn_mm, sn_e, sn_out, pt_in = sem("sn_c"), sem("sn_mm"), sem("sn_e"), sem("sn_out"), sem("pt_in")
        pg_in, vn_in = [sem("pg_in0"), sem("pg_in1")], [sem("vn_in0"), sem("vn_in1")]
        kt_mm, kt_ea, kt_ed, sc_mm = sem("kt_mm"), sem("kt_ea"), sem("kt_ed"), sem("sc_mm")
        ch_pe, ch_dve, ch_act, dpv, olat_r = sem("ch_pe"), sem("ch_dve"), sem("ch_act"), sem("dpv"), sem("olat_r")
        neg_ready, wv_in, ov_mm, ov_e, ov_out = (sem("neg_ready"), sem("wv_in"), sem("ov_mm"), sem("ov_e"),
                                                 sem("ov_out"))
        yt_mm, yt_e, y_out = sem("yt_mm"), sem("yt_e"), [sem("y_out0"), sem("y_out1")]

        SETS = 3 * KD // 2 + KF
        NORMS = ND + 4 * ND
        PARTS8 = [(0, 4), (4, 8)]
        PARTS22 = [(0, 8), (8, 16), (16, 22)]

        def down_steps(parts):
            steps = []
            for m in range(0, KD, 2):
                for n, (k0, k1) in enumerate(parts):
                    for u in range(2):
                        steps.append((m + u, n, len(steps) % len(parts), k0, k1))
            return steps

        def down_counts(parts):
            return [(s, KD) for s in range(len(parts))]

        def first_blocks(parts):
            return [(s, k1 - k0) for _, _, s, k0, k1 in down_steps(parts)[:len(parts)]]

        DOWN_BANK = [0, 1, 2, 3, 4, 5, 7, 2]
        DOWN_AGO = [8, 8, 3, 8, 8, 8, 8, 5]

        def block_cols(w, c):
            return w[:, bass.ds(c, P)].rearrange("(k p) m -> p k m", p=P)

        block = ctx.enter_context(nc.Block())

        @block.sync
        def _(sp):
            raws = [Tally() for _ in range(3)]

            def load(slot, dst, src):
                wait(sp, w_ready[slot], raws[slot]())
                sp.dma_start(dst, src).then_inc(raw_ready[slot], 16)
                raws[slot].add()

            def load_block(slot, w, c):
                load(slot, w_raw[slot][:], block_cols(w, c))

            def vrows(t, r0, src):
                sp.dma_start(packs[r0:r0 + src.shape[0], t, :], src).then_inc(vec_in, 16)

            sp.dma_start(c_in[0:1, :], c_prompt).then_inc(c_loaded, 16)
            sp.dma_start(c_in[1:MLANES, :], c_sample).then_inc(c_loaded, 16)
            vrows(0, 0, mod_b.rearrange("l (m p) -> (l m) p", p=P))
            vrows(0, 96, sc_conv_w.rearrange("k (m p) -> (k m) p", p=P))
            vrows(0, 120, qa_norm.rearrange("l (m p) -> (l m) p", p=P))
            vrows(0, 123, kv_norm.rearrange("l (m p) -> (l m) p", p=P))
            for n, v in enumerate((n_mix_pre, n_mix_post, n_ffn_pre, n_ffn_post)):
                vrows(1, 16 * n, v.rearrange("l (m p) -> (l m) p", p=P))
            vrows(1, 64, ffn_conv_b.rearrange("l (m p) -> (l m) p", p=P))
            for l in range(2):
                vrows(2 + l, 0, ffn_conv_w[l].rearrange("k (m p) -> (k m) p", p=P))
            sp.dma_start(mix_in[:], state_mix.rearrange("b k d -> (b k) d")).then_inc(mix_loaded, 16)
            sp.dma_start(ffn_in[:], state_ffn.rearrange("l b k d -> (b k) l d")).then_inc(ffn_loaded, 16)
            sp.dma_start(x_in[:], x_prompt.rearrange("(t p) d -> p t d", p=P)).then_inc(x_loaded, 16)
            sp.dma_start(xs_in[:], x_sample).then_inc(xs_loaded, 16)
            mods = Tally(1)
            for l in range(2):
                with loop(sp, MODS, {mods: 2}) as i:
                    for b in range(2):
                        c = sp.snap(i * (2 * MB) + b * MB)
                        sp.wait_ge(mod_mm, mods())
                        mods.add()
                        sp.dma_start(mod_raw[b][:], mod_w[l][:, bass.ds(c, MB)].rearrange("(k p) m -> p k m", p=P)
                                     ).then_inc(mod_loaded[b], 16)
            for s, c in ((0, D), (1, 2 * D), (2, 0)):
                load(s, w_raw[s][:], block_cols(sc_w_in, c))
            with loop(sp, KD - 1, {raws[0]: 1, raws[1]: 1, raws[2]: 1}) as i:
                for s, c in ((0, D), (1, 2 * D), (2, 0)):
                    cc = sp.snap(i * P + (c + P))
                    load_block(s, sc_w_in, cc)

            def loads_down(w, parts, guards):
                src = w.rearrange("(k p) m -> p k m", p=P)
                with loop(sp, ND, {raws[s]: KD for s in range(len(parts))}) as d:
                    col = sp.snap(d * DC)
                    for n, (m, part, s, k0, k1) in enumerate(down_steps(parts)):
                        load(s, w_raw[s][:, 0:k1 - k0, :], src[:, k0:k1, m * P:(m + 1) * P])
                        if n < 2 * len(parts) and n % 2 == 1:
                            p = n // 2
                            k0, k1 = parts[p]
                            if p == 0:
                                for g, v in guards:
                                    sp.wait_ge(g, v)
                            sp.wait_ge(w_done[s], raws[s](-2))
                            for z, dst in enumerate((act_hi, act_lo)):
                                sp.dma_start(dst[:, k0:k1, :].bitcast(F32), mid_d[z, k0 * P:k1 * P, bass.ds(col, DC)].rearrange(
                                    "(k p) c -> p k c", p=P)).then_inc(act_in[p], 16)

            def loads_ffn(l, guards):
                with loop(sp, KF, {raws[0]: 1, raws[1]: 1}) as i:
                    for s in range(2):
                        cc = sp.snap(i * P + s * F)
                        load_block(s, ffn_w_in[l], cc)
                loads_down(ffn_w_out[l], PARTS22, guards)

            loads_down(sc_w_out, PARTS8, [(g_out, 16 * KD), (tail_out, 32)])
            loads_ffn(0, [(g_out, 16 * (KD + KF)), (tail_out, 64)])
            for m in range(KQ):
                load(m, w_raw[m][:], block_cols(w_qa, m * P))
            for m in range(KC):
                load(m, w_raw[m][:], block_cols(w_kva, m * P))
            src = w_kva.rearrange("(k p) m -> p k m", p=P)
            wait(sp, w_ready[2], raws[2]())
            for d0, c, n in ((0, KR, DR), (DR, KR + DR // 2, DR // 2), (DR + DR // 2, KR, DR // 2)):
                sp.dma_start(w_raw[2][:, :, d0:d0 + n], src[:, :, c:c + n]).then_inc(raw_ready[2], 16)
            raws[2].add()
            wait(sp, w_done[2], raws[2](-2))
            sp.dma_start(tab[:], rope_tab).then_inc(tab_in, 16)
            qsrc = w_qb.rearrange("(k p) m -> p k m", p=P)
            ksrc = w_kvb.rearrange("(k p) m -> p k m", p=P)

            def head_loads(h, first):
                cols = [h * (DN + DR), h * (DN + DR) + DN, h * (DN + DR) + (DN + DR // 2), h * (DN + DV)]
                if not first:
                    cols = [sp.snap(c) for c in cols]
                load(0, w_raw[0][:, 0:KQ, :], qsrc[:, :, bass.ds(cols[0], P)])
                wait(sp, w_ready[1], raws[1]())
                for d0, c, n in ((0, cols[1], DR), (DR, cols[2], DR // 2), (DR + DR // 2, cols[1], DR // 2)):
                    sp.dma_start(w_raw[1][:, 0:KQ, d0:d0 + n], qsrc[:, :, bass.ds(c, n)]).then_inc(raw_ready[1], 16)
                raws[1].add()
                if not first:
                    sp.wait_ge(kv_mm, kvs())
                    kvs.add(4)
                sp.dma_start(kvb[:], ksrc[:, :, bass.ds(cols[3], DN + DV)]).then_inc(kvb_in, 16)

            kvs = Tally(3)
            head_loads(0, True)
            with loop(sp, H - 1, {raws[0]: 1, raws[1]: 1, kvs: 4}) as h:
                head_loads(h + 1, False)
            sp.dma_start(ptab[:], page_table.rearrange("(a b) n -> a (b n)", a=1)).then_inc(pt_in, 16)
            sp.wait_ge(pt_in, 16)
            sp.wait_ge(pv_mm, 2 * H)
            sp.wait_ge(qlat_r, H)
            sp.wait_ge(sn_out, 16)
            sp.wait_ge(neg_ready, 2)
            sp.wait_ge(tok_out[0], 16 * 10)
            seqs = Tally(1)
            with loop(sp, NS // 2, {seqs: 2}) as i:
                for u in range(2):
                    nb = i * 2 + u
                    e0 = sp.snap(nb * NPG)
                    r1 = sp.snap(nb)
                    r2 = sp.snap(nb * (NS * H + H))
                    sp.wait_ge(dpv, seqs())
                    seqs.add()
                    sp.dma_start(vnew[u][:], lat_s[bass.ds(r1, 1), :]).then_inc(vn_in[u], 16)
                    sp.dma_start(s_sb[u][0:1, NPG, :],
                                 snew_d.rearrange("(a b) n -> a (b n)", a=1)[:, bass.ds(r2, H)]).then_inc(vn_in[u], 16)
                    with sp.Fori(0, NPG) as j:
                        page = sp.value_load(ptab[0:1, bass.ds(e0 + j, 1)], min_val=0, max_val=cache_lat.shape[0] - 1)
                        sp.dma_start(pg[u][:, bass.ds(j, 1), :],
                                     cache_lat[bass.ds(page, 1)].rearrange("a p c -> p a c")).then_inc(pg_in[u], 16)
                        sp.dma_start(pgr[u][:, bass.ds(j, 1), :],
                                     cache_pe[bass.ds(page, 1)].rearrange("a p c -> p a c")).then_inc(pg_in[u], 16)
            sp.wait_ge(dpv, NS + 2)
            for c in range(KC):
                sp.dma_start(wv[:, c], w_kvb[c * P:(c + 1) * P, :].rearrange("p (h n) -> p h n", h=H)[:, :, DN:DN + DV]
                             ).then_inc(wv_in, 16)
            sp.wait_ge(ov_e, 1)
            for z in range(2):
                sp.dma_start(mid_d[z, 0:H * DV, TP:T].rearrange("(h p) b -> p h b", p=P), ovs[:, z].bitcast(F32)
                             ).then_inc(ov_out, 16)
            loads_down(w_o, PARTS8, [(head_out[0], 16 * H), (head_out[1], 16 * H), (ov_out, 32)])
            loads_ffn(1, [(g_out, 16 * (KD + 2 * KF)), (tail_out, 96)])
            for t in range(KT_TOK + 1):
                sp.wait_ge(yt_e, 2 * (t + 1))
                if t < KT_TOK:
                    sp.dma_start(y_prompt[t * P:(t + 1) * P, :], y_tok[t % 2][:]).then_inc(y_out[t % 2], 16)
                else:
                    sp.dma_start(y_sample, y_tok[t % 2][0:NS, :]).then_inc(y_out[t % 2], 16)
            sp.wait_ge(y_out[0], 16 * 5)
            sp.wait_ge(y_out[1], 16 * 4)

        @block.gpsimd
        def _(pool):
            pool.memset(ones[:], 1.0)
            pool.memset(ident[:], 0.0).then_inc(const_ready, 1)
            pool.memset(mask_b[:], 0.0).then_inc(const_ready, 1)
            pool.wait_ge(const_ready, 2)
            pool.affine_select(out=ident[:], in_=ident[:], compare_op=ALU.not_equal, fill=1.0, base=0,
                               pattern=[[-1, P]], channel_multiplier=1).then_inc(const_ready, 1)
            pool.affine_select(out=mask_b[:], in_=mask_b[:], compare_op=ALU.is_ge, fill=NEG, base=0,
                               pattern=[[-1, P]], channel_multiplier=1).then_inc(const_ready, 1)
            pool.wait_ge(const_ready, 4)
            pool.tensor_copy(ident_b[:], ident[:]).then_inc(const_ready, 1)
            stores = Tally()

            pool.dma_start(mix_s[:, 0:1, :], state_mix[:, 1:2, :]).then_inc(state_out, 16)
            for l in range(2):
                pool.dma_start(ffn_s[l, :, 0:1, :], state_ffn[l, :, 1:2, :]).then_inc(state_out, 16)

            def store_g(n):
                with loop(pool, n, {stores: 1}) as i:
                    r = pool.snap(i * P)
                    pool.wait_ge(gl_ready, stores(1))
                    pool.dma_start(mid_d[:, bass.ds(r, P), :].rearrange("z p t -> p z t"), g_parts[:].bitcast(F32)
                                   ).then_inc(g_out, 16)
                    stores.add()

            def store_tail(f, dst_p, dst_s, n):
                pool.wait_ge(tail_e, n)
                pool.dma_start(dst_p, tail_t[0:2, 0:f]).then_inc(tail_out, 16)
                pool.dma_start(dst_s, tail_t[2:TAIL, 0:f]).then_inc(tail_out, 16)

            store_g(KD)
            store_tail(D, mix_p, mix_s[:, 1, :], 2)
            store_g(KF)
            store_tail(F, ffn_p[0], ffn_s[0, :, 1, :], 8)
            for t in range(KT_TOK + 1):
                pool.wait_ge(tok_e, t + 1)
                n = P if t < KT_TOK else NS
                dl = lat_p[t * P:(t + 1) * P, :] if t < KT_TOK else lat_s
                dp = pe_p[t * P:(t + 1) * P, :] if t < KT_TOK else pe_s
                pool.dma_start(dl, tok[t % 2][0:n, 0:KR]).then_inc(tok_out[t % 2], 16)
                pool.dma_start(dp, tok[t % 2][0:n, KR:KR + DR]).then_inc(tok_out[t % 2], 16)
            with loop(pool, H, {}) as h:
                r = pool.snap(h * DV)
                for half in range(2):
                    pool.wait_ge(pv_e, h * 2 + (half + 1))
                    pool.dma_start(mid_d[:, bass.ds(r, DV), half * 512:(half + 1) * 512].rearrange(
                        "z p t -> p z t"), oh[half][:].bitcast(F32)).then_inc(head_out[half], 16)
            pool.wait_ge(sn_e, 1)
            pool.dma_start(snew_d, sx[:]).then_inc(sn_out, 16)
            store_g(KF)
            store_tail(F, ffn_p[1], ffn_s[1, :, 1, :], 14)
            pool.wait_ge(tail_out, 16 * 6)
            pool.wait_ge(state_out, 16 * 3)
            pool.wait_ge(tok_out[0], 16 * 10)
            pool.wait_ge(tok_out[1], 16 * 8)

        @block.scalar
        def _(act):
            splits = [Tally() for _ in range(3)]
            raw_n = [Tally() for _ in range(3)]
            pres, steps, roots = Tally(), Tally(), Tally()

            def hi_split(s, k, dmas=1):
                raw_n[s].add(16 * dmas)
                act.wait_ge(raw_ready[s], raw_n[s]())
                wait(act, w_done[s], splits[s]())
                act.activation(w_hi[s][:, 0:k, :], w_raw[s][:, 0:k, :], ACT.Copy).then_inc(hi_ready[s], 1)
                splits[s].add()

            def split_next(blocks):
                for b in blocks:
                    hi_split(*b)

            act.preload_act_table(ACT.Silu)
            act.wait_ge(c_loaded, 32)
            act.activation(csil[:], c_in[:], ACT.Silu).then_inc(csil_ready, 1)
            n = 0
            for t in range(KT_TOK + 1):
                w = P if t < KT_TOK else NS
                for half in range(2):
                    act.wait_ge(xt_t, n + 1)
                    act.activation(xT[:, 4 * half:4 * half + 4, t * P:t * P + w],
                                   bank(5 + n % 3).rearrange("p (k t) -> p k t", k=4)[:, :, 0:w], ACT.Copy
                                   ).then_inc(xt_e, 1)
                    n += 1

            def pre_squares(cols):
                act.wait_ge(x_done, pres(1))
                act.activation(sq[:], xT[:, :, cols], ACT.Square).then_inc(sq_ready, 1)

            def pre_round(cols):
                act.wait_ge(t_ready, pres(1))
                act.activation(h_hi[:, :, cols], sq[:], ACT.Copy).then_inc(hh_ready, 1)
                pres.add()

            def square_root(v=var, w=root_b):
                act.wait_ge(var_ready, roots(1))
                roots.add()
                act.activation(w[:], v[:], ACT.Sqrt).then_inc(root_ready, 1)

            def post_squares():
                act.wait_ge(act_step, steps())
                act.activation(sq[:], o_sb[:], ACT.Square).then_inc(sq_ready, 1)

            act.wait_ge(xt_e, 2 * (KT_TOK + 1))
            for d in range(ND):
                if d:
                    act.wait_ge(h_ready, d)
                pre_squares(slice(d * DC, (d + 1) * DC))
                square_root()
                pre_round(slice(d * DC, (d + 1) * DC))

            def down(parts, nxt, last_norm):
                order, ahead = down_steps(parts), len(parts)

                def tiles(m0, m1, nxt_blocks=None):
                    for n, (m, _, s, _, _) in enumerate(order):
                        if m0 <= m < m1:
                            if n + ahead >= len(order) and nxt_blocks is not None:
                                continue
                            _, _, s, k0, k1 = order[(n + ahead) % len(order)]
                            hi_split(s, k1 - k0)
                    if m1 == KD and nxt_blocks is not None:
                        split_next(nxt_blocks)

                def evac(m0, m1):
                    for m in range(m0, m1):
                        s = [s for m_, _, s, _, _ in order if m_ == m][-1]
                        act.wait_ge(w_done[s], done[s](m // 2 * 2 + 2))
                        act.activation(o_sb[:, m, :], bank(DOWN_BANK[m])[:, 0:DC], ACT.Copy).then_inc(act_step, 1)
                        steps.add()
                        if m == KD - 1:
                            for t in done.values():
                                t.add(KD)

                def chunk(prev_cols, nxt_blocks=None):
                    tiles(0, 2)
                    if prev_cols is not None:
                        square_root()
                        act.wait_ge(x_done, pres(1))
                    evac(0, 2)
                    if prev_cols is not None and not last_norm:
                        pre_squares(prev_cols)
                    tiles(2, 4)
                    evac(2, 4)
                    tiles(4, 6)
                    evac(4, 6)
                    if prev_cols is not None:
                        if last_norm:
                            pres.add()
                        else:
                            square_root()
                            pre_round(prev_cols)
                    tiles(6, 8, nxt_blocks)
                    evac(6, 8)
                    if prev_cols is not None and not last_norm:
                        act.wait_ge(h_ready, pres())
                    post_squares()

                done = {s: Tally(splits[s].n - 1) for s in range(len(parts))}
                per = {splits[s]: KD for s in done}
                per.update({raw_n[s]: 16 * KD for s in done})
                per.update({t: KD for t in done.values()})
                act.preload_act_table(ACT.Sqrt)
                chunk(None)
                per.update({steps: KD, pres: 1, roots: 1 if last_norm else 2})
                with loop(act, ND - 2, per) as i:
                    c = act.snap(i * DC)
                    chunk(bass.ds(c, DC))
                chunk(slice((ND - 2) * DC, (ND - 1) * DC), nxt)
                cols = slice((ND - 1) * DC, T)
                square_root()
                if last_norm:
                    pres.add()
                else:
                    pre_squares(cols)
                    square_root()
                    pre_round(cols)

            conv_base = [0]
            gs, g_n = Tally(), Tally()

            def up_run(n, n_slots, ffn_layer, nxt):
                own = [(s, KD) for s in range(n_slots)]
                convs = Tally(conv_base[0])

                def body(j, blocks, parity):
                    for s in range(n_slots):
                        if s == 0:
                            act.wait_ge(w_done[0], splits[0]())
                        if blocks is own:
                            hi_split(s, KD)
                        if s == 0:
                            wait(act, conv_done, convs())
                            act.activation(chunked(a_sb[:, 2:2 + T]), upset(parity), ACT.Copy
                                           ).then_inc(set_free[parity], 1)
                            convs.add()
                            if ffn_layer is not None:
                                act.wait_ge(conv_done, convs())
                                act.activation(y_sb[:], y_sb[:], ACT.Silu,
                                               bias=v_cb[:, bass.ds(j + ffn_layer * KF, 1)]).then_inc(act_done, 1)
                    gs.add()
                    act.wait_ge(g_ready, gs())
                    wait(act, g_out, g_n())
                    g_n.add(16)
                    act.activation(g_parts[:, 0, :], g_sb[:], ACT.Copy).then_inc(gh_ready, 1)
                    if blocks is not own:
                        split_next(blocks)

                per = {splits[s]: 1 for s in range(n_slots)}
                per.update({raw_n[s]: 16 for s in range(n_slots)})
                per.update({convs: 1, gs: 1, g_n: 16})
                if n_slots == 2:
                    with loop(act, n - 1, per) as i:
                        body(i, own, 0)
                    body(n - 1, nxt, 0)
                else:
                    with loop(act, n // 2 - 1, {t: 2 * k for t, k in per.items()}) as i:
                        body(None, own, 0)
                        body(None, own, 1)
                    body(None, own, 0)
                    body(None, nxt, 1)
                conv_base[0] = convs.n

            split_next([(0, KD), (1, KD), (2, KD)])
            P8, P22 = first_blocks(PARTS8), first_blocks(PARTS22)
            up_run(KD, 3, None, P8)
            down(PARTS8, [(0, KD), (1, KD)], False)
            act.preload_act_table(ACT.Silu)
            up_run(KF, 2, 0, P22)
            down(PARTS22, [(0, KD), (1, KD), (2, KD)], False)

            for m in range(KQ + KC):
                s = m % 3
                act.wait_ge(w_done[s], splits[s]())
                if m < 3:
                    hi_split(s, KD, 3 if m == 2 else 1)
                dst = q_raw[:, m, :] if m < KQ else l_raw[:, m - KQ, :]
                act.activation(chunked(dst), upset(m % 2), ACT.Copy).then_inc(set_free[m % 2], 1)
            act.wait_ge(set_free[0], SETS + 2)
            act.wait_ge(set_free[1], SETS + 1)
            act.activation(sqm[:], q_raw[:], ACT.Square).then_inc(sq_ready, 1)
            act.wait_ge(ss_ready, NORMS + 1)
            act.wait_ge(set_free[1], SETS + 2)
            act.wait_ge(set_free[0], SETS + 3)
            act.activation(sqm[:, 0:KC, :], l_raw[:], ACT.Square).then_inc(sq_ready, 1)
            act.wait_ge(w_done[2], splits[2]())
            square_root(varm, rootm)
            act.wait_ge(qn_t, 1)
            act.activation(qn_hi[:], q_raw[:], ACT.Copy).then_inc(hh_ready, 1)
            square_root(varm, rootm)

            act.preload_act_table(ACT.Exp)
            hi_split(0, KQ)
            hi_split(1, KQ, 3)

            def head(more):
                act.wait_ge(w_done[0], splits[0]())
                if more:
                    hi_split(0, KQ)
                act.activation(chunked(qno[:]), upset(0), ACT.Copy).then_inc(set_free[0], 1)
                act.wait_ge(w_done[1], splits[1]())
                if more:
                    hi_split(1, KQ, 3)
                act.wait_ge(kv_mm, h4(1))
                act.activation(kno[:].rearrange("p (c n) -> p c n", c=2), ps[:, 6:8, :], ACT.Copy).then_inc(kv_e, 1)
                act.wait_ge(kv_mm, h4(2))
                act.activation(v_sb[:].rearrange("p (c t) v -> p c (t v)", c=2), ps[:, 0:2, :], ACT.Copy
                               ).then_inc(kv_e, 1)
                act.wait_ge(kv_mm, h4(3))
                act.activation(wkT[:].rearrange("p c n -> p (c n)"), bank(2)[:, 0:KC * P], ACT.Copy
                               ).then_inc(kv_e, 1)
                h4.add(4)

                def exp(q):
                    nk = (q + 1) * P
                    act.wait_ge(nm_ready, h8(q + 1))
                    wait(act, p_t_mm, h8(q - 1))
                    act.activation(p_sb[q % 2][:, 0:nk], ps[:, 2 * (q % 2):2 * (q % 2) + 2, :].rearrange(
                        "p b n -> p (b n)")[:, 0:nk], ACT.Exp, bias=st[:, 2 + q % 2, 0:1], scale=SCALE,
                        accum_out=st[:, 4 + q % 2, 0:1]).then_inc(e_ready, 1)

                def evac_t(q):
                    act.wait_ge(p_t_mm, h8(q + 1))
                    if q in (0, 4):
                        wait(act, pv_mm, h2(q // 4))
                    ins = None
                    for b in range(q // 4 + 1):
                        k0, k1 = 4 * b, min(4 * b + 4, q + 1)
                        ins = act.activation(p_t[:, k0:k1, (q % 4) * P:(q % 4 + 1) * P],
                                             bank(4 + b)[:, 0:(k1 - k0) * P].rearrange("p (k n) -> p k n", n=P),
                                             ACT.Copy)
                    ins.then_inc(p_t_e, 1)

                def evac_o(half):
                    act.wait_ge(pv_mm, h2(half + 1))
                    wait(act, head_out[half], h16())
                    act.activation(oh[half][:, 0, :], bank(6 + half), ACT.Copy).then_inc(pv_h, 1)

                exp(0)
                for q in range(1, KT_TOK):
                    exp(q)
                    if q == 5:
                        evac_o(0)
                    evac_t(q - 1)
                evac_t(KT_TOK - 1)
                evac_o(1)
                h8.add(8)
                h2.add(2)
                h16.add(16)

            h4, h8, h2, h16 = Tally(), Tally(), Tally(), Tally()
            head(True)
            with loop(act, H - 2, {splits[0]: 1, splits[1]: 1, raw_n[0]: 16, raw_n[1]: 48, h4: 4, h8: 8, h2: 2,
                                   h16: 16}):
                head(True)
            head(False)

            groups = Tally()
            seqs = Tally()
            act.wait_ge(neg_ready, 2)

            def decode_seq(u):
                for g in range(8):
                    b0 = 3 * (g % 2)
                    act.wait_ge(kt_mm, groups(1))
                    wait(act, sc_mm, groups(-1))
                    act.activation(kT[g % 2][:, 0, :], bank(b0), ACT.Copy)
                    act.activation(kT[g % 2][0:DR, 2, :], bank(b0 + 2)[0:DR, :], ACT.Copy).then_inc(kt_ea, 1)
                    groups.add()
                act.wait_ge(ch_dve, seqs(4))
                seqs.add(6)
                act.activation(e_sb[u][:], e_sb[u][:], ACT.Exp, scale=SCALE).then_inc(ch_act, 1)

            decode_seq(0)
            decode_seq(1)
            with loop(act, NS // 2 - 1, {groups: 16, seqs: 12}):
                decode_seq(0)
                decode_seq(1)
            act.wait_ge(ov_mm, 1)
            act.activation(ovs[:, 0], bank(0)[:, 0:H * NS].rearrange("p (h b) -> p h b", h=H), ACT.Copy
                           ).then_inc(ov_h, 1)
            split_next(P8)
            down(PARTS8, [(0, KD), (1, KD)], False)
            act.preload_act_table(ACT.Silu)
            up_run(KF, 2, 1, P22)
            down(PARTS22, [], True)
            for n in range(2 * (KT_TOK + 1)):
                t, half = n // 2, n % 2
                w = P if t < KT_TOK else NS
                act.wait_ge(yt_mm, n + 1)
                if t >= 2:
                    act.wait_ge(y_out[t % 2], 16 * (t // 2))
                act.activation(y_tok[t % 2][0:w, half * 512:(half + 1) * 512], bank(n % 4)[0:w, :], ACT.Copy
                               ).then_inc(yt_e, 1)

        @block.vector
        def _(dve):
            steps = Tally()
            splits = [Tally() for _ in range(3)]
            stats, pres = Tally(), Tally()

            def step(ins):
                ins.then_inc(dve_step, 1)
                steps.add()

            def settle():
                dve.wait_ge(dve_step, steps())

            def lo_split(s, k, dmas=1):
                dve.wait_ge(hi_ready[s], splits[s](1))
                dve.tensor_tensor(w_lo[s][:, 0:k, :], w_raw[s][:, 0:k, :], w_hi[s][:, 0:k, :].bitcast(F32),
                                  ALU.subtract).then_inc(w_ready[s], 1)
                splits[s].add()

            def split_next(blocks):
                for b in blocks:
                    lo_split(*b)

            dve.wait_ge(setup_t, 1)
            for t, r in enumerate((125, 108, 66, 66)):
                step(dve.tensor_copy(vec[:, t, 0:r], bank(0)[:, t * P:t * P + r]))
            dve.wait_ge(setup_t, 2)
            dve.tensor_copy(csT[:], bank(1)[:, 0:KD * MLANES].rearrange("p (k c) -> p k c", k=KD)).then_inc(setup_e, 1)
            settle()

            def taps(b, kt, w, dst):
                state = bank(b)[:, 0:kt * 2 * NS].rearrange("p (m b k) -> p m b k", m=kt, b=NS)
                for k, out in ((0, dst), (1, ptmp[:, 0:kt, :])):
                    step(dve.tensor_tensor(out, state[:, :, :, k],
                                           w[:, k * kt:(k + 1) * kt].unsqueeze(2).to_broadcast([P, kt, NS]), ALU.mult))
                settle()
                step(dve.tensor_tensor(dst, dst, ptmp[:, 0:kt, :], ALU.add))
                settle()

            dve.wait_ge(setup_t, 3)
            taps(2, KD, v_scw, prev_mix[:])
            for l in range(2):
                dve.wait_ge(setup_t, 4 + l)
                taps(3 + l, KF, vec[:, 2 + l, :], prev_ffn[:, l])
            dve.sem_inc(setup_e, 1)

            mods = Tally(2)
            with loop(dve, MODS, {mods: 4}) as i:
                for b in range(4):
                    mods.add()
                    dve.wait_ge(mod_mm, mods())
                    m0 = i * 16 + 4 * b
                    dve.tensor_tensor(modv[:, bass.ds(m0, 4), :],
                                      bank(b % 2)[:, 0:4 * MLANES].rearrange("p (m c) -> p m c", m=4),
                                      v_modb[:, bass.ds(m0, 4)].unsqueeze(2).to_broadcast([P, 4, MLANES]),
                                      ALU.add).then_inc(mod_done, 1)
            dve.wait_ge(mod_done, 4 * MODS)

            def mod(l, kind):
                return modv[:, (l * MODS + kind) * KD:(l * MODS + kind + 1) * KD, :]

            def gain(n, l):
                return v_norm[:, (2 * n + l) * KD:(2 * n + l + 1) * KD].unsqueeze(2).to_broadcast([P, KD, MLANES])

            for l in range(2):
                for s in range(2):
                    step(dve.scalar_tensor_tensor(mod(l, 3 * s + 1), mod(l, 3 * s + 1), 1.0, gain(2 * s, l),
                                                  ALU.add, ALU.mult))
                    step(dve.tensor_tensor(mod(l, 3 * s + 2), mod(l, 3 * s + 2), gain(2 * s + 1, l), ALU.mult))
            settle()

            def rsqrt(dst, v, w, src, n):
                dve.wait_ge(stat_ready, stats(1))
                stats.add()
                dve.tensor_scalar(v, src, 1.0 / n, EPS, ALU.mult, ALU.add).then_inc(var_ready, 1)
                dve.wait_ge(root_ready, stats())
                newton(dst, v, w)

            def newton(dst, v, w):
                step(dve.reciprocal(dst, w))
                settle()
                step(dve.tensor_tensor(w, dst, v, ALU.mult))
                settle()
                step(dve.scalar_tensor_tensor(w, w, -0.5, dst, ALU.mult, ALU.mult))
                settle()
                step(dve.scalar_tensor_tensor(dst, w, 1.5, dst, ALU.add, ALU.mult))
                settle()

            def sum_squares(src, dst):
                dve.wait_ge(sq_ready, stats(1))
                dve.tensor_reduce(dst, src.rearrange("p k t -> p t k"), AX.X, ALU.add).then_inc(ss_ready, 1)

            def root(n):
                rsqrt(rs[:], var[:], root_b[:], bank(6)[:, 0:DC], n)

            def pre_norm(l, s, cols, last):
                root(D)
                step(dve.tensor_tensor(sq[:], xT[:, :, cols], rs[:].unsqueeze(1).to_broadcast([P, KD, DC]), ALU.mult))
                settle()
                n = PL if last else DC
                A, B = mod(l, 3 * s + 1), mod(l, 3 * s)
                ins = None
                if last:
                    step(dve.tensor_tensor(tmp_s[:], sq[:, :, PL:DC], A[:, :, 1:MLANES], ALU.mult))
                    settle()
                    dve.tensor_tensor(sq[:, :, PL:DC], tmp_s[:], B[:, :, 1:MLANES], ALU.add)
                for k in range(KD):
                    ins = dve.tensor_scalar(sq[:, k, 0:n], sq[:, k, 0:n], A[:, k, 0:1], B[:, k, 0:1], ALU.mult, ALU.add)
                ins.then_inc(t_ready, 1)
                pres.add()
                dve.wait_ge(hh_ready, pres(hh_more[0]))
                dve.tensor_tensor(h_lo[:, :, cols], sq[:], h_hi[:, :, cols].bitcast(F32), ALU.subtract
                                  ).then_inc(h_ready, 1)

            hh_more = [0]

            def post_norm(l, s, cols, last):
                root(D)
                step(dve.tensor_tensor(o_sb[:], o_sb[:], rs[:].unsqueeze(1).to_broadcast([P, KD, DC]), ALU.mult))
                settle()
                n = PL if last else DC
                G = mod(l, 3 * s + 2)
                if last:
                    step(dve.tensor_tensor(tmp_s[:], o_sb[:, :, PL:DC], G[:, :, 1:MLANES], ALU.mult))
                    settle()
                    dve.tensor_tensor(xT[:, :, TP:T], xT[:, :, TP:T], tmp_s[:], ALU.add)
                    cols = slice((ND - 1) * DC, TP)
                for k in range(KD):
                    ins = dve.scalar_tensor_tensor(xT[:, k, cols], o_sb[:, k, 0:n], G[:, k, 0:1], xT[:, k, cols],
                                                   ALU.mult, ALU.add)
                ins.then_inc(x_done, 1)

            dve.wait_ge(xt_e, 2 * (KT_TOK + 1))
            dve.sem_inc(x_done, ND)
            for d in range(ND):
                sum_squares(sq[:], rs[:])
                pre_norm(0, 0, slice(d * DC, (d + 1) * DC), d == ND - 1)

            def down(parts, nxt, norm, nxt_norm):
                order, ahead = down_steps(parts), len(parts)

                def tiles(m0, m1, nxt_blocks=None):
                    for n, (m, _, s, _, _) in enumerate(order):
                        if m0 <= m < m1:
                            if n + ahead >= len(order) and nxt_blocks is not None:
                                continue
                            _, _, s, k0, k1 = order[(n + ahead) % len(order)]
                            lo_split(s, k1 - k0)
                    if m1 == KD and nxt_blocks is not None:
                        split_next(nxt_blocks)

                def chunk(prev, nxt_blocks=None):
                    tiles(0, 2)
                    if prev is not None:
                        post_norm(*norm, prev, False)
                        if nxt_norm is not None:
                            sum_squares(sq[:], rs[:])
                    tiles(2, 6)
                    if prev is not None and nxt_norm is not None:
                        pre_norm(*nxt_norm, prev, False)
                    tiles(6, 8, nxt_blocks)
                    sum_squares(sq[:], rs[:])

                per_norm = 1 if nxt_norm is None else 2
                chunk(None)
                per = {splits[s]: KD for s in range(len(parts))}
                per.update({stats: per_norm, steps: STEP_POST + (per_norm - 1) * STEP_PRE})
                if nxt_norm is not None:
                    per[pres] = 1
                with loop(dve, ND - 2, per) as i:
                    c = dve.snap(i * DC)
                    chunk(bass.ds(c, DC))
                chunk(slice((ND - 2) * DC, (ND - 1) * DC), nxt)
                cols = slice((ND - 1) * DC, T)
                post_norm(*norm, cols, True)
                if nxt_norm is not None:
                    sum_squares(sq[:], rs[:])
                    pre_norm(*nxt_norm, cols, True)

            STEP_POST, STEP_PRE = 5, 5

            def conv(j, taps_w, kt, prev):
                w = [taps_w[:, bass.ds(j + k * kt, 1)] for k in range(3)]
                step(dve.tensor_copy(tail[:, bass.ds(j, 1), :], a_sb[:, 2 + TP - 2:2 + T].unsqueeze(1)))
                step(dve.tensor_scalar(y_sb[:, 0:TP], a_sb[:, 0:TP], w[0], None, ALU.mult))
                step(dve.tensor_copy(y_sb[:, TP:T].unsqueeze(1), prev[:, bass.ds(j, 1), :]))
                settle()
                step(dve.scalar_tensor_tensor(y_sb[:, 0:TP], a_sb[:, 1:1 + TP], w[1], y_sb[:, 0:TP],
                                              ALU.mult, ALU.add))
                settle()
                dve.scalar_tensor_tensor(y_sb[:], a_sb[:, 2:2 + T], w[2], y_sb[:], ALU.mult, ALU.add
                                         ).then_inc(conv_done, 1)

            def tails_out(kt, t0):
                for g in range(-(-kt // 4)):
                    n = min(4, kt - 4 * g)
                    dve.wait_ge(tail_t_done, t0 + g + 1)
                    dve.tensor_copy(tail_t[:, g * 4 * P:(g * 4 + n) * P], bank(6 + g % 2)[0:TAIL, 0:n * P]
                                    ).then_inc(tail_e, 1)

            conv_n, g_n, set0 = Tally(), Tally(), Tally()

            def gate(parity):
                dve.tensor_tensor(chunked(g_sb[:]), chunked(y_sb[:]), upset(parity), ALU.mult).then_inc(g_ready, 1)
                gs.add()
                dve.wait_ge(g_ready, gs())
                dve.sem_inc(set_free[parity], 1)
                wait(dve, g_out, g_n())
                g_n.add(16)
                dve.wait_ge(gh_ready, gs())
                dve.tensor_tensor(g_parts[:, 1, :], g_sb[:], g_parts[:, 0, :].bitcast(F32), ALU.subtract
                                  ).then_inc(gl_ready, 1)

            split_next([(0, KD), (1, KD), (2, KD)])
            step(dve.memset(a_sb[:, 0:2], 0.0))
            settle()
            f0, f1 = Tally(), Tally()

            def mixer(j, parity, own):
                if own:
                    lo_split(0, KD)
                f = (f0, f1)
                f[parity].add()
                dve.wait_ge(set_free[parity], f[parity]())
                if own:
                    lo_split(1, KD)
                else:
                    dve.wait_ge(w_done[1], splits[1]())
                f[1 - parity].add()
                step(dve.tensor_tensor(chunked(a_sb[:, 2:2 + T]), chunked(a_sb[:, 2:2 + T]), upset(1 - parity),
                                       ALU.mult))
                settle()
                dve.sem_inc(set_free[1 - parity], 1)
                conv(j, v_scw, KD, prev_mix[:])
                conv_n.add()
                dve.wait_ge(conv_done, conv_n())
                if own:
                    lo_split(2, KD)
                else:
                    dve.wait_ge(w_done[2], splits[2]())
                f[parity].add()
                gate(parity)

            gs = Tally()
            mixer(0, 0, True)
            mixer(1, 1, True)
            with loop(dve, KD // 2 - 2, {splits[0]: 2, splits[1]: 2, splits[2]: 2, f0: 3, f1: 3, conv_n: 2,
                                         g_n: 32, gs: 2, steps: 10}) as i:
                j = dve.snap(i * 2)
                mixer(j + 2, 0, True)
                mixer(j + 3, 1, True)
            mixer(KD - 2, 0, True)
            mixer(KD - 1, 1, False)
            P8, P22 = first_blocks(PARTS8), first_blocks(PARTS22)
            settle()
            dve.sem_inc(tail_ready, 1)
            tails_out(KD, 0)
            split_next(P8)
            down(PARTS8, [(0, KD), (1, KD)], (0, 0), (0, 1))

            def ffn(l, nxt, t0):
                step(dve.memset(a_sb[:, 0:2], 0.0))
                settle()

                def body(j, own):
                    lo_split(0, KD) if own else dve.wait_ge(w_done[0], splits[0]())
                    f0.add()
                    dve.wait_ge(set_free[0], f0())
                    conv(j, vec[:, 2 + l, :], KF, prev_ffn[:, l])
                    lo_split(1, KD) if own else dve.wait_ge(w_done[1], splits[1]())
                    silus.add()
                    dve.wait_ge(act_done, silus())
                    f1.add()
                    gate(1)

                with loop(dve, KF - 1, {splits[0]: 1, splits[1]: 1, f0: 1, f1: 1, silus: 1, g_n: 16, gs: 1,
                                        steps: 4}) as i:
                    body(i, True)
                body(KF - 1, False)
                settle()
                dve.sem_inc(tail_ready, 1)
                tails_out(KF, t0)
                split_next(nxt)

            silus = Tally()
            ffn(0, P22, 2)
            down(PARTS22, [(0, KD), (1, KD), (2, KD)], (0, 1), (1, 0))

            lo_split(0, KD)
            lo_split(1, KD)
            lo_split(2, KD)
            dve.wait_ge(w_done[2], splits[2]())

            def rope(u, dst, ready):
                step(dve.tensor_tensor(chunked(rope1[:]), upset(u)[0:DR], chunked(tab[0:DR, :]), ALU.mult))
                step(dve.tensor_tensor(chunked(dst[:]), upset(u)[DR:P], chunked(tab[DR:P, :]), ALU.mult))
                settle()
                dve.sem_inc(set_free[u], 1)
                dve.tensor_tensor(dst[:], dst[:], rope1[:], ALU.add).then_inc(ready, 1)

            dve.wait_ge(tab_in, 16)

            def root_all(n):
                dve.wait_ge(stat_ready, stats(1))
                stats.add()
                dve.tensor_scalar(chunked(varm[:]), upset(0), 1.0 / n, EPS, ALU.mult, ALU.add).then_inc(var_ready, 1)
                dve.wait_ge(root_ready, stats())
                newton(rsm[:], varm[:], rootm[:])

            sum_squares(sqm[:], rsm[:])
            root_all(QR)
            step(dve.tensor_tensor(q_raw[:], q_raw[:], rsm[:].unsqueeze(1).to_broadcast([P, KQ, T]), ALU.mult))
            settle()
            for k in range(KQ):
                ins = dve.tensor_scalar(q_raw[:, k, :], q_raw[:, k, :], v_qan[:, k:k + 1], None, ALU.mult)
            ins.then_inc(qn_t, 1)
            sum_squares(sqm[:, 0:KC, :], rsm[:])
            dve.wait_ge(hh_ready, pres(1))
            hh_more[0] = 1
            dve.tensor_tensor(qn_lo[:], q_raw[:], qn_hi[:].bitcast(F32), ALU.subtract).then_inc(qn_r, 1)
            root_all(KR)
            step(dve.tensor_tensor(l_raw[:], l_raw[:], rsm[:].unsqueeze(1).to_broadcast([P, KC, T]), ALU.mult))
            settle()
            for k in range(KC):
                ins = dve.tensor_scalar(latn[:, k, :], l_raw[:, k, :], v_kvn[:, k:k + 1], None, ALU.mult)
            ins.then_inc(lat_r, 1)
            rope(1, kpe, kpe_r)
            lo_split(0, KQ)
            lo_split(1, KQ)
            dve.wait_ge(kpe_r, 1)
            dve.wait_ge(lat_r, 1)
            dve.wait_ge(qn_r, 1)
            step(dve.tensor_copy(lats[:], latn[:, :, TP:T]))
            step(dve.tensor_copy(kpes[:], kpe[:, TP:T]))
            for t in range(KT_TOK + 1):
                n = P if t < KT_TOK else NS
                dve.wait_ge(tok_t, t + 1)
                if t >= 2:
                    dve.wait_ge(tok_out[t % 2], 32 * (t // 2))
                dve.tensor_copy(tok[t % 2][0:n, :], bank(6 + t % 2)[0:n, 0:KR + DR]).then_inc(tok_e, 1)
            h2, h4, h8 = Tally(), Tally(), Tally()

            def head(h, more):
                if more:
                    lo_split(0, KQ)
                    lo_split(1, KQ)
                else:
                    dve.wait_ge(w_done[1], splits[1]())
                step(dve.tensor_tensor(chunked(rope1[:]), upset(1)[0:DR], chunked(tab[0:DR, :]), ALU.mult))
                step(dve.tensor_tensor(chunked(qpe[:]), upset(1)[DR:P], chunked(tab[DR:P, :]), ALU.mult))
                settle()
                step(dve.tensor_tensor(qpe[:], qpe[:], rope1[:], ALU.add))
                settle()
                dve.sem_inc(qpe_r, 1)
                step(dve.tensor_copy(qpes[:, :, bass.ds(h, 1)], qpe[:, TP:T].unsqueeze(2)))
                dve.wait_ge(kv_mm, h4(4))
                h4.add(4)
                dve.tensor_copy(qlat[:, :, :, bass.ds(h, 1)], bank(5)[:, 0:KC * NS].rearrange(
                    "p (c b o) -> p c b o", c=KC, o=1)).then_inc(qlat_r, 1)

                def top(q):
                    u = q % 2
                    dve.wait_ge(s_mm, h8(q + 1))
                    step(dve.tensor_reduce(st[:, u, 0:1], ps[:, 2 * u:2 * u + 2, :].rearrange("p b n -> p (b n)")
                                           [:, 0:(q + 1) * P], AX.X, ALU.max))
                    settle()
                    dve.tensor_scalar(st[:, 2 + u, 0:1], st[:, u, 0:1], -SCALE, None, ALU.mult).then_inc(nm_ready, 1)

                def norm(q):
                    u = q % 2
                    dve.wait_ge(e_ready, h8(q + 1))
                    step(dve.reciprocal(st[:, 6 + u, 0:1], st[:, 4 + u, 0:1]))
                    settle()
                    dve.tensor_scalar(p_sb[u][:, 0:(q + 1) * P], p_sb[u][:, 0:(q + 1) * P], st[:, 6 + u, 0:1], None,
                                      ALU.mult).then_inc(p_ready, 1)

                def low_out(half):
                    dve.wait_ge(pv_h, h2(half + 1))
                    dve.tensor_tensor(oh[half][:, 1, :], bank(6 + half), oh[half][:, 0, :].bitcast(F32), ALU.subtract
                                      ).then_inc(pv_e, 1)

                top(0)
                for q in range(1, KT_TOK):
                    top(q)
                    norm(q - 1)
                    if q == 6:
                        low_out(0)
                norm(KT_TOK - 1)
                low_out(1)
                h8.add(8)
                h2.add(2)

            with loop(dve, H - 1, {splits[0]: 1, splits[1]: 1, h2: 2, h4: 4, h8: 8, steps: 20}) as h:
                head(h, True)
            head(H - 1, False)
            settle()
            dve.wait_ge(sn_mm, 1)
            dve.wait_ge(qlat_r, H)
            dve.tensor_copy(sx[:], bank(0)[0:NS, 0:NS * H]).then_inc(sn_e, 1)
            for u in range(2):
                dve.memset(s_sb[u][:, NPG, :], NEG).then_inc(neg_ready, 1)

            groups, seqs, olats, dpvs = Tally(), Tally(), Tally(), Tally(2)

            def decode_seq(b, u):
                for g in range(8):
                    dve.wait_ge(kt_mm, groups(1))
                    wait(dve, sc_mm, groups(-1))
                    dve.tensor_copy(kT[g % 2][:, 1, :], bank(3 * (g % 2) + 1)).then_inc(kt_ed, 1)
                    groups.add()
                dve.wait_ge(sc_mm, groups())
                dve.tensor_copy(s_sb[u][:, 0:NPG, :], bank(6)[:, 0:NPG * H].rearrange("p (n h) -> p n h", h=H)
                                ).then_inc(ch_dve, 1)
                dve.wait_ge(ch_dve, seqs(1))
                dve.wait_ge(vn_in[u], vns[u](32))
                vns[u].add(32)
                dve.tensor_reduce(dm[:, 0:H], s_sb[u][:].rearrange("p n h -> p h n"), AX.X, ALU.max
                                  ).then_inc(ch_dve, 1)
                dve.wait_ge(ch_pe, seqs3(1))
                step(dve.tensor_reduce(dm[0:H, 8:9], bank(7)[0:H, 0:P], AX.X, ALU.max))
                settle()
                dve.tensor_scalar(dm[0:H, 16:16 + H], ident[0:H, 0:H], dm[0:H, 8:9], None, ALU.mult
                                  ).then_inc(ch_dve, 1)
                dve.wait_ge(ch_pe, seqs3(2))
                dve.tensor_tensor(e_sb[u][:], s_sb[u][:], bank(7)[:, P:P + H].unsqueeze(1).to_broadcast(
                    [P, NPG + 1, H]), ALU.subtract).then_inc(ch_dve, 1)
                dve.wait_ge(ch_act, acts_n(1))
                acts_n.add()
                dve.tensor_reduce(dm[:, 24:24 + H], e_sb[u][:].rearrange("p n h -> p h n"), AX.X, ALU.add
                                  ).then_inc(ch_dve, 1)
                dve.wait_ge(ch_pe, seqs3(3))
                dve.reciprocal(dm[:, 32:32 + H], bank(7)[:, P + H:P + 2 * H]).then_inc(ch_dve, 1)
                seqs.add(6)
                seqs3.add(3)
                dve.wait_ge(ch_dve, seqs())
                dve.wait_ge(dpv, dpvs(1))
                dpvs.add()
                dve.tensor_tensor(olat[:, :, :, bass.ds(b, 1)],
                                  bank(7)[:, 256:256 + KC * H].rearrange("p (c h o) -> p c h o", c=KC, o=1),
                                  dm[:, 32:32 + H].unsqueeze(1).unsqueeze(3).to_broadcast([P, KC, H, 1]),
                                  ALU.mult).then_inc(olat_r, 1)

            vns, acts_n, seqs3 = [Tally(), Tally()], Tally(), Tally()
            decode_seq(0, 0)
            decode_seq(1, 1)
            with loop(dve, NS // 2 - 1, {groups: 16, seqs: 12, seqs3: 6, dpvs: 2, acts_n: 2, steps: 2,
                                         vns[0]: 32, vns[1]: 32}) as i:
                b = dve.snap(i * 2)
                decode_seq(b + 2, 0)
                decode_seq(b + 3, 1)
            dve.wait_ge(ov_h, 1)
            dve.tensor_tensor(ovs[:, 1], bank(0)[:, 0:H * NS].rearrange("p (h b) -> p h b", h=H),
                              ovs[:, 0].bitcast(F32), ALU.subtract).then_inc(ov_e, 1)
            split_next(P8)
            down(PARTS8, [(0, KD), (1, KD)], (1, 0), (1, 1))
            f0.add(KQ + H)
            f1.add(KQ)
            ffn(1, P22, 8)
            down(PARTS22, [], (1, 1), None)

        @block.tensor
        def _(pe):
            uses = [Tally() for _ in range(3)]
            f = [Tally(), Tally()]
            stats, acts = Tally(), [Tally() for _ in range(3)]

            def trans(out, in_):
                r = in_.shape[0]
                return pe.transpose(out, in_, ident[0:r, 0:r])

            pe.sem_inc(mod_mm, 2)
            pe.sem_inc(dpv, 2)
            pe.wait_ge(const_ready, 5)
            pe.wait_ge(vec_in, 16 * 11)
            for t, r in enumerate((125, 108, 66, 66)):
                ins = trans(bank(0)[:, t * P:t * P + r], packs[0:r, t, :])
            ins.then_inc(setup_t, 1)
            pe.wait_ge(csil_ready, 1)
            for k in range(KD):
                ins = trans(bank(1)[:, k * MLANES:(k + 1) * MLANES], csil[:, k * P:(k + 1) * P])
            ins.then_inc(setup_t, 1)
            pe.wait_ge(mix_loaded, 16)
            for k in range(KD):
                ins = trans(bank(2)[:, k * 2 * NS:(k + 1) * 2 * NS], mix_in[:, k * P:(k + 1) * P])
            ins.then_inc(setup_t, 1)
            pe.wait_ge(ffn_loaded, 16)
            for l in range(2):
                for k in range(KF):
                    ins = trans(bank(3 + l)[:, k * 2 * NS:(k + 1) * 2 * NS], ffn_in[:, l, k * P:(k + 1) * P])
                ins.then_inc(setup_t, 1)
            pe.wait_ge(x_loaded, 16)
            pe.wait_ge(xs_loaded, 16)
            for n in range(2 * (KT_TOK + 1)):
                t, half = n // 2, n % 2
                wait(pe, xt_e, n - 2)
                for k in range(4):
                    c = (4 * half + k) * P
                    src = x_in[:, t, c:c + P] if t < KT_TOK else xs_in[:, c:c + P]
                    w = P if t < KT_TOK else NS
                    ins = trans(bank(5 + n % 3)[:, k * P:k * P + w], src)
                ins.then_inc(xt_t, 1)
            pe.wait_ge(setup_e, 2)
            mods = [Tally(), Tally()]
            md = Tally(-1)

            def mod_pair():
                for b in range(2):
                    mods[b].add(16)
                    pe.wait_ge(mod_loaded[b], mods[b]())
                    wait(pe, mod_done, md())
                    md.add()
                    for m in range(4):
                        for k in range(KD):
                            ins = pe.matmul(bank(b)[:, m * MLANES:(m + 1) * MLANES],
                                            mod_raw[b][:, k, m * P:(m + 1) * P], csT[:, k, :],
                                            start=k == 0, stop=k == KD - 1)
                    ins.then_inc(mod_mm, 1)

            mod_pair()
            with loop(pe, 2 * MODS - 1, {mods[0]: 16, mods[1]: 16, md: 2}):
                mod_pair()

            def stat(src, out):
                pe.wait_ge(ss_ready, stats(1))
                stats.add()
                for o, r in zip(out, src):
                    ins = pe.matmul(o, ones[:], r, start=True, stop=True)
                ins.then_inc(stat_ready, 1)

            def stat_chunk():
                stat([rs[:]], [bank(6)[:, 0:DC]])

            for d in range(ND):
                stat_chunk()

            def product(slot, ks, rhs, outs_, first=True, last=True):
                pe.wait_ge(w_ready[slot], uses[slot](1))
                uses[slot].add()
                for o, (hi, lo) in zip(outs_, rhs):
                    for n, k in enumerate(ks):
                        f_, l_ = first and n == 0, last and n == len(ks) - 1
                        pe.matmul(o, w_hi[slot][:, n, :], hi(k), start=f_, stop=False)
                        pe.matmul(o, w_hi[slot][:, n, :], lo(k), start=False, stop=False)
                        ins = pe.matmul(o, w_lo[slot][:, n, :], hi(k), start=False, stop=l_)
                ins.then_inc(w_done[slot], 1)

            def wide(hi, lo):
                return [(lambda k, c=c: hi[:, k, c * UC:(c + 1) * UC], lambda k, c=c: lo[:, k, c * UC:(c + 1) * UC])
                        for c in range(NU)]

            def up_product(slot, s, kt=KD, hi=None, lo=None):
                wait(pe, set_free[s], f[s]())
                f[s].add()
                product(slot, range(kt), wide(hi or h_hi, lo or h_lo), [upset(s)[:, c, :] for c in range(NU)])

            def down(parts, norm_next, tail_tiles=0):
                def pair(m, start):
                    for u in range(2):
                        wait(pe, act_step, evs(1 + u - DOWN_AGO[m + u]))
                    evs.add(2)
                    if m == 6 and tail_tiles:
                        pe.wait_ge(tail_e, tail_tiles)
                    for m_, n, s, k0, k1 in down_steps(parts):
                        if m_ // 2 == m // 2:
                            if start and m_ == m:
                                acts[n].add(32)
                                pe.wait_ge(act_in[n], acts[n]())
                            product(s, range(k0, k1), [(lambda k: act_hi[:, k, :], lambda k: act_lo[:, k, :])],
                                    [bank(DOWN_BANK[m_])[:, 0:DC]], n == 0, n == len(parts) - 1)

                def chunk(prev):
                    pair(0, True)
                    if prev:
                        stat_chunk()
                    pair(2, False)
                    if prev and norm_next:
                        stat_chunk()
                    pair(4, False)
                    pair(6, False)

                chunk(False)
                per = {uses[s]: KD for s in range(len(parts))}
                per.update({acts[n]: 32 for n in range(len(parts))})
                per.update({evs: KD, stats: 2 if norm_next else 1})
                with loop(pe, ND - 1, per):
                    chunk(True)
                stat_chunk()
                if norm_next:
                    stat_chunk()

            evs = Tally()

            def tails(kt, n):
                pe.wait_ge(tail_ready, n)
                for g in range(-(-kt // 4)):
                    if g >= 2:
                        pe.wait_ge(tail_e, te[0] + g - 1)
                    for k in range(4 * g, min(kt, 4 * g + 4)):
                        ins = trans(bank(6 + g % 2)[0:TAIL, (k % 4) * P:(k % 4 + 1) * P], tail[:, k, :])
                    ins.then_inc(tail_t_done, 1)
                te[0] += -(-kt // 4)

            te = [0]

            pe.wait_ge(h_ready, ND)

            def triple(par):
                up_product(0, par)
                up_product(1, 1 - par)
                up_product(2, par)

            triple(0)
            triple(1)
            with loop(pe, KD // 2 - 1, {uses[0]: 2, uses[1]: 2, uses[2]: 2, f[0]: 3, f[1]: 3}):
                triple(0)
                triple(1)
            tails(KD, 1)
            down(PARTS8, True, te[0])

            def ffn(n):
                pe.wait_ge(h_ready, n)
                with loop(pe, KF, {uses[0]: 1, uses[1]: 1, f[0]: 1, f[1]: 1}):
                    up_product(0, 0)
                    up_product(1, 1)

            ffn(2 * ND)
            tails(KF, 2)
            down(PARTS22, True, te[0])
            pe.wait_ge(h_ready, 3 * ND)
            for m in range(KQ + KC + 1):
                up_product(m % 3, m % 2)
            pe.wait_ge(set_free[0], f[0]())
            for _ in range(2):
                stat([rsm[:, c * UC:(c + 1) * UC] for c in range(NU)], [upset(0)[:, c, :] for c in range(NU)])
            pe.wait_ge(lat_r, 1)
            pe.wait_ge(kpe_r, 1)
            for t in range(KT_TOK + 1):
                n = P if t < KT_TOK else NS
                wait(pe, tok_e, t - 1)
                for c in range(KC):
                    trans(bank(6 + t % 2)[0:n, c * P:(c + 1) * P], latn[:, c, t * P:t * P + n])
                trans(bank(6 + t % 2)[0:n, KR:KR + DR], kpe[:, t * P:t * P + n]).then_inc(tok_t, 1)

            pe.wait_ge(tok_e, KT_TOK + 1)
            pe.wait_ge(qn_r, 1)
            hq, h1, h2, h3, h8 = Tally(), Tally(), Tally(), Tally(), Tally()

            def head(first):
                if not first:
                    pe.wait_ge(e_ready, h8())
                    pe.wait_ge(p_t_e, h8())
                product(0, range(KQ), wide(qn_hi, qn_lo), [upset(0)[:, c, :] for c in range(NU)])
                product(1, range(KQ), wide(qn_hi, qn_lo), [upset(1)[:, c, :] for c in range(NU)])
                hq.add(16)
                pe.wait_ge(kvb_in, hq())
                if not first:
                    pe.wait_ge(pv_e, h2())
                for c in range(2):
                    for k in range(KC):
                        ins = pe.matmul(bank(6 + c), kvb[:, k, 0:DN], latn[:, k, c * 512:(c + 1) * 512],
                                        start=k == 0, stop=k == KC - 1)
                ins.then_inc(kv_mm, 1)
                fq.add()
                pe.wait_ge(set_free[0], fq())
                for t in range(KT_TOK):
                    for k in range(KC):
                        ins = pe.matmul(bank(t // 4)[:, (t % 4) * P:(t % 4 + 1) * P], latn[:, k, t * P:(t + 1) * P],
                                        kvb[:, k, DN:DN + DV], start=k == 0, stop=k == KC - 1)
                ins.then_inc(kv_mm, 1)
                for k in range(KC):
                    ins = trans(bank(2)[:, k * P:(k + 1) * P], kvb[:, k, 0:DN])
                ins.then_inc(kv_mm, 1)
                h1.add()
                pe.wait_ge(qpe_r, h1())
                pe.wait_ge(kv_e, h3(3))
                for k in range(KC):
                    ins = pe.matmul(bank(5)[:, k * NS:(k + 1) * NS], wkT[:, k, :], qno[:, TP:T], start=True, stop=True)
                ins.then_inc(kv_mm, 1)
                h3.add(3)

                def scores(q):
                    u = q % 2
                    if q >= 2:
                        pe.wait_ge(e_ready, h8(q - 1))
                    for b in range(q // 4 + 1):
                        n = min(512, (q + 1) * P - b * 512)
                        keys = slice(b * 512, b * 512 + n)
                        diag = b == q // 4
                        pe.matmul(bank(2 * u + b)[:, 0:n], qno[:, q * P:(q + 1) * P], kno[:, keys],
                                  start=True, stop=False)
                        if diag:
                            pe.matmul(bank(2 * u + b)[:, n - P:n], ident_b[:], mask_b[:], start=False, stop=False,
                                      skip_group_check=True)
                        ins = pe.matmul(bank(2 * u + b)[:, 0:n], qpe[:, q * P:(q + 1) * P], kpe[:, keys],
                                        start=False, stop=True)
                    ins.then_inc(s_mm, 1)

                def turn(q):
                    pe.wait_ge(p_ready, h8(q + 1))
                    if q == 0:
                        pe.wait_ge(qlat_r, h1())
                    else:
                        pe.wait_ge(p_t_e, h8(q))
                    for k in range(q + 1):
                        ins = trans(bank(4 + k // 4)[:, (k % 4) * P:(k % 4 + 1) * P], p_sb[q % 2][:, k * P:(k + 1) * P])
                    ins.then_inc(p_t_mm, 1)

                def values(half):
                    pe.wait_ge(p_t_e, h8(4 * half + 4))
                    n = 4 * half + 4
                    for k in range(n):
                        c = max(0, k - 4 * half) * P
                        ins = pe.matmul(bank(6 + half)[:, c:512], v_sb[:, k, :], p_t[:, k, c:512], start=k == 0,
                                        stop=k >= 4 * half, skip_group_check=True)
                    ins.then_inc(pv_mm, 1)

                scores(0)
                for q in range(1, KT_TOK):
                    scores(q)
                    turn(q - 1)
                    if q == 4:
                        values(0)
                turn(KT_TOK - 1)
                values(1)
                h8.add(8)
                h2.add(2)

            fq = Tally(SETS + 3)
            head(True)
            with loop(pe, H - 1, {uses[0]: 1, uses[1]: 1, hq: 16, h1: 1, h2: 2, h3: 3, h8: 8, fq: 1}):
                head(False)
            pe.wait_ge(qlat_r, H)
            for k in range(KC):
                pe.matmul(bank(0)[0:NS, 0:NS * H], lats[:, k, :], qlat[:, k].rearrange("p b h -> p (b h)"),
                          start=k == 0, stop=False)
            pe.matmul(bank(0)[0:NS, 0:NS * H], kpes[:], qpes[:].rearrange("p b h -> p (b h)"),
                      start=False, stop=True).then_inc(sn_mm, 1)

            pe.wait_ge(sn_e, 1)
            pe.wait_ge(pv_e, 2 * H)
            groups, seqs, seqs6, acts_n, pgs, vns = Tally(), Tally(), Tally(), Tally(), [Tally(), Tally()], [Tally(), Tally()]

            def decode_seq(b, u):
                pgs[u].add(2 * 16 * NPG)
                pe.wait_ge(pg_in[u], pgs[u]())
                wait(pe, ch_dve, seqs6(-5))

                def scores(g):
                    pe.wait_ge(kt_ea, groups())
                    pe.wait_ge(kt_ed, groups())
                    for n in range(4):
                        out = bank(6)[:, (4 * g + n) * H:(4 * g + n + 1) * H]
                        for k in range(KC):
                            pe.matmul(out, kT[g % 2][:, k, n * P:(n + 1) * P], qlat[:, k, bass.ds(b, 1), :].rearrange(
                                "p b h -> p (b h)"), start=k == 0, stop=False)
                        ins = pe.matmul(out, kT[g % 2][0:DR, 2, n * P:(n + 1) * P],
                                        qpes[:, bass.ds(b, 1), :].rearrange("p b h -> p (b h)"), start=False, stop=True)
                    ins.then_inc(sc_mm, 1)

                for g in range(8):
                    wait(pe, kt_ea, groups(-1))
                    wait(pe, kt_ed, groups(-1))
                    b0 = 3 * (g % 2)
                    for n in range(4):
                        for k in range(KC):
                            trans(bank(b0 + k)[:, n * P:(n + 1) * P], pg[u][:, 4 * g + n, k * P:(k + 1) * P])
                        ins = trans(bank(b0 + 2)[0:DR, n * P:(n + 1) * P], pgr[u][:, 4 * g + n, :])
                    ins.then_inc(kt_mm, 1)
                    if g:
                        scores(g - 1)
                    groups.add()
                scores(7)
                pe.wait_ge(ch_dve, seqs6(2))
                wait(pe, olat_r, seqs())
                seqs.add()
                trans(bank(7)[0:H, 0:P], dm[:, 0:H]).then_inc(ch_pe, 1)
                pe.wait_ge(ch_dve, seqs6(3))
                pe.matmul(bank(7)[:, P:P + H], ones[0:H, :], dm[0:H, 16:16 + H], start=True, stop=True
                          ).then_inc(ch_pe, 1)
                pe.wait_ge(ch_dve, seqs6(5))
                pe.matmul(bank(7)[:, P + H:P + 2 * H], ones[:], dm[:, 24:24 + H], start=True, stop=True
                          ).then_inc(ch_pe, 1)
                pe.wait_ge(ch_dve, seqs6(6))
                seqs6.add(6)
                for k in range(KC):
                    out = bank(7)[:, 256 + k * H:256 + (k + 1) * H]
                    for n in range(NPG):
                        pe.matmul(out, pg[u][:, n, k * P:(k + 1) * P], e_sb[u][:, n, :], start=n == 0, stop=False)
                    ins = pe.matmul(out, vnew[u][:, k * P:(k + 1) * P], e_sb[u][0:1, NPG, :], start=False, stop=True)
                ins.then_inc(dpv, 1)

            decode_seq(0, 0)
            decode_seq(1, 1)
            with loop(pe, NS // 2 - 1, {groups: 16, seqs: 2, seqs6: 12, pgs[0]: 1024, pgs[1]: 1024}) as i:
                b = pe.snap(i * 2)
                decode_seq(b + 2, 0)
                decode_seq(b + 3, 1)
            pe.wait_ge(wv_in, 32)
            pe.wait_ge(olat_r, NS)
            for h in range(H):
                for k in range(KC):
                    ins = pe.matmul(bank(0)[:, h * NS:(h + 1) * NS], wv[:, k, h, :], olat[:, k, h, :],
                                    start=k == 0, stop=k == KC - 1)
            ins.then_inc(ov_mm, 1)
            down(PARTS8, True)
            f[0].add(H)
            ffn(4 * ND)
            tails(KF, 3)
            down(PARTS22, False, te[0])
            pe.wait_ge(x_done, 5 * ND)
            for n in range(2 * (KT_TOK + 1)):
                t, half = n // 2, n % 2
                wait(pe, yt_e, n - 3)
                w = P if t < KT_TOK else NS
                for k in range(4):
                    ins = trans(bank(n % 4)[0:w, k * P:(k + 1) * P], xT[:, 4 * half + k, t * P:t * P + w])
                ins.then_inc(yt_mm, 1)


_INS = ["x_prompt", "x_sample", "cache_kv_latent", "cache_k_rope", "state_mixconv", "state_ffnconv", "page_table",
        "c_prompt", "c_sample", "mod_w", "mod_b", "norm_mix_pre", "norm_mix_post", "norm_ffn_pre", "norm_ffn_post",
        "sc_w_in", "sc_conv_w", "sc_w_out", "mla_w_qa", "mla_qa_norm", "mla_w_qb", "mla_w_kva", "mla_kv_norm",
        "mla_w_kvb", "mla_w_o", "ffn_w_in", "ffn_conv_w", "ffn_conv_b", "ffn_w_out"]
_FLAT = {"x_prompt", "cache_kv_latent", "cache_k_rope", "state_mixconv", "sc_w_in", "sc_conv_w", "sc_w_out",
         "mla_w_qa", "mla_w_qb", "mla_w_kva", "mla_w_kvb", "mla_w_o"}
_OUTS = [("y_prompt", (TP, D)), ("y_sample", (NS, D)), ("lat_p", (TP, KR)), ("pe_p", (TP, DR)), ("lat_s", (NS, KR)),
         ("pe_s", (NS, DR)), ("mix_p", (2, D)), ("mix_s", (NS, 2, D)), ("ffn_p", (2, 2, F)), ("ffn_s", (2, NS, 2, F))]
_SHAPES = [(1, TP, D), (NS, 1, D), (1, 1, TP, KR), (1, 1, TP, DR), (1, NS, 1, KR), (1, NS, 1, DR), (1, 1, 2, D),
           (1, NS, 2, D), (2, 1, 2, F), (2, NS, 2, F)]


def rope_table():
    half = DR // 2
    inv = (10000.0 ** (-np.arange(half) * 2.0 / DR)).astype(np.float32)
    pos = np.concatenate([np.arange(TP), np.full(NS, PAST)]).astype(np.float32)
    ang = (inv[:, None] * pos[None, :]).astype(np.float32)
    cos, sin = np.cos(ang), np.sin(ang)
    return np.ascontiguousarray(np.concatenate([cos, cos, -sin, sin]).astype(np.float32))


def kernel(**inputs):
    import concourse.bacc as bacc
    from concourse.bass_utils import run_bass_kernel_spmd

    nc = bacc.Bacc("TRN2", target_bir_lowering=False, num_devices=1)
    arrays, ins, outs = {}, [], []
    for name in _INS:
        a = np.ascontiguousarray(inputs[name])
        if name in _FLAT:
            a = a[0]
        elif name == "x_sample":
            a = a[:, 0]
        arrays[f"in_{name}"] = a
        ins.append(nc.dram_tensor(f"in_{name}", a.shape, mybir.dt.from_np(a.dtype), kind="ExternalInput").ap())
    arrays["in_rope"] = rope_table()
    ins.append(nc.dram_tensor("in_rope", (P, T), F32, kind="ExternalInput").ap())
    for name, shape in _OUTS:
        outs.append(nc.dram_tensor(f"out_{name}", shape, F32, kind="ExternalOutput").ap())
    build(nc, ins, outs)
    r = run_bass_kernel_spmd(nc, [arrays], core_ids=[0])
    return tuple(r.results[0][f"out_{name}"].reshape(s) for (name, _), s in zip(_OUTS, _SHAPES))
```

```python
from contextlib import ExitStack, contextmanager

import numpy as np

import concourse.bass as bass
from concourse import mybir

F32 = mybir.dt.float32
F32R = mybir.dt.float32r
BF16 = mybir.dt.bfloat16
I32 = mybir.dt.int32
ALU = mybir.AluOpType
ACT = mybir.ActivationFunctionType
AX = mybir.AxisListType

P = 128
D = 1024
KD = D // P
TP = 1024
NS = 8
T = TP + NS
KT_TOK = TP // P
F = 2816
KF = F // P
UC, NU = T // 3, 3
DC, ND = T // 4, 4
PL = TP - (ND - 1) * DC
H = 8
DN, DR, DV = 128, 64, 128
QR, KR = 384, 256
KQ, KC = QR // P, KR // P
PAGE = 128
NPG = 32
PAST = PAGE * NPG
EPS = 1e-6
SCALE = float(DN + DR) ** -0.5
NEG = -1e30
TAIL = 2 + NS
MODS = 6
MLANES = 1 + NS
MB = 512


class Tally:

    def __init__(self, n=0):
        self.n, self.loops = n, []

    def __call__(self, more=0):
        value = self.n + more
        for i, per in self.loops:
            value = i * per + value
        return value

    def add(self, k=1):
        self.n += k


def wait(eng, sem, value):
    if isinstance(value, int) and value <= 0:
        return
    eng.wait_ge(sem, value)


@contextmanager
def loop(eng, trips, per):
    entry = {t: t.n for t in per}
    with eng.Fori(0, trips) as i:
        for t, k in per.items():
            t.loops.append((i, k))
        yield i
    for t, k in per.items():
        assert t.n - entry[t] == k, (t.n - entry[t], k)
        t.n += (trips - 1) * k
        t.loops.pop()


def build(nc, ins, outs):
    (x_prompt, x_sample, cache_lat, cache_pe, state_mix, state_ffn, page_table, c_prompt, c_sample, mod_w, mod_b,
     n_mix_pre, n_mix_post, n_ffn_pre, n_ffn_post, sc_w_in, sc_conv_w, sc_w_out, w_qa, qa_norm, w_qb, w_kva,
     kv_norm, w_kvb, w_o, ffn_w_in, ffn_conv_w, ffn_conv_b, ffn_w_out, rope_tab) = ins
    (y_prompt, y_sample, lat_p, pe_p, lat_s, pe_s, mix_p, mix_s, ffn_p, ffn_s) = outs

    mid_d = nc.dram_tensor("mid_d", (2, F, T), F32).ap()

    base = (nc.sbuf_base + 63) // 64 * 64
    room = [base]

    def arena(size):
        at = room[0]
        room[0] += (size + 31) // 32 * 32
        return at

    names = set()

    def at(name, shape, off, dt=F32):
        assert name not in names
        names.add(name)
        return nc.alloc_sbuf_tensor_at(name, shape, dt, offset=off, align_bytes=8)

    T4, D4 = T * 4, DC * 4
    A_X = arena(KD * T4)
    A_H = arena(2 * KD * T4)
    A_W = arena(9 * KD * P * 4)
    A_A = arena(2 * KF * D4)
    A_O = arena(2 * KD * D4)
    A_C = arena(12 * 1024)
    assert room[0] <= nc.sbuf_usable_end, (room[0], nc.sbuf_usable_end)

    xT = at("xT", [P, KD, T], A_X)
    h_hi = at("h_hi", [P, KD, T], A_H, F32R)
    h_lo = at("h_lo", [P, KD, T], A_H + KD * T4, F32R)
    WB = KD * P * 4
    w_raw = [at(f"w_raw{s}", [P, KD, P], A_W + s * WB) for s in range(3)]
    w_hi = [at(f"w_hi{s}", [P, KD, P], A_W + (3 + s) * WB, F32R) for s in range(3)]
    w_lo = [at(f"w_lo{s}", [P, KD, P], A_W + (6 + s) * WB, F32R) for s in range(3)]
    act_hi = at("act_hi", [P, KF, DC], A_A, F32R)
    act_lo = at("act_lo", [P, KF, DC], A_A + KF * D4, F32R)
    o_sb = at("o_sb", [P, KD, DC], A_O)
    sq = at("sq", [P, KD, DC], A_O + KD * D4)
    c0 = [A_C]

    def small(name, shape, dt=F32):
        n = int(np.prod(shape[1:])) * (2 if dt == BF16 else 4)
        off = c0[0]
        c0[0] += (n + 31) // 32 * 32
        assert c0[0] <= A_C + 12 * 1024, name
        return at(name, shape, off, dt)

    modv = small("modv", [P, 2 * MODS * KD, MLANES])
    vec = small("vec", [P, 4, P])
    ident = small("ident", [P, P])
    ones = small("ones", [P, P])
    ident_b = small("ident_b", [P, P], BF16)
    mask_b = small("mask_b", [P, P], BF16)
    prev_mix = small("prev_mix", [P, KD, NS])
    prev_ffn = small("prev_ffn", [P, 2, KF, NS])
    rs = small("rs", [P, DC])
    var, root_b = small("var", [P, DC]), small("root_b", [P, DC])
    tmp_s = small("tmp_s", [P, KD, NS])
    VA, VB = vec[:, 0, :], vec[:, 1, :]
    v_modb, v_scw, v_qan, v_kvn = VA[:, 0:96], VA[:, 96:120], VA[:, 120:123], VA[:, 123:125]
    v_norm = VB[:, 0:64]
    v_cb = VB[:, 64:108]

    x_in = at("x_in", [P, KT_TOK, D], A_H)
    mod_raw = [at(f"mod_raw{b}", [P, KD, MB], A_H + KT_TOK * D * 4 + b * KD * MB * 4) for b in range(2)]
    off = A_A
    xs_in = at("xs_in", [NS, D], off); off += D * 4
    c_in = at("c_in", [MLANES, D], off); off += D * 4
    packs = at("packs", [P, 4, P], off); off += 4 * P * 4
    mix_in = at("mix_in", [2 * NS, D], off); off += D * 4
    ffn_in = at("ffn_in", [2 * NS, 2, F], off); off += 2 * F * 4
    assert off <= A_O
    csil = at("csil", [MLANES, D], A_O)
    csT = at("csT", [P, KD, MLANES], A_O + D * 4)
    ptmp = at("ptmp", [P, KF, NS], A_O + D * 4 + 512)
    mrow = [at(f"mrow{i}", [MLANES, MB], A_O + D * 4 + 1536 + i * MB * 4) for i in range(2)]
    off = A_A
    a_sb = at("a_sb", [P, 2 + T], off); off += (2 + T) * 4 + 24
    y_sb = at("y_sb", [P, T], off); off += T4
    g_sb = at("g_sb", [P, T], off); off += T4
    g_parts = at("g_parts", [P, 2, T], off, F32R); off += 2 * T4
    tail = at("tail", [P, KF, TAIL], off); off += KF * TAIL * 4 + 16
    tail_t = at("tail_t", [TAIL, F], off); off += F * 4
    assert off <= A_O
    off = A_A
    q_raw = at("q_raw", [P, KQ, T], off); off += KQ * T4
    l_raw = at("l_raw", [P, KC, T], off); off += KC * T4
    tab = at("tab", [P, T], off); off += T4
    p_t = at("p_t", [P, KT_TOK, 512], off); off += KT_TOK * 2048
    kvb = at("kvb", [P, KC, DN + DV], off); off += KC * (DN + DV) * 4
    assert off <= A_O
    tok = [at(f"tok{i}", [P, KR + DR], A_A + i * 1280) for i in range(2)]
    off = A_H
    qn_hi = at("qn_hi", [P, KQ, T], off, F32R); off += KQ * T4
    qn_lo = at("qn_lo", [P, KQ, T], off, F32R); off += KQ * T4
    latn = at("latn", [P, KC, T], off); off += KC * T4
    kpe = at("kpe", [DR, T], off); off += T4
    qno = at("qno", [P, T], off); off += T4
    qpe = at("qpe", [DR, T], off); off += T4
    kno = at("kno", [P, TP], off); off += TP * 4
    v_sb = at("v_sb", [P, KT_TOK, P], off); off += KT_TOK * P * 4
    p_sb = [at(f"p_sb{i}", [P, TP], off + i * TP * 4) for i in range(2)]; off += 2 * TP * 4
    wkT = at("wkT", [P, KC, P], off); off += KC * P * 4
    assert off <= A_W
    sqm = at("sqm", [P, KQ, T], A_O)
    rsm = at("rsm", [P, T], A_O + KQ * T4)
    varm = at("varm", [P, T], A_H + 2 * KQ * T4 + KC * T4 + T4)
    rootm = at("rootm", [P, T], A_H + 2 * KQ * T4 + KC * T4 + 2 * T4)
    off = A_O
    oh = [at(f"oh{i}", [P, 2, 512], off + i * 4096, F32R) for i in range(2)]; off += 8192
    rope1 = at("rope1", [DR, T], off); off += T4
    st = at("st", [P, 8, 2], off); off += 64
    qlat = at("qlat", [P, KC, NS, H], off); off += KC * 256
    qpes = at("qpes", [DR, NS, H], off); off += 256
    lats = at("lats", [P, KC, NS], off); off += KC * 32
    kpes = at("kpes", [DR, NS], off); off += 32
    q_now = [at(f"q_now{i}", [P, KC + 1, H], off + i * (KC + 1) * 32) for i in range(2)]; off += 2 * (KC + 1) * 32
    l_now = [at(f"l_now{i}", [P, KC + 1, 1], off + i * 32) for i in range(2)]; off += 64
    olat = at("olat", [P, KC, H, NS], off); off += KC * 256
    ovs = at("ovs", [P, 2, H, NS], off, F32R); off += 512
    dm = at("dm", [P, 8 * 6], off); off += 192
    ptab = at("ptab", [1, NS * NPG], off, I32); off += NS * NPG * 4
    assert off <= A_C
    pg = [at(f"pg{i}", [P, NPG, KR], A_H + i * NPG * KR * 4) for i in range(2)]
    off = A_A
    pgr = [at(f"pgr{i}", [P, NPG, DR], off + i * NPG * DR * 4) for i in range(2)]; off += 2 * NPG * DR * 4
    kT = [at(f"kT{i}", [P, 3, 512], off + i * 6144) for i in range(2)]; off += 2 * 6144
    e_t = at("e_t", [P, NPG, H], off); off += NPG * 32
    e_new = at("e_new", [1, H], off); off += 32
    o_row = at("o_row", [H, KR], off); off += KR * 4
    vnew = [at(f"vnew{i}", [1, KR], off + i * 1024) for i in range(2)]; off += 2048
    assert off <= A_O
    s_row = [at(f"s_row{i}", [H, PAST + 1], A_W + i * (PAST + 8) * 4) for i in range(2)]
    assert 2 * (PAST + 8) <= 9 * KD * P
    y_tok = [at(f"y_tok{i}", [P, D], A_H + i * D * 4) for i in range(2)]
    wv = at("wv", [P, KC, H, DV], A_A)

    with ExitStack() as ctx:
        ps = ctx.enter_context(nc.psum_tensor("ps", [P, 8, 512], F32))

        def bank(b):
            return ps[:, b, :]

        def upset(s):
            return ps[:, 3 * s:3 * s + NU, 0:UC]

        def chunked(ap):
            return ap.rearrange("p (c n) -> p c n", c=NU)

        def sem(name):
            return ctx.enter_context(nc.semaphore(name))

        const_ready = sem("const_ready")
        vec_in, c_loaded, mix_loaded, ffn_loaded = sem("vec_in"), sem("c_loaded"), sem("mix_loaded"), sem("ffn_loaded")
        x_loaded, xs_loaded, state_out = sem("x_loaded"), sem("xs_loaded"), sem("state_out")
        csil_ready = sem("csil_ready")
        setup_t, setup_e = sem("setup_t"), sem("setup_e")
        xt_t, xt_e = sem("xt_t"), sem("xt_e")
        mod_loaded = [sem("mod_loaded0"), sem("mod_loaded1")]
        mod_mm, mrow_e = sem("mod_mm"), sem("mrow_e")
        mod_t, mod_done = sem("mod_t"), sem("mod_done")
        raw_ready = [sem(f"raw_ready{s}") for s in range(3)]
        hi_ready = [sem(f"hi_ready{s}") for s in range(3)]
        w_ready = [sem(f"w_ready{s}") for s in range(3)]
        w_done = [sem(f"w_done{s}") for s in range(3)]
        set_free = [sem("set_free0"), sem("set_free1")]
        conv_done, act_done, g_ready, g_out = sem("conv_done"), sem("act_done"), sem("g_ready"), sem("g_out")
        gh_ready, gl_ready = sem("gh_ready"), sem("gl_ready")
        tail_ready, tail_t_done, tail_e, tail_out = sem("tail_ready"), sem("tail_t_done"), sem("tail_e"), sem("tail_out")
        act_in = [sem(f"act_in{n}") for n in range(3)]
        var_ready, root_ready = sem("var_ready"), sem("root_ready")
        sq_ready, ss_ready, stat_ready = sem("sq_ready"), sem("ss_ready"), sem("stat_ready")
        x_done, t_ready, hh_ready, h_ready = sem("x_done"), sem("t_ready"), sem("hh_ready"), sem("h_ready")
        dve_step, act_step = sem("dve_step"), sem("act_step")
        tab_in, kvb_in = sem("tab_in"), sem("kvb_in")
        qn_r, lat_r, kpe_r = sem("qn_r"), sem("lat_r"), sem("kpe_r")
        qn_t = sem("qn_t")
        tok_t, tok_e, tok_out = sem("tok_t"), sem("tok_e"), [sem("tok_out0"), sem("tok_out1")]
        qpe_r, qlat_r = sem("qpe_r"), sem("qlat_r")
        kv_mm, kv_e = sem("kv_mm"), sem("kv_e")
        s_mm, nm_ready, e_ready, p_ready = sem("s_mm"), sem("nm_ready"), sem("e_ready"), sem("p_ready")
        p_t_mm, p_t_e, pv_mm, pv_e = sem("p_t_mm"), sem("p_t_e"), sem("pv_mm"), sem("pv_e")
        pv_h, ov_h = sem("pv_h"), sem("ov_h")
        head_out = [sem("head_out0"), sem("head_out1")]
        sn_mm, pt_in, sc_e = sem("sn_mm"), sem("pt_in"), sem("sc_e")
        pg_in = [[sem(f"pg_in{u}_{q}") for q in range(4)] for u in range(2)]
        rope_go = sem("rope_go")
        pgr_in, vn_in = [sem("pgr_in0"), sem("pgr_in1")], [sem("vn_in0"), sem("vn_in1")]
        kt_mm, kt_ea, kt_ed, sc_mm = sem("kt_mm"), sem("kt_ea"), sem("kt_ed"), sem("sc_mm")
        ch_pe, ch_dve, ch_act, dpv, olat_r = sem("ch_pe"), sem("ch_dve"), sem("ch_act"), sem("dpv"), sem("olat_r")
        wv_in, ov_mm, ov_e, ov_out = sem("wv_in"), sem("ov_mm"), sem("ov_e"), sem("ov_out")
        yt_mm, yt_e, y_out = sem("yt_mm"), sem("yt_e"), [sem("y_out0"), sem("y_out1")]

        SETS = 3 * KD // 2 + KF
        NORMS = ND + 4 * ND
        PARTS8 = [(0, 4), (4, 8)]
        PARTS22 = [(0, 8), (8, 16), (16, 22)]

        def down_steps(parts):
            steps = []
            for m in range(0, KD, 2):
                for n, (k0, k1) in enumerate(parts):
                    for u in range(2):
                        steps.append((m + u, n, len(steps) % len(parts), k0, k1))
            return steps

        def down_counts(parts):
            return [(s, KD) for s in range(len(parts))]

        def first_blocks(parts):
            return [(s, k1 - k0) for _, _, s, k0, k1 in down_steps(parts)[:len(parts)]]

        DOWN_BANK = [0, 1, 2, 3, 4, 5, 7, 2]
        DOWN_AGO = [8, 8, 3, 8, 8, 8, 8, 5]

        def block_cols(w, c):
            return w[:, bass.ds(c, P)].rearrange("(k p) m -> p k m", p=P)

        block = ctx.enter_context(nc.Block())

        @block.sync
        def _(sp):
            raws = [Tally() for _ in range(3)]

            def load(slot, dst, src):
                wait(sp, w_ready[slot], raws[slot]())
                sp.dma_start(dst, src).then_inc(raw_ready[slot], 16)
                raws[slot].add()

            def load_block(slot, w, c):
                load(slot, w_raw[slot][:], block_cols(w, c))

            def vrows(t, r0, src):
                sp.dma_start(packs[r0:r0 + src.shape[0], t, :], src).then_inc(vec_in, 16)

            sp.dma_start(c_in[0:1, :], c_prompt).then_inc(c_loaded, 16)
            sp.dma_start(c_in[1:MLANES, :], c_sample).then_inc(c_loaded, 16)
            vrows(0, 0, mod_b.rearrange("l (m p) -> (l m) p", p=P))
            vrows(0, 96, sc_conv_w.rearrange("k (m p) -> (k m) p", p=P))
            vrows(0, 120, qa_norm.rearrange("l (m p) -> (l m) p", p=P))
            vrows(0, 123, kv_norm.rearrange("l (m p) -> (l m) p", p=P))
            for n, v in enumerate((n_mix_pre, n_mix_post, n_ffn_pre, n_ffn_post)):
                vrows(1, 16 * n, v.rearrange("l (m p) -> (l m) p", p=P))
            vrows(1, 64, ffn_conv_b.rearrange("l (m p) -> (l m) p", p=P))
            for l in range(2):
                vrows(2 + l, 0, ffn_conv_w[l].rearrange("k (m p) -> (k m) p", p=P))
            sp.dma_start(mix_in[:], state_mix.rearrange("b k d -> (b k) d")).then_inc(mix_loaded, 16)
            sp.dma_start(ffn_in[:], state_ffn.rearrange("l b k d -> (b k) l d")).then_inc(ffn_loaded, 16)
            sp.dma_start(x_in[:], x_prompt.rearrange("(t p) d -> p t d", p=P)).then_inc(x_loaded, 16)
            sp.dma_start(xs_in[:], x_sample).then_inc(xs_loaded, 16)
            mods = Tally(1)
            for l in range(2):
                with loop(sp, MODS, {mods: 2}) as i:
                    for b in range(2):
                        c = sp.snap(i * (2 * MB) + b * MB)
                        sp.wait_ge(mod_mm, mods())
                        mods.add()
                        sp.dma_start(mod_raw[b][:], mod_w[l][:, bass.ds(c, MB)].rearrange("(k p) m -> p k m", p=P)
                                     ).then_inc(mod_loaded[b], 16)
            for s, c in ((0, D), (1, 2 * D), (2, 0)):
                load(s, w_raw[s][:], block_cols(sc_w_in, c))
            with loop(sp, KD - 1, {raws[0]: 1, raws[1]: 1, raws[2]: 1}) as i:
                for s, c in ((0, D), (1, 2 * D), (2, 0)):
                    cc = sp.snap(i * P + (c + P))
                    load_block(s, sc_w_in, cc)

            def loads_down(w, parts, guards):
                src = w.rearrange("(k p) m -> p k m", p=P)
                with loop(sp, ND, {raws[s]: KD for s in range(len(parts))}) as d:
                    col = sp.snap(d * DC)
                    for n, (m, part, s, k0, k1) in enumerate(down_steps(parts)):
                        load(s, w_raw[s][:, 0:k1 - k0, :], src[:, k0:k1, m * P:(m + 1) * P])
                        if n < 2 * len(parts) and n % 2 == 1:
                            p = n // 2
                            k0, k1 = parts[p]
                            if p == 0:
                                for g, v in guards:
                                    sp.wait_ge(g, v)
                            sp.wait_ge(w_done[s], raws[s](-2))
                            for z, dst in enumerate((act_hi, act_lo)):
                                sp.dma_start(dst[:, k0:k1, :].bitcast(F32), mid_d[z, k0 * P:k1 * P, bass.ds(col, DC)].rearrange(
                                    "(k p) c -> p k c", p=P)).then_inc(act_in[p], 16)

            def loads_ffn(l, guards):
                with loop(sp, KF, {raws[0]: 1, raws[1]: 1}) as i:
                    for s in range(2):
                        cc = sp.snap(i * P + s * F)
                        load_block(s, ffn_w_in[l], cc)
                loads_down(ffn_w_out[l], PARTS22, guards)

            loads_down(sc_w_out, PARTS8, [(g_out, 16 * KD), (tail_out, 32)])
            loads_ffn(0, [(g_out, 16 * (KD + KF)), (tail_out, 64)])
            for m in range(KQ):
                load(m, w_raw[m][:], block_cols(w_qa, m * P))
            for m in range(KC):
                load(m, w_raw[m][:], block_cols(w_kva, m * P))
            src = w_kva.rearrange("(k p) m -> p k m", p=P)
            wait(sp, w_ready[2], raws[2]())
            for d0, c, n in ((0, KR, DR), (DR, KR + DR // 2, DR // 2), (DR + DR // 2, KR, DR // 2)):
                sp.dma_start(w_raw[2][:, :, d0:d0 + n], src[:, :, c:c + n]).then_inc(raw_ready[2], 16)
            raws[2].add()
            wait(sp, w_done[2], raws[2](-2))
            sp.dma_start(tab[:], rope_tab).then_inc(tab_in, 16)
            qsrc = w_qb.rearrange("(k p) m -> p k m", p=P)
            ksrc = w_kvb.rearrange("(k p) m -> p k m", p=P)

            def head_loads(h, first):
                cols = [h * (DN + DR), h * (DN + DR) + DN, h * (DN + DR) + (DN + DR // 2), h * (DN + DV)]
                if not first:
                    cols = [sp.snap(c) for c in cols]
                load(0, w_raw[0][:, 0:KQ, :], qsrc[:, :, bass.ds(cols[0], P)])
                wait(sp, w_ready[1], raws[1]())
                for d0, c, n in ((0, cols[1], DR), (DR, cols[2], DR // 2), (DR + DR // 2, cols[1], DR // 2)):
                    sp.dma_start(w_raw[1][:, 0:KQ, d0:d0 + n], qsrc[:, :, bass.ds(c, n)]).then_inc(raw_ready[1], 16)
                raws[1].add()
                if not first:
                    sp.wait_ge(kv_mm, kvs())
                    kvs.add(4)
                sp.dma_start(kvb[:], ksrc[:, :, bass.ds(cols[3], DN + DV)]).then_inc(kvb_in, 16)

            kvs = Tally(3)
            head_loads(0, True)
            with loop(sp, H - 1, {raws[0]: 1, raws[1]: 1, kvs: 4}) as h:
                head_loads(h + 1, False)
            sp.wait_ge(pv_mm, 2 * H)
            sp.wait_ge(qlat_r, H)
            sp.wait_ge(pt_in, 16)
            sp.wait_ge(tok_out[0], 16 * 10)
            seqs = Tally(1)
            with loop(sp, NS // 2, {seqs: 2}) as i:
                for u in range(2):
                    nb = i * 2 + u
                    r1 = sp.snap(nb)
                    starts = [sp.snap(nb * NPG + q * (NPG // 4)) for q in range(4)]
                    sp.wait_ge(dpv, seqs())
                    sp.dma_start(vnew[u][:], lat_s[bass.ds(r1, 1), :]).then_inc(vn_in[u], 16)
                    seqs.add()
                    for q, e0 in enumerate(starts):
                        with sp.Fori(0, NPG // 4) as j:
                            page = sp.value_load(ptab[0:1, bass.ds(e0 + j, 1)], min_val=0,
                                                 max_val=cache_lat.shape[0] - 1)
                            sp.dma_start(pg[u][:, bass.ds(j + q * (NPG // 4), 1), :],
                                         cache_lat[bass.ds(page, 1)].rearrange("a p c -> p a c")
                                         ).then_inc(pg_in[u][q], 16)
            sp.wait_ge(dpv, NS + 2)
            for c in range(KC):
                sp.dma_start(wv[:, c], w_kvb[c * P:(c + 1) * P, :].rearrange("p (h n) -> p h n", h=H)[:, :, DN:DN + DV]
                             ).then_inc(wv_in, 16)
            sp.wait_ge(ov_e, 1)
            for z in range(2):
                sp.dma_start(mid_d[z, 0:H * DV, TP:T].rearrange("(h p) b -> p h b", p=P), ovs[:, z].bitcast(F32)
                             ).then_inc(ov_out, 16)
            loads_down(w_o, PARTS8, [(head_out[0], 16 * H), (head_out[1], 16 * H), (ov_out, 32)])
            loads_ffn(1, [(g_out, 16 * (KD + 2 * KF)), (tail_out, 96)])
            for t in range(KT_TOK + 1):
                sp.wait_ge(yt_e, 2 * (t + 1))
                if t < KT_TOK:
                    sp.dma_start(y_prompt[t * P:(t + 1) * P, :], y_tok[t % 2][:]).then_inc(y_out[t % 2], 16)
                else:
                    sp.dma_start(y_sample, y_tok[t % 2][0:NS, :]).then_inc(y_out[t % 2], 16)
            sp.wait_ge(y_out[0], 16 * 5)
            sp.wait_ge(y_out[1], 16 * 4)

        @block.gpsimd
        def _(pool):
            pool.memset(ones[:], 1.0)
            pool.memset(ident[:], 0.0).then_inc(const_ready, 1)
            pool.memset(mask_b[:], 0.0).then_inc(const_ready, 1)
            pool.wait_ge(const_ready, 2)
            pool.affine_select(out=ident[:], in_=ident[:], compare_op=ALU.not_equal, fill=1.0, base=0,
                               pattern=[[-1, P]], channel_multiplier=1).then_inc(const_ready, 1)
            pool.affine_select(out=mask_b[:], in_=mask_b[:], compare_op=ALU.is_ge, fill=NEG, base=0,
                               pattern=[[-1, P]], channel_multiplier=1).then_inc(const_ready, 1)
            pool.wait_ge(const_ready, 4)
            pool.tensor_copy(ident_b[:], ident[:]).then_inc(const_ready, 1)
            stores = Tally()

            pool.dma_start(mix_s[:, 0:1, :], state_mix[:, 1:2, :]).then_inc(state_out, 16)
            for l in range(2):
                pool.dma_start(ffn_s[l, :, 0:1, :], state_ffn[l, :, 1:2, :]).then_inc(state_out, 16)

            def store_g(n):
                with loop(pool, n, {stores: 1}) as i:
                    r = pool.snap(i * P)
                    pool.wait_ge(gl_ready, stores(1))
                    pool.dma_start(mid_d[:, bass.ds(r, P), :].rearrange("z p t -> p z t"), g_parts[:].bitcast(F32)
                                   ).then_inc(g_out, 16)
                    stores.add()

            def store_tail(f, dst_p, dst_s, n):
                pool.wait_ge(tail_e, n)
                pool.dma_start(dst_p, tail_t[0:2, 0:f]).then_inc(tail_out, 16)
                pool.dma_start(dst_s, tail_t[2:TAIL, 0:f]).then_inc(tail_out, 16)

            store_g(KD)
            store_tail(D, mix_p, mix_s[:, 1, :], 2)
            store_g(KF)
            store_tail(F, ffn_p[0], ffn_s[0, :, 1, :], 8)
            for t in range(KT_TOK + 1):
                pool.wait_ge(tok_e, t + 1)
                n = P if t < KT_TOK else NS
                dl = lat_p[t * P:(t + 1) * P, :] if t < KT_TOK else lat_s
                dp = pe_p[t * P:(t + 1) * P, :] if t < KT_TOK else pe_s
                pool.dma_start(dl, tok[t % 2][0:n, 0:KR]).then_inc(tok_out[t % 2], 16)
                pool.dma_start(dp, tok[t % 2][0:n, KR:KR + DR]).then_inc(tok_out[t % 2], 16)
            pool.dma_start(ptab[:], page_table.rearrange("(a b) n -> a (b n)", a=1)).then_inc(pt_in, 16)
            pool.wait_ge(pt_in, 16)
            pool.wait_ge(tok_out[0], 16 * 10)
            pool.wait_ge(tok_out[1], 16 * 8)

            def rope_pages(e0, u):
                with pool.Fori(0, NPG) as j:
                    page = pool.value_load(ptab[0:1, bass.ds(e0 + j, 1)], min_val=0, max_val=cache_pe.shape[0] - 1)
                    pool.dma_start(pgr[u][:, bass.ds(j, 1), :],
                                   cache_pe[bass.ds(page, 1)].rearrange("a p c -> p a c")).then_inc(pgr_in[u], 16)

            for u in range(2):
                rope_pages(u * NPG, u)
            with loop(pool, H, {}) as h:
                r = pool.snap(h * DV)
                for half in range(2):
                    pool.wait_ge(pv_e, h * 2 + (half + 1))
                    pool.dma_start(mid_d[:, bass.ds(r, DV), half * 512:(half + 1) * 512].rearrange(
                        "z p t -> p z t"), oh[half][:].bitcast(F32)).then_inc(head_out[half], 16)
            seqs = Tally(3)
            with loop(pool, NS // 2 - 1, {seqs: 2}) as i:
                for u in range(2):
                    e0 = pool.snap(i * (2 * NPG) + (2 + u) * NPG)
                    pool.wait_ge(dpv, seqs())
                    pool.sem_inc(rope_go, 1)
                    seqs.add()
                    rope_pages(e0, u)
            store_g(KF)
            store_tail(F, ffn_p[1], ffn_s[1, :, 1, :], 14)
            pool.wait_ge(tail_out, 16 * 6)
            pool.wait_ge(state_out, 16 * 3)
            pool.wait_ge(tok_out[0], 16 * 10)
            pool.wait_ge(tok_out[1], 16 * 8)

        @block.scalar
        def _(act):
            splits = [Tally() for _ in range(3)]
            raw_n = [Tally() for _ in range(3)]
            pres, steps, roots = Tally(), Tally(), Tally()

            def hi_split(s, k, dmas=1):
                raw_n[s].add(16 * dmas)
                act.wait_ge(raw_ready[s], raw_n[s]())
                wait(act, w_done[s], splits[s]())
                act.activation(w_hi[s][:, 0:k, :], w_raw[s][:, 0:k, :], ACT.Copy).then_inc(hi_ready[s], 1)
                splits[s].add()

            def split_next(blocks):
                for b in blocks:
                    hi_split(*b)

            act.preload_act_table(ACT.Silu)
            act.wait_ge(c_loaded, 32)
            act.activation(csil[:], c_in[:], ACT.Silu).then_inc(csil_ready, 1)
            n = 0
            for t in range(KT_TOK + 1):
                w = P if t < KT_TOK else NS
                for half in range(2):
                    act.wait_ge(xt_t, n + 1)
                    act.activation(xT[:, 4 * half:4 * half + 4, t * P:t * P + w],
                                   bank(5 + n % 3).rearrange("p (k t) -> p k t", k=4)[:, :, 0:w], ACT.Copy
                                   ).then_inc(xt_e, 1)
                    n += 1

            mms, turned = Tally(2), Tally(-2)

            def mod_evac():
                for b in range(2):
                    act.wait_ge(mod_mm, mms(1))
                    wait(act, mod_t, turned(1))
                    mms.add()
                    turned.add()
                    act.activation(mrow[b][:], bank(b)[0:MLANES, :], ACT.Copy).then_inc(mrow_e, 1)

            mod_evac()
            with loop(act, 2 * MODS - 1, {mms: 2, turned: 2}):
                mod_evac()

            def pre_squares(cols):
                act.wait_ge(x_done, pres(1))
                act.activation(sq[:], xT[:, :, cols], ACT.Square).then_inc(sq_ready, 1)

            def pre_round(cols):
                act.wait_ge(t_ready, pres(1))
                act.activation(h_hi[:, :, cols], sq[:], ACT.Copy).then_inc(hh_ready, 1)
                pres.add()

            def square_root(v=var, w=root_b):
                act.wait_ge(var_ready, roots(1))
                roots.add()
                act.activation(w[:], v[:], ACT.Sqrt).then_inc(root_ready, 1)

            def post_squares():
                act.wait_ge(act_step, steps())
                act.activation(sq[:], o_sb[:], ACT.Square).then_inc(sq_ready, 1)

            act.wait_ge(xt_e, 2 * (KT_TOK + 1))
            for d in range(ND):
                if d:
                    act.wait_ge(h_ready, d)
                pre_squares(slice(d * DC, (d + 1) * DC))
                square_root()
                pre_round(slice(d * DC, (d + 1) * DC))

            def down(parts, nxt, last_norm):
                order, ahead = down_steps(parts), len(parts)

                def tiles(m0, m1, nxt_blocks=None):
                    for n, (m, _, s, _, _) in enumerate(order):
                        if m0 <= m < m1:
                            if n + ahead >= len(order) and nxt_blocks is not None:
                                continue
                            _, _, s, k0, k1 = order[(n + ahead) % len(order)]
                            hi_split(s, k1 - k0)
                    if m1 == KD and nxt_blocks is not None:
                        split_next(nxt_blocks)

                def evac(m0, m1):
                    for m in range(m0, m1):
                        s = [s for m_, _, s, _, _ in order if m_ == m][-1]
                        act.wait_ge(w_done[s], done[s](m // 2 * 2 + 2))
                        act.activation(o_sb[:, m, :], bank(DOWN_BANK[m])[:, 0:DC], ACT.Copy).then_inc(act_step, 1)
                        steps.add()
                        if m == KD - 1:
                            for t in done.values():
                                t.add(KD)

                def chunk(prev_cols, nxt_blocks=None):
                    tiles(0, 2)
                    if prev_cols is not None:
                        square_root()
                        act.wait_ge(x_done, pres(1))
                    evac(0, 2)
                    if prev_cols is not None and not last_norm:
                        pre_squares(prev_cols)
                    tiles(2, 4)
                    evac(2, 4)
                    tiles(4, 6)
                    evac(4, 6)
                    if prev_cols is not None:
                        if last_norm:
                            pres.add()
                        else:
                            square_root()
                            pre_round(prev_cols)
                    tiles(6, 8, nxt_blocks)
                    evac(6, 8)
                    if prev_cols is not None and not last_norm:
                        act.wait_ge(h_ready, pres())
                    post_squares()

                done = {s: Tally(splits[s].n - 1) for s in range(len(parts))}
                per = {splits[s]: KD for s in done}
                per.update({raw_n[s]: 16 * KD for s in done})
                per.update({t: KD for t in done.values()})
                act.preload_act_table(ACT.Sqrt)
                chunk(None)
                per.update({steps: KD, pres: 1, roots: 1 if last_norm else 2})
                with loop(act, ND - 2, per) as i:
                    c = act.snap(i * DC)
                    chunk(bass.ds(c, DC))
                chunk(slice((ND - 2) * DC, (ND - 1) * DC), nxt)
                cols = slice((ND - 1) * DC, T)
                square_root()
                if last_norm:
                    pres.add()
                else:
                    pre_squares(cols)
                    square_root()
                    pre_round(cols)

            conv_base = [0]
            gs, g_n = Tally(), Tally()

            def up_run(n, n_slots, ffn_layer, nxt):
                own = [(s, KD) for s in range(n_slots)]
                convs = Tally(conv_base[0])

                def body(j, blocks, parity):
                    for s in range(n_slots):
                        if s == 0:
                            act.wait_ge(w_done[0], splits[0]())
                        if blocks is own:
                            hi_split(s, KD)
                        if s == 0:
                            wait(act, conv_done, convs())
                            act.activation(chunked(a_sb[:, 2:2 + T]), upset(parity), ACT.Copy
                                           ).then_inc(set_free[parity], 1)
                            convs.add()
                            if ffn_layer is not None:
                                act.wait_ge(conv_done, convs())
                                act.activation(y_sb[:], y_sb[:], ACT.Silu,
                                               bias=v_cb[:, bass.ds(j + ffn_layer * KF, 1)]).then_inc(act_done, 1)
                    gs.add()
                    act.wait_ge(g_ready, gs())
                    wait(act, g_out, g_n())
                    g_n.add(16)
                    act.activation(g_parts[:, 0, :], g_sb[:], ACT.Copy).then_inc(gh_ready, 1)
                    if blocks is not own:
                        split_next(blocks)

                per = {splits[s]: 1 for s in range(n_slots)}
                per.update({raw_n[s]: 16 for s in range(n_slots)})
                per.update({convs: 1, gs: 1, g_n: 16})
                if n_slots == 2:
                    with loop(act, n - 1, per) as i:
                        body(i, own, 0)
                    body(n - 1, nxt, 0)
                else:
                    with loop(act, n // 2 - 1, {t: 2 * k for t, k in per.items()}) as i:
                        body(None, own, 0)
                        body(None, own, 1)
                    body(None, own, 0)
                    body(None, nxt, 1)
                conv_base[0] = convs.n

            split_next([(0, KD), (1, KD), (2, KD)])
            P8, P22 = first_blocks(PARTS8), first_blocks(PARTS22)
            up_run(KD, 3, None, P8)
            down(PARTS8, [(0, KD), (1, KD)], False)
            act.preload_act_table(ACT.Silu)
            up_run(KF, 2, 0, P22)
            down(PARTS22, [(0, KD), (1, KD), (2, KD)], False)

            for m in range(KQ + KC):
                s = m % 3
                act.wait_ge(w_done[s], splits[s]())
                if m < 3:
                    hi_split(s, KD, 3 if m == 2 else 1)
                dst = q_raw[:, m, :] if m < KQ else l_raw[:, m - KQ, :]
                act.activation(chunked(dst), upset(m % 2), ACT.Copy).then_inc(set_free[m % 2], 1)
            act.wait_ge(set_free[0], SETS + 2)
            act.wait_ge(set_free[1], SETS + 1)
            act.activation(sqm[:], q_raw[:], ACT.Square).then_inc(sq_ready, 1)
            act.wait_ge(ss_ready, NORMS + 1)
            act.wait_ge(set_free[1], SETS + 2)
            act.wait_ge(set_free[0], SETS + 3)
            act.activation(sqm[:, 0:KC, :], l_raw[:], ACT.Square).then_inc(sq_ready, 1)
            act.wait_ge(w_done[2], splits[2]())
            square_root(varm, rootm)
            act.wait_ge(qn_t, 1)
            act.activation(qn_hi[:], q_raw[:], ACT.Copy).then_inc(hh_ready, 1)
            square_root(varm, rootm)

            act.preload_act_table(ACT.Exp)
            hi_split(0, KQ)
            hi_split(1, KQ, 3)

            def head(more):
                act.wait_ge(w_done[0], splits[0]())
                if more:
                    hi_split(0, KQ)
                act.activation(chunked(qno[:]), upset(0), ACT.Copy).then_inc(set_free[0], 1)
                act.wait_ge(w_done[1], splits[1]())
                if more:
                    hi_split(1, KQ, 3)
                act.wait_ge(kv_mm, h4(1))
                act.activation(kno[:].rearrange("p (c n) -> p c n", c=2), ps[:, 6:8, :], ACT.Copy).then_inc(kv_e, 1)
                act.wait_ge(kv_mm, h4(2))
                act.activation(v_sb[:].rearrange("p (c t) v -> p c (t v)", c=2), ps[:, 0:2, :], ACT.Copy
                               ).then_inc(kv_e, 1)
                act.wait_ge(kv_mm, h4(3))
                act.activation(wkT[:].rearrange("p c n -> p (c n)"), bank(2)[:, 0:KC * P], ACT.Copy
                               ).then_inc(kv_e, 1)
                h4.add(4)

                def exp(q):
                    nk = (q + 1) * P
                    act.wait_ge(nm_ready, h8(q + 1))
                    wait(act, p_t_mm, h8(q - 1))
                    act.activation(p_sb[q % 2][:, 0:nk], ps[:, 2 * (q % 2):2 * (q % 2) + 2, :].rearrange(
                        "p b n -> p (b n)")[:, 0:nk], ACT.Exp, bias=st[:, 2 + q % 2, 0:1], scale=SCALE,
                        accum_out=st[:, 4 + q % 2, 0:1]).then_inc(e_ready, 1)

                def evac_t(q):
                    act.wait_ge(p_t_mm, h8(q + 1))
                    if q in (0, 4):
                        wait(act, pv_mm, h2(q // 4))
                    ins = None
                    for b in range(q // 4 + 1):
                        k0, k1 = 4 * b, min(4 * b + 4, q + 1)
                        ins = act.activation(p_t[:, k0:k1, (q % 4) * P:(q % 4 + 1) * P],
                                             bank(4 + b)[:, 0:(k1 - k0) * P].rearrange("p (k n) -> p k n", n=P),
                                             ACT.Copy)
                    ins.then_inc(p_t_e, 1)

                def evac_o(half):
                    act.wait_ge(pv_mm, h2(half + 1))
                    wait(act, head_out[half], h16())
                    act.activation(oh[half][:, 0, :], bank(6 + half), ACT.Copy).then_inc(pv_h, 1)

                exp(0)
                for q in range(1, KT_TOK):
                    exp(q)
                    if q == 5:
                        evac_o(0)
                    evac_t(q - 1)
                evac_t(KT_TOK - 1)
                evac_o(1)
                h8.add(8)
                h2.add(2)
                h16.add(16)

            h4, h8, h2, h16 = Tally(), Tally(), Tally(), Tally()
            head(True)
            with loop(act, H - 2, {splits[0]: 1, splits[1]: 1, raw_n[0]: 16, raw_n[1]: 48, h4: 4, h8: 8, h2: 2,
                                   h16: 16}):
                head(True)
            head(False)

            groups = Tally()
            seqs = Tally()

            def decode_exp(u):
                act.wait_ge(ch_dve, seqs(1))
                seqs.add(3)
                act.activation(s_row[u][:], s_row[u][:], ACT.Exp, bias=dm[0:H, 1:2], scale=SCALE,
                               accum_out=dm[0:H, 2:3]).then_inc(ch_act, 1)

            def decode_scores_e(u, g):
                act.wait_ge(sc_mm, score_n(1))
                score_n.add()
                act.activation(s_row[u][:, g * 512:(g + 1) * 512], bank(6)[0:H, :], ACT.Copy).then_inc(sc_e, 1)

            def decode_seq(u, prev):
                for g in range(8):
                    b0 = 3 * (g % 2)
                    act.wait_ge(kt_mm, groups(1))
                    wait(act, sc_mm, groups(-1))
                    act.activation(kT[g % 2][:, 0, :], bank(b0), ACT.Copy)
                    act.activation(kT[g % 2][0:DR, 2, :], bank(b0 + 2)[0:DR, :], ACT.Copy).then_inc(kt_ea, 1)
                    groups.add()
                    if g:
                        decode_scores_e(u, g - 1)
                    elif prev:
                        decode_exp(1 - u)
                decode_scores_e(u, 7)

            score_n = Tally()
            decode_seq(0, False)
            decode_seq(1, True)
            with loop(act, NS // 2 - 1, {groups: 16, seqs: 6, score_n: 16}):
                decode_seq(0, True)
                decode_seq(1, True)
            decode_exp(1)
            act.wait_ge(ov_mm, 1)
            act.activation(ovs[:, 0], bank(0)[:, 0:H * NS].rearrange("p (h b) -> p h b", h=H), ACT.Copy
                           ).then_inc(ov_h, 1)
            split_next(P8)
            down(PARTS8, [(0, KD), (1, KD)], False)
            act.preload_act_table(ACT.Silu)
            up_run(KF, 2, 1, P22)
            down(PARTS22, [], True)
            for n in range(2 * (KT_TOK + 1)):
                t, half = n // 2, n % 2
                w = P if t < KT_TOK else NS
                act.wait_ge(yt_mm, n + 1)
                if t >= 2:
                    act.wait_ge(y_out[t % 2], 16 * (t // 2))
                act.activation(y_tok[t % 2][0:w, half * 512:(half + 1) * 512], bank(n % 4)[0:w, :], ACT.Copy
                               ).then_inc(yt_e, 1)

        @block.vector
        def _(dve):
            steps = Tally()
            splits = [Tally() for _ in range(3)]
            stats, pres = Tally(), Tally()

            def step(ins):
                ins.then_inc(dve_step, 1)
                steps.add()

            def settle():
                dve.wait_ge(dve_step, steps())

            def lo_split(s, k, dmas=1):
                dve.wait_ge(hi_ready[s], splits[s](1))
                dve.tensor_tensor(w_lo[s][:, 0:k, :], w_raw[s][:, 0:k, :], w_hi[s][:, 0:k, :].bitcast(F32),
                                  ALU.subtract).then_inc(w_ready[s], 1)
                splits[s].add()

            def split_next(blocks):
                for b in blocks:
                    lo_split(*b)

            dve.wait_ge(setup_t, 1)
            for t, r in enumerate((125, 108, 66, 66)):
                step(dve.tensor_copy(vec[:, t, 0:r], bank(0)[:, t * P:t * P + r]))
            dve.wait_ge(setup_t, 2)
            dve.tensor_copy(csT[:], bank(1)[:, 0:KD * MLANES].rearrange("p (k c) -> p k c", k=KD)).then_inc(setup_e, 1)
            settle()

            def taps(b, kt, w, dst):
                state = bank(b)[:, 0:kt * 2 * NS].rearrange("p (m b k) -> p m b k", m=kt, b=NS)
                for k, out in ((0, dst), (1, ptmp[:, 0:kt, :])):
                    step(dve.tensor_tensor(out, state[:, :, :, k],
                                           w[:, k * kt:(k + 1) * kt].unsqueeze(2).to_broadcast([P, kt, NS]), ALU.mult))
                settle()
                step(dve.tensor_tensor(dst, dst, ptmp[:, 0:kt, :], ALU.add))
                settle()

            dve.wait_ge(setup_t, 3)
            taps(2, KD, v_scw, prev_mix[:])
            for l in range(2):
                dve.wait_ge(setup_t, 4 + l)
                taps(3 + l, KF, vec[:, 2 + l, :], prev_ffn[:, l])
            dve.sem_inc(setup_e, 1)

            mods = Tally()
            with loop(dve, MODS, {mods: 4}) as i:
                for b in range(4):
                    mods.add()
                    dve.wait_ge(mod_t, mods())
                    m0 = i * 16 + 4 * b
                    dve.tensor_tensor(modv[:, bass.ds(m0, 4), :],
                                      bank(2 + b % 2)[:, 0:4 * MLANES].rearrange("p (m c) -> p m c", m=4),
                                      v_modb[:, bass.ds(m0, 4)].unsqueeze(2).to_broadcast([P, 4, MLANES]),
                                      ALU.add).then_inc(mod_done, 1)
            dve.wait_ge(mod_done, 4 * MODS)

            def mod(l, kind):
                return modv[:, (l * MODS + kind) * KD:(l * MODS + kind + 1) * KD, :]

            def gain(n, l):
                return v_norm[:, (2 * n + l) * KD:(2 * n + l + 1) * KD].unsqueeze(2).to_broadcast([P, KD, MLANES])

            for l in range(2):
                for s in range(2):
                    step(dve.scalar_tensor_tensor(mod(l, 3 * s + 1), mod(l, 3 * s + 1), 1.0, gain(2 * s, l),
                                                  ALU.add, ALU.mult))
                    step(dve.tensor_tensor(mod(l, 3 * s + 2), mod(l, 3 * s + 2), gain(2 * s + 1, l), ALU.mult))
            settle()

            def rsqrt(dst, v, w, src, n):
                dve.wait_ge(stat_ready, stats(1))
                stats.add()
                dve.tensor_scalar(v, src, 1.0 / n, EPS, ALU.mult, ALU.add).then_inc(var_ready, 1)
                dve.wait_ge(root_ready, stats())
                newton(dst, v, w)

            def newton(dst, v, w):
                step(dve.reciprocal(dst, w))
                settle()
                step(dve.tensor_tensor(w, dst, v, ALU.mult))
                settle()
                step(dve.scalar_tensor_tensor(w, w, -0.5, dst, ALU.mult, ALU.mult))
                settle()
                step(dve.scalar_tensor_tensor(dst, w, 1.5, dst, ALU.add, ALU.mult))
                settle()

            def sum_squares(src, dst):
                dve.wait_ge(sq_ready, stats(1))
                dve.tensor_reduce(dst, src.rearrange("p k t -> p t k"), AX.X, ALU.add).then_inc(ss_ready, 1)

            def root(n):
                rsqrt(rs[:], var[:], root_b[:], bank(6)[:, 0:DC], n)

            def pre_norm(l, s, cols, last):
                root(D)
                step(dve.tensor_tensor(sq[:], xT[:, :, cols], rs[:].unsqueeze(1).to_broadcast([P, KD, DC]), ALU.mult))
                settle()
                n = PL if last else DC
                A, B = mod(l, 3 * s + 1), mod(l, 3 * s)
                ins = None
                if last:
                    step(dve.tensor_tensor(tmp_s[:], sq[:, :, PL:DC], A[:, :, 1:MLANES], ALU.mult))
                    settle()
                    dve.tensor_tensor(sq[:, :, PL:DC], tmp_s[:], B[:, :, 1:MLANES], ALU.add)
                for k in range(KD):
                    ins = dve.tensor_scalar(sq[:, k, 0:n], sq[:, k, 0:n], A[:, k, 0:1], B[:, k, 0:1], ALU.mult, ALU.add)
                ins.then_inc(t_ready, 1)
                pres.add()
                dve.wait_ge(hh_ready, pres(hh_more[0]))
                dve.tensor_tensor(h_lo[:, :, cols], sq[:], h_hi[:, :, cols].bitcast(F32), ALU.subtract
                                  ).then_inc(h_ready, 1)

            hh_more = [0]

            def post_norm(l, s, cols, last):
                root(D)
                step(dve.tensor_tensor(o_sb[:], o_sb[:], rs[:].unsqueeze(1).to_broadcast([P, KD, DC]), ALU.mult))
                settle()
                n = PL if last else DC
                G = mod(l, 3 * s + 2)
                if last:
                    step(dve.tensor_tensor(tmp_s[:], o_sb[:, :, PL:DC], G[:, :, 1:MLANES], ALU.mult))
                    settle()
                    dve.tensor_tensor(xT[:, :, TP:T], xT[:, :, TP:T], tmp_s[:], ALU.add)
                    cols = slice((ND - 1) * DC, TP)
                for k in range(KD):
                    ins = dve.scalar_tensor_tensor(xT[:, k, cols], o_sb[:, k, 0:n], G[:, k, 0:1], xT[:, k, cols],
                                                   ALU.mult, ALU.add)
                ins.then_inc(x_done, 1)

            dve.wait_ge(xt_e, 2 * (KT_TOK + 1))
            dve.sem_inc(x_done, ND)
            for d in range(ND):
                sum_squares(sq[:], rs[:])
                pre_norm(0, 0, slice(d * DC, (d + 1) * DC), d == ND - 1)

            def down(parts, nxt, norm, nxt_norm):
                order, ahead = down_steps(parts), len(parts)

                def tiles(m0, m1, nxt_blocks=None):
                    for n, (m, _, s, _, _) in enumerate(order):
                        if m0 <= m < m1:
                            if n + ahead >= len(order) and nxt_blocks is not None:
                                continue
                            _, _, s, k0, k1 = order[(n + ahead) % len(order)]
                            lo_split(s, k1 - k0)
                    if m1 == KD and nxt_blocks is not None:
                        split_next(nxt_blocks)

                def chunk(prev, nxt_blocks=None):
                    tiles(0, 2)
                    if prev is not None:
                        post_norm(*norm, prev, False)
                        if nxt_norm is not None:
                            sum_squares(sq[:], rs[:])
                    tiles(2, 6)
                    if prev is not None and nxt_norm is not None:
                        pre_norm(*nxt_norm, prev, False)
                    tiles(6, 8, nxt_blocks)
                    sum_squares(sq[:], rs[:])

                per_norm = 1 if nxt_norm is None else 2
                chunk(None)
                per = {splits[s]: KD for s in range(len(parts))}
                per.update({stats: per_norm, steps: STEP_POST + (per_norm - 1) * STEP_PRE})
                if nxt_norm is not None:
                    per[pres] = 1
                with loop(dve, ND - 2, per) as i:
                    c = dve.snap(i * DC)
                    chunk(bass.ds(c, DC))
                chunk(slice((ND - 2) * DC, (ND - 1) * DC), nxt)
                cols = slice((ND - 1) * DC, T)
                post_norm(*norm, cols, True)
                if nxt_norm is not None:
                    sum_squares(sq[:], rs[:])
                    pre_norm(*nxt_norm, cols, True)

            STEP_POST, STEP_PRE = 5, 5

            def conv(j, taps_w, kt, prev):
                w = [taps_w[:, bass.ds(j + k * kt, 1)] for k in range(3)]
                step(dve.tensor_copy(tail[:, bass.ds(j, 1), :], a_sb[:, 2 + TP - 2:2 + T].unsqueeze(1)))
                step(dve.tensor_scalar(y_sb[:, 0:TP], a_sb[:, 0:TP], w[0], None, ALU.mult))
                step(dve.tensor_copy(y_sb[:, TP:T].unsqueeze(1), prev[:, bass.ds(j, 1), :]))
                settle()
                step(dve.scalar_tensor_tensor(y_sb[:, 0:TP], a_sb[:, 1:1 + TP], w[1], y_sb[:, 0:TP],
                                              ALU.mult, ALU.add))
                settle()
                dve.scalar_tensor_tensor(y_sb[:], a_sb[:, 2:2 + T], w[2], y_sb[:], ALU.mult, ALU.add
                                         ).then_inc(conv_done, 1)

            def tails_out(kt, t0):
                for g in range(-(-kt // 4)):
                    n = min(4, kt - 4 * g)
                    dve.wait_ge(tail_t_done, t0 + g + 1)
                    dve.tensor_copy(tail_t[:, g * 4 * P:(g * 4 + n) * P], bank(6 + g % 2)[0:TAIL, 0:n * P]
                                    ).then_inc(tail_e, 1)

            conv_n, g_n, set0 = Tally(), Tally(), Tally()

            def gate(parity):
                dve.tensor_tensor(chunked(g_sb[:]), chunked(y_sb[:]), upset(parity), ALU.mult).then_inc(g_ready, 1)
                gs.add()
                dve.wait_ge(g_ready, gs())
                dve.sem_inc(set_free[parity], 1)
                wait(dve, g_out, g_n())
                g_n.add(16)
                dve.wait_ge(gh_ready, gs())
                dve.tensor_tensor(g_parts[:, 1, :], g_sb[:], g_parts[:, 0, :].bitcast(F32), ALU.subtract
                                  ).then_inc(gl_ready, 1)

            split_next([(0, KD), (1, KD), (2, KD)])
            step(dve.memset(a_sb[:, 0:2], 0.0))
            settle()
            f0, f1 = Tally(), Tally()

            def mixer(j, parity, own):
                if own:
                    lo_split(0, KD)
                f = (f0, f1)
                f[parity].add()
                dve.wait_ge(set_free[parity], f[parity]())
                if own:
                    lo_split(1, KD)
                else:
                    dve.wait_ge(w_done[1], splits[1]())
                f[1 - parity].add()
                step(dve.tensor_tensor(chunked(a_sb[:, 2:2 + T]), chunked(a_sb[:, 2:2 + T]), upset(1 - parity),
                                       ALU.mult))
                settle()
                dve.sem_inc(set_free[1 - parity], 1)
                conv(j, v_scw, KD, prev_mix[:])
                conv_n.add()
                dve.wait_ge(conv_done, conv_n())
                if own:
                    lo_split(2, KD)
                else:
                    dve.wait_ge(w_done[2], splits[2]())
                f[parity].add()
                gate(parity)

            gs = Tally()
            mixer(0, 0, True)
            mixer(1, 1, True)
            with loop(dve, KD // 2 - 2, {splits[0]: 2, splits[1]: 2, splits[2]: 2, f0: 3, f1: 3, conv_n: 2,
                                         g_n: 32, gs: 2, steps: 10}) as i:
                j = dve.snap(i * 2)
                mixer(j + 2, 0, True)
                mixer(j + 3, 1, True)
            mixer(KD - 2, 0, True)
            mixer(KD - 1, 1, False)
            P8, P22 = first_blocks(PARTS8), first_blocks(PARTS22)
            settle()
            dve.sem_inc(tail_ready, 1)
            tails_out(KD, 0)
            split_next(P8)
            down(PARTS8, [(0, KD), (1, KD)], (0, 0), (0, 1))

            def ffn(l, nxt, t0):
                step(dve.memset(a_sb[:, 0:2], 0.0))
                settle()

                def body(j, own):
                    lo_split(0, KD) if own else dve.wait_ge(w_done[0], splits[0]())
                    f0.add()
                    dve.wait_ge(set_free[0], f0())
                    conv(j, vec[:, 2 + l, :], KF, prev_ffn[:, l])
                    lo_split(1, KD) if own else dve.wait_ge(w_done[1], splits[1]())
                    silus.add()
                    dve.wait_ge(act_done, silus())
                    f1.add()
                    gate(1)

                with loop(dve, KF - 1, {splits[0]: 1, splits[1]: 1, f0: 1, f1: 1, silus: 1, g_n: 16, gs: 1,
                                        steps: 4}) as i:
                    body(i, True)
                body(KF - 1, False)
                settle()
                dve.sem_inc(tail_ready, 1)
                tails_out(KF, t0)
                split_next(nxt)

            silus = Tally()
            ffn(0, P22, 2)
            down(PARTS22, [(0, KD), (1, KD), (2, KD)], (0, 1), (1, 0))

            lo_split(0, KD)
            lo_split(1, KD)
            lo_split(2, KD)
            dve.wait_ge(w_done[2], splits[2]())

            def rope(u, dst, ready):
                step(dve.tensor_tensor(chunked(rope1[:]), upset(u)[0:DR], chunked(tab[0:DR, :]), ALU.mult))
                step(dve.tensor_tensor(chunked(dst[:]), upset(u)[DR:P], chunked(tab[DR:P, :]), ALU.mult))
                settle()
                dve.sem_inc(set_free[u], 1)
                dve.tensor_tensor(dst[:], dst[:], rope1[:], ALU.add).then_inc(ready, 1)

            dve.wait_ge(tab_in, 16)

            def root_all(n):
                dve.wait_ge(stat_ready, stats(1))
                stats.add()
                dve.tensor_scalar(chunked(varm[:]), upset(0), 1.0 / n, EPS, ALU.mult, ALU.add).then_inc(var_ready, 1)
                dve.wait_ge(root_ready, stats())
                newton(rsm[:], varm[:], rootm[:])

            sum_squares(sqm[:], rsm[:])
            root_all(QR)
            step(dve.tensor_tensor(q_raw[:], q_raw[:], rsm[:].unsqueeze(1).to_broadcast([P, KQ, T]), ALU.mult))
            settle()
            for k in range(KQ):
                ins = dve.tensor_scalar(q_raw[:, k, :], q_raw[:, k, :], v_qan[:, k:k + 1], None, ALU.mult)
            ins.then_inc(qn_t, 1)
            sum_squares(sqm[:, 0:KC, :], rsm[:])
            dve.wait_ge(hh_ready, pres(1))
            hh_more[0] = 1
            dve.tensor_tensor(qn_lo[:], q_raw[:], qn_hi[:].bitcast(F32), ALU.subtract).then_inc(qn_r, 1)
            root_all(KR)
            step(dve.tensor_tensor(l_raw[:], l_raw[:], rsm[:].unsqueeze(1).to_broadcast([P, KC, T]), ALU.mult))
            settle()
            for k in range(KC):
                ins = dve.tensor_scalar(latn[:, k, :], l_raw[:, k, :], v_kvn[:, k:k + 1], None, ALU.mult)
            ins.then_inc(lat_r, 1)
            rope(1, kpe, kpe_r)
            lo_split(0, KQ)
            lo_split(1, KQ)
            dve.wait_ge(kpe_r, 1)
            dve.wait_ge(lat_r, 1)
            dve.wait_ge(qn_r, 1)
            step(dve.tensor_copy(lats[:], latn[:, :, TP:T]))
            step(dve.tensor_copy(kpes[:], kpe[:, TP:T]))
            for t in range(KT_TOK + 1):
                n = P if t < KT_TOK else NS
                dve.wait_ge(tok_t, t + 1)
                if t >= 2:
                    dve.wait_ge(tok_out[t % 2], 32 * (t // 2))
                dve.tensor_copy(tok[t % 2][0:n, :], bank(6 + t % 2)[0:n, 0:KR + DR]).then_inc(tok_e, 1)
            h2, h4, h8 = Tally(), Tally(), Tally()

            def head(h, more):
                if more:
                    lo_split(0, KQ)
                    lo_split(1, KQ)
                else:
                    dve.wait_ge(w_done[1], splits[1]())
                step(dve.tensor_tensor(chunked(rope1[:]), upset(1)[0:DR], chunked(tab[0:DR, :]), ALU.mult))
                step(dve.tensor_tensor(chunked(qpe[:]), upset(1)[DR:P], chunked(tab[DR:P, :]), ALU.mult))
                settle()
                step(dve.tensor_tensor(qpe[:], qpe[:], rope1[:], ALU.add))
                settle()
                dve.sem_inc(qpe_r, 1)
                step(dve.tensor_copy(qpes[:, :, bass.ds(h, 1)], qpe[:, TP:T].unsqueeze(2)))
                dve.wait_ge(kv_mm, h4(4))
                h4.add(4)
                dve.tensor_copy(qlat[:, :, :, bass.ds(h, 1)], bank(5)[:, 0:KC * NS].rearrange(
                    "p (c b o) -> p c b o", c=KC, o=1)).then_inc(qlat_r, 1)

                def top(q):
                    u = q % 2
                    dve.wait_ge(s_mm, h8(q + 1))
                    step(dve.tensor_reduce(st[:, u, 0:1], ps[:, 2 * u:2 * u + 2, :].rearrange("p b n -> p (b n)")
                                           [:, 0:(q + 1) * P], AX.X, ALU.max))
                    settle()
                    dve.tensor_scalar(st[:, 2 + u, 0:1], st[:, u, 0:1], -SCALE, None, ALU.mult).then_inc(nm_ready, 1)

                def norm(q):
                    u = q % 2
                    dve.wait_ge(e_ready, h8(q + 1))
                    step(dve.reciprocal(st[:, 6 + u, 0:1], st[:, 4 + u, 0:1]))
                    settle()
                    dve.tensor_scalar(p_sb[u][:, 0:(q + 1) * P], p_sb[u][:, 0:(q + 1) * P], st[:, 6 + u, 0:1], None,
                                      ALU.mult).then_inc(p_ready, 1)

                def low_out(half):
                    dve.wait_ge(pv_h, h2(half + 1))
                    dve.tensor_tensor(oh[half][:, 1, :], bank(6 + half), oh[half][:, 0, :].bitcast(F32), ALU.subtract
                                      ).then_inc(pv_e, 1)

                top(0)
                for q in range(1, KT_TOK):
                    top(q)
                    norm(q - 1)
                    if q == 6:
                        low_out(0)
                norm(KT_TOK - 1)
                low_out(1)
                h8.add(8)
                h2.add(2)

            with loop(dve, H - 1, {splits[0]: 1, splits[1]: 1, h2: 2, h4: 4, h8: 8, steps: 20}) as h:
                head(h, True)
            head(H - 1, False)
            groups, chains, scored = Tally(), Tally(), Tally()

            def top_all(u):
                scored.add(8)
                dve.wait_ge(sc_e, scored())
                chains.add()
                dve.wait_ge(sn_mm, chains())
                step(dve.tensor_copy(s_row[u][:, PAST:PAST + 1], bank(7)[0:H, 500:501]))
                settle()
                step(dve.tensor_reduce(dm[0:H, 0:1], s_row[u][:], AX.X, ALU.max))
                settle()
                dve.tensor_scalar(dm[0:H, 1:2], dm[0:H, 0:1], -SCALE, None, ALU.mult).then_inc(ch_dve, 1)

            def chain(n, b):
                if n == 0:
                    dve.wait_ge(ch_pe, turned(1))
                    step(dve.reciprocal(dm[0:H, 3:4], dm[0:H, 2:3]))
                    dve.tensor_copy(e_new[:], bank(7)[0:1, NPG * H:(NPG + 1) * H])
                    dve.tensor_copy(e_t[:], bank(7)[:, 0:NPG * H].rearrange("p (n h) -> p n h", h=H)
                                    ).then_inc(ch_dve, 1)
                elif n == 1:
                    dve.wait_ge(dpv, dpvs(1))
                    dpvs.add()
                    settle()
                    dve.tensor_scalar(o_row[:], bank(7)[0:H, 0:KR], dm[0:H, 3:4], None, ALU.mult).then_inc(ch_dve, 1)
                else:
                    dve.wait_ge(ch_pe, turned(2))
                    turned.add(2)
                    dve.tensor_copy(olat[:, :, :, bass.ds(b, 1)], bank(7)[:, 272:272 + KC * H].rearrange(
                        "p (c h o) -> p c h o", c=KC, o=1)).then_inc(olat_r, 1)

            def decode_seq(b, u, prev):
                dve.tensor_copy(l_now[u][:, 0:KC, :], lats[:, :, bass.ds(b, 1)])
                dve.tensor_copy(l_now[u][0:DR, KC, :], kpes[:, bass.ds(b, 1)])
                dve.tensor_copy(q_now[u][:, 0:KC, :].unsqueeze(2), qlat[:, :, bass.ds(b, 1), :])
                dve.tensor_copy(q_now[u][0:DR, KC, :].unsqueeze(1), qpes[:, bass.ds(b, 1), :])
                for g in range(8):
                    dve.wait_ge(kt_mm, groups(1))
                    wait(dve, sc_mm, groups(-1))
                    dve.tensor_copy(kT[g % 2][:, 1, :], bank(3 * (g % 2) + 1)).then_inc(kt_ed, 1)
                    groups.add()
                    if prev is not None and g in (2, 3, 4):
                        chain(g - 2, prev)
                top_all(u)

            turned, dpvs = Tally(), Tally(2)
            settle()
            dve.wait_ge(qlat_r, H)
            decode_seq(0, 0, None)
            decode_seq(1, 1, 0)
            with loop(dve, NS // 2 - 1, {groups: 16, chains: 2, scored: 16, turned: 4, dpvs: 2, steps: 6}) as i:
                b = dve.snap(i * 2 + 1)
                decode_seq(b + 1, 0, b)
                decode_seq(b + 2, 1, b + 1)
            for n in range(3):
                chain(n, NS - 1)
            dve.wait_ge(ov_h, 1)
            dve.tensor_tensor(ovs[:, 1], bank(0)[:, 0:H * NS].rearrange("p (h b) -> p h b", h=H),
                              ovs[:, 0].bitcast(F32), ALU.subtract).then_inc(ov_e, 1)
            split_next(P8)
            down(PARTS8, [(0, KD), (1, KD)], (1, 0), (1, 1))
            f0.add(KQ + H)
            f1.add(KQ)
            ffn(1, P22, 8)
            down(PARTS22, [], (1, 1), None)

        @block.tensor
        def _(pe):
            uses = [Tally() for _ in range(3)]
            f = [Tally(), Tally()]
            stats, acts = Tally(), [Tally() for _ in range(3)]

            def trans(out, in_):
                r = in_.shape[0]
                return pe.transpose(out, in_, ident[0:r, 0:r])

            pe.sem_inc(mod_mm, 2)
            pe.sem_inc(dpv, 2)
            pe.wait_ge(const_ready, 5)
            pe.wait_ge(vec_in, 16 * 11)
            for t, r in enumerate((125, 108, 66, 66)):
                ins = trans(bank(0)[:, t * P:t * P + r], packs[0:r, t, :])
            ins.then_inc(setup_t, 1)
            pe.wait_ge(csil_ready, 1)
            for k in range(KD):
                ins = trans(bank(1)[:, k * MLANES:(k + 1) * MLANES], csil[:, k * P:(k + 1) * P])
            ins.then_inc(setup_t, 1)
            pe.wait_ge(mix_loaded, 16)
            for k in range(KD):
                ins = trans(bank(2)[:, k * 2 * NS:(k + 1) * 2 * NS], mix_in[:, k * P:(k + 1) * P])
            ins.then_inc(setup_t, 1)
            pe.wait_ge(ffn_loaded, 16)
            for l in range(2):
                for k in range(KF):
                    ins = trans(bank(3 + l)[:, k * 2 * NS:(k + 1) * 2 * NS], ffn_in[:, l, k * P:(k + 1) * P])
                ins.then_inc(setup_t, 1)
            pe.wait_ge(x_loaded, 16)
            pe.wait_ge(xs_loaded, 16)
            for n in range(2 * (KT_TOK + 1)):
                t, half = n // 2, n % 2
                wait(pe, xt_e, n - 2)
                for k in range(4):
                    c = (4 * half + k) * P
                    src = x_in[:, t, c:c + P] if t < KT_TOK else xs_in[:, c:c + P]
                    w = P if t < KT_TOK else NS
                    ins = trans(bank(5 + n % 3)[:, k * P:k * P + w], src)
                ins.then_inc(xt_t, 1)
            pe.wait_ge(setup_e, 2)
            mods, evacs, turns = [Tally(), Tally()], Tally(), Tally()

            def mod_product(b):
                mods[b].add(16)
                pe.wait_ge(mod_loaded[b], mods[b]())
                wait(pe, mrow_e, evacs(-1))
                evacs.add()
                for k in range(KD):
                    ins = pe.matmul(bank(b)[0:MLANES, :], csT[:, k, :], mod_raw[b][:, k, :],
                                    start=k == 0, stop=k == KD - 1)
                ins.then_inc(mod_mm, 1)

            def mod_turn(b):
                pe.wait_ge(mrow_e, turns(1))
                wait(pe, mod_done, turns(-1))
                turns.add()
                for m in range(4):
                    ins = pe.matmul(bank(2 + b)[:, m * MLANES:(m + 1) * MLANES], mrow[b][:, m * P:(m + 1) * P],
                                    ident[0:MLANES, 0:MLANES], start=True, stop=True)
                ins.then_inc(mod_t, 1)

            mod_product(0)
            mod_product(1)
            mod_turn(0)
            mod_product(0)
            mod_turn(1)
            mod_product(1)
            mod_turn(0)
            with loop(pe, 2 * MODS - 2, {mods[0]: 16, mods[1]: 16, evacs: 2, turns: 2}):
                mod_product(0)
                mod_turn(1)
                mod_product(1)
                mod_turn(0)
            mod_turn(1)

            def stat(src, out):
                pe.wait_ge(ss_ready, stats(1))
                stats.add()
                for o, r in zip(out, src):
                    ins = pe.matmul(o, ones[:], r, start=True, stop=True)
                ins.then_inc(stat_ready, 1)

            def stat_chunk():
                stat([rs[:]], [bank(6)[:, 0:DC]])

            for d in range(ND):
                stat_chunk()

            def product(slot, ks, rhs, outs_, first=True, last=True):
                pe.wait_ge(w_ready[slot], uses[slot](1))
                uses[slot].add()
                for o, (hi, lo) in zip(outs_, rhs):
                    for n, k in enumerate(ks):
                        f_, l_ = first and n == 0, last and n == len(ks) - 1
                        pe.matmul(o, w_hi[slot][:, n, :], hi(k), start=f_, stop=False)
                        pe.matmul(o, w_hi[slot][:, n, :], lo(k), start=False, stop=False)
                        ins = pe.matmul(o, w_lo[slot][:, n, :], hi(k), start=False, stop=l_)
                ins.then_inc(w_done[slot], 1)

            def wide(hi, lo):
                return [(lambda k, c=c: hi[:, k, c * UC:(c + 1) * UC], lambda k, c=c: lo[:, k, c * UC:(c + 1) * UC])
                        for c in range(NU)]

            def up_product(slot, s, kt=KD, hi=None, lo=None):
                wait(pe, set_free[s], f[s]())
                f[s].add()
                product(slot, range(kt), wide(hi or h_hi, lo or h_lo), [upset(s)[:, c, :] for c in range(NU)])

            def down(parts, norm_next, tail_tiles=0):
                def pair(m, start):
                    for u in range(2):
                        wait(pe, act_step, evs(1 + u - DOWN_AGO[m + u]))
                    evs.add(2)
                    if m == 6 and tail_tiles:
                        pe.wait_ge(tail_e, tail_tiles)
                    for m_, n, s, k0, k1 in down_steps(parts):
                        if m_ // 2 == m // 2:
                            if start and m_ == m:
                                acts[n].add(32)
                                pe.wait_ge(act_in[n], acts[n]())
                            product(s, range(k0, k1), [(lambda k: act_hi[:, k, :], lambda k: act_lo[:, k, :])],
                                    [bank(DOWN_BANK[m_])[:, 0:DC]], n == 0, n == len(parts) - 1)

                def chunk(prev):
                    pair(0, True)
                    if prev:
                        stat_chunk()
                    pair(2, False)
                    if prev and norm_next:
                        stat_chunk()
                    pair(4, False)
                    pair(6, False)

                chunk(False)
                per = {uses[s]: KD for s in range(len(parts))}
                per.update({acts[n]: 32 for n in range(len(parts))})
                per.update({evs: KD, stats: 2 if norm_next else 1})
                with loop(pe, ND - 1, per):
                    chunk(True)
                stat_chunk()
                if norm_next:
                    stat_chunk()

            evs = Tally()

            def tails(kt, n):
                pe.wait_ge(tail_ready, n)
                for g in range(-(-kt // 4)):
                    if g >= 2:
                        pe.wait_ge(tail_e, te[0] + g - 1)
                    for k in range(4 * g, min(kt, 4 * g + 4)):
                        ins = trans(bank(6 + g % 2)[0:TAIL, (k % 4) * P:(k % 4 + 1) * P], tail[:, k, :])
                    ins.then_inc(tail_t_done, 1)
                te[0] += -(-kt // 4)

            te = [0]

            pe.wait_ge(h_ready, ND)

            def triple(par):
                up_product(0, par)
                up_product(1, 1 - par)
                up_product(2, par)

            triple(0)
            triple(1)
            with loop(pe, KD // 2 - 1, {uses[0]: 2, uses[1]: 2, uses[2]: 2, f[0]: 3, f[1]: 3}):
                triple(0)
                triple(1)
            tails(KD, 1)
            down(PARTS8, True, te[0])

            def ffn(n):
                pe.wait_ge(h_ready, n)
                with loop(pe, KF, {uses[0]: 1, uses[1]: 1, f[0]: 1, f[1]: 1}):
                    up_product(0, 0)
                    up_product(1, 1)

            ffn(2 * ND)
            tails(KF, 2)
            down(PARTS22, True, te[0])
            pe.wait_ge(h_ready, 3 * ND)
            for m in range(KQ + KC + 1):
                up_product(m % 3, m % 2)
            pe.wait_ge(set_free[0], f[0]())
            for _ in range(2):
                stat([rsm[:, c * UC:(c + 1) * UC] for c in range(NU)], [upset(0)[:, c, :] for c in range(NU)])
            pe.wait_ge(lat_r, 1)
            pe.wait_ge(kpe_r, 1)
            for t in range(KT_TOK + 1):
                n = P if t < KT_TOK else NS
                wait(pe, tok_e, t - 1)
                for c in range(KC):
                    trans(bank(6 + t % 2)[0:n, c * P:(c + 1) * P], latn[:, c, t * P:t * P + n])
                trans(bank(6 + t % 2)[0:n, KR:KR + DR], kpe[:, t * P:t * P + n]).then_inc(tok_t, 1)

            pe.wait_ge(tok_e, KT_TOK + 1)
            pe.wait_ge(qn_r, 1)
            hq, h1, h2, h3, h8 = Tally(), Tally(), Tally(), Tally(), Tally()

            def head(first):
                if not first:
                    pe.wait_ge(e_ready, h8())
                    pe.wait_ge(p_t_e, h8())
                product(0, range(KQ), wide(qn_hi, qn_lo), [upset(0)[:, c, :] for c in range(NU)])
                product(1, range(KQ), wide(qn_hi, qn_lo), [upset(1)[:, c, :] for c in range(NU)])
                hq.add(16)
                pe.wait_ge(kvb_in, hq())
                if not first:
                    pe.wait_ge(pv_e, h2())
                for c in range(2):
                    for k in range(KC):
                        ins = pe.matmul(bank(6 + c), kvb[:, k, 0:DN], latn[:, k, c * 512:(c + 1) * 512],
                                        start=k == 0, stop=k == KC - 1)
                ins.then_inc(kv_mm, 1)
                fq.add()
                pe.wait_ge(set_free[0], fq())
                for t in range(KT_TOK):
                    for k in range(KC):
                        ins = pe.matmul(bank(t // 4)[:, (t % 4) * P:(t % 4 + 1) * P], latn[:, k, t * P:(t + 1) * P],
                                        kvb[:, k, DN:DN + DV], start=k == 0, stop=k == KC - 1)
                ins.then_inc(kv_mm, 1)
                for k in range(KC):
                    ins = trans(bank(2)[:, k * P:(k + 1) * P], kvb[:, k, 0:DN])
                ins.then_inc(kv_mm, 1)
                h1.add()
                pe.wait_ge(qpe_r, h1())
                pe.wait_ge(kv_e, h3(3))
                for k in range(KC):
                    ins = pe.matmul(bank(5)[:, k * NS:(k + 1) * NS], wkT[:, k, :], qno[:, TP:T], start=True, stop=True)
                ins.then_inc(kv_mm, 1)
                h3.add(3)

                def scores(q):
                    u = q % 2
                    if q >= 2:
                        pe.wait_ge(e_ready, h8(q - 1))
                    for b in range(q // 4 + 1):
                        n = min(512, (q + 1) * P - b * 512)
                        keys = slice(b * 512, b * 512 + n)
                        diag = b == q // 4
                        pe.matmul(bank(2 * u + b)[:, 0:n], qno[:, q * P:(q + 1) * P], kno[:, keys],
                                  start=True, stop=False)
                        if diag:
                            pe.matmul(bank(2 * u + b)[:, n - P:n], ident_b[:], mask_b[:], start=False, stop=False,
                                      skip_group_check=True)
                        ins = pe.matmul(bank(2 * u + b)[:, 0:n], qpe[:, q * P:(q + 1) * P], kpe[:, keys],
                                        start=False, stop=True)
                    ins.then_inc(s_mm, 1)

                def turn(q):
                    pe.wait_ge(p_ready, h8(q + 1))
                    if q == 0:
                        pe.wait_ge(qlat_r, h1())
                    else:
                        pe.wait_ge(p_t_e, h8(q))
                    for k in range(q + 1):
                        ins = trans(bank(4 + k // 4)[:, (k % 4) * P:(k % 4 + 1) * P], p_sb[q % 2][:, k * P:(k + 1) * P])
                    ins.then_inc(p_t_mm, 1)

                def values(half):
                    pe.wait_ge(p_t_e, h8(4 * half + 4))
                    n = 4 * half + 4
                    for k in range(n):
                        c = max(0, k - 4 * half) * P
                        ins = pe.matmul(bank(6 + half)[:, c:512], v_sb[:, k, :], p_t[:, k, c:512], start=k == 0,
                                        stop=k >= 4 * half, skip_group_check=True)
                    ins.then_inc(pv_mm, 1)

                scores(0)
                for q in range(1, KT_TOK):
                    scores(q)
                    turn(q - 1)
                    if q == 4:
                        values(0)
                turn(KT_TOK - 1)
                values(1)
                h8.add(8)
                h2.add(2)

            fq = Tally(SETS + 3)
            head(True)
            with loop(pe, H - 1, {uses[0]: 1, uses[1]: 1, hq: 16, h1: 1, h2: 2, h3: 3, h8: 8, fq: 1}):
                head(False)
            pe.wait_ge(qlat_r, H)

            pe.wait_ge(pv_e, 2 * H)
            groups, olats, seqs = Tally(), Tally(), Tally()
            pages, ropes, vns = [Tally(), Tally()], [Tally(), Tally()], [Tally(), Tally()]

            def decode_scores(g, u):
                pe.wait_ge(kt_ea, groups())
                pe.wait_ge(kt_ed, groups())
                wait(pe, sc_e, groups(-1))
                for k in range(KC):
                    pe.matmul(bank(6)[0:H, :], q_now[u][:, k, :], kT[g % 2][:, k, :], start=k == 0, stop=False)
                pe.matmul(bank(6)[0:H, :], q_now[u][0:DR, KC, :], kT[g % 2][0:DR, 2, :], start=False, stop=True
                          ).then_inc(sc_mm, 1)

            def decode_chain(n, u):
                if n == 0:
                    pe.wait_ge(ch_act, seqs(1))
                    pe.matmul(bank(7)[:, 0:H], s_row[u][:, 0:P], ident[0:H, 0:H], start=True, stop=True)
                    pe.matmul(bank(7)[0:1, NPG * H:(NPG + 1) * H], s_row[u][:, PAST:PAST + 1], ident[0:H, 0:H],
                              start=True, stop=True)
                    for j in range(1, NPG):
                        ins = trans(bank(7)[:, j * H:(j + 1) * H], s_row[u][:, j * P:(j + 1) * P])
                    ins.then_inc(ch_pe, 1)
                elif n == 1:
                    pe.wait_ge(ch_dve, seqs3(2))
                    vns[u].add(16)
                    pe.wait_ge(vn_in[u], vns[u]())
                    for j in range(NPG):
                        pe.matmul(bank(7)[0:H, 0:KR], e_t[:, j, :], pg[u][:, j, :], start=j == 0, stop=False)
                    pe.matmul(bank(7)[0:H, 0:KR], e_new[:], vnew[u][:], start=False, stop=True).then_inc(dpv, 1)
                else:
                    pe.wait_ge(ch_dve, seqs3(3))
                    for k in range(KC):
                        ins = pe.matmul(bank(7)[:, 272 + k * H:272 + (k + 1) * H], o_row[:, k * P:(k + 1) * P],
                                        ident[0:H, 0:H], start=True, stop=True)
                    ins.then_inc(ch_pe, 1)
                    seqs.add()
                    seqs3.add(3)

            def decode_seq(u, prev):
                pages[u].add(16 * NPG // 4)
                ropes[u].add(16 * NPG)
                pe.wait_ge(pgr_in[u], ropes[u]())
                for g in range(8):
                    if g % 2 == 0:
                        pe.wait_ge(pg_in[u][g // 2], pages[u]())
                    wait(pe, kt_ea, groups(-1))
                    wait(pe, kt_ed, groups(-1))
                    b0 = 3 * (g % 2)
                    for n in range(4):
                        for k in range(KC):
                            trans(bank(b0 + k)[:, n * P:(n + 1) * P], pg[u][:, 4 * g + n, k * P:(k + 1) * P])
                        ins = trans(bank(b0 + 2)[0:DR, n * P:(n + 1) * P], pgr[u][:, 4 * g + n, :])
                    ins.then_inc(kt_mm, 1)
                    if g:
                        decode_scores(g - 1, u)
                    if prev and g in (2, 3, 4):
                        decode_chain(g - 2, 1 - u)
                    groups.add()
                decode_scores(7, u)
                wait(pe, olat_r, olats())
                olats.add()
                for k in range(KC):
                    pe.matmul(bank(7)[0:H, 500:501], q_now[u][:, k, :], l_now[u][:, k, :],
                              start=k == 0, stop=False)
                pe.matmul(bank(7)[0:H, 500:501], q_now[u][0:DR, KC, :], l_now[u][0:DR, KC, :],
                          start=False, stop=True).then_inc(sn_mm, 1)

            seqs3 = Tally()
            decode_seq(0, False)
            decode_seq(1, True)
            with loop(pe, NS // 2 - 1, {groups: 16, olats: 2, seqs: 2, seqs3: 6, pages[0]: 128, pages[1]: 128,
                                        ropes[0]: 512, ropes[1]: 512, vns[0]: 16, vns[1]: 16}):
                decode_seq(0, True)
                decode_seq(1, True)
            for n in range(3):
                decode_chain(n, 1)
            pe.wait_ge(wv_in, 32)
            pe.wait_ge(olat_r, NS)
            for h in range(H):
                for k in range(KC):
                    ins = pe.matmul(bank(0)[:, h * NS:(h + 1) * NS], wv[:, k, h, :], olat[:, k, h, :],
                                    start=k == 0, stop=k == KC - 1)
            ins.then_inc(ov_mm, 1)
            down(PARTS8, True)
            f[0].add(H)
            ffn(4 * ND)
            tails(KF, 3)
            down(PARTS22, False, te[0])
            pe.wait_ge(x_done, 5 * ND)
            for n in range(2 * (KT_TOK + 1)):
                t, half = n // 2, n % 2
                wait(pe, yt_e, n - 3)
                w = P if t < KT_TOK else NS
                for k in range(4):
                    ins = trans(bank(n % 4)[0:w, k * P:(k + 1) * P], xT[:, 4 * half + k, t * P:t * P + w])
                ins.then_inc(yt_mm, 1)


_INS = ["x_prompt", "x_sample", "cache_kv_latent", "cache_k_rope", "state_mixconv", "state_ffnconv", "page_table",
        "c_prompt", "c_sample", "mod_w", "mod_b", "norm_mix_pre", "norm_mix_post", "norm_ffn_pre", "norm_ffn_post",
        "sc_w_in", "sc_conv_w", "sc_w_out", "mla_w_qa", "mla_qa_norm", "mla_w_qb", "mla_w_kva", "mla_kv_norm",
        "mla_w_kvb", "mla_w_o", "ffn_w_in", "ffn_conv_w", "ffn_conv_b", "ffn_w_out"]
_FLAT = {"x_prompt", "cache_kv_latent", "cache_k_rope", "state_mixconv", "sc_w_in", "sc_conv_w", "sc_w_out",
         "mla_w_qa", "mla_w_qb", "mla_w_kva", "mla_w_kvb", "mla_w_o"}
_OUTS = [("y_prompt", (TP, D)), ("y_sample", (NS, D)), ("lat_p", (TP, KR)), ("pe_p", (TP, DR)), ("lat_s", (NS, KR)),
         ("pe_s", (NS, DR)), ("mix_p", (2, D)), ("mix_s", (NS, 2, D)), ("ffn_p", (2, 2, F)), ("ffn_s", (2, NS, 2, F))]
_SHAPES = [(1, TP, D), (NS, 1, D), (1, 1, TP, KR), (1, 1, TP, DR), (1, NS, 1, KR), (1, NS, 1, DR), (1, 1, 2, D),
           (1, NS, 2, D), (2, 1, 2, F), (2, NS, 2, F)]


def rope_table():
    half = DR // 2
    inv = (10000.0 ** (-np.arange(half) * 2.0 / DR)).astype(np.float32)
    pos = np.concatenate([np.arange(TP), np.full(NS, PAST)]).astype(np.float32)
    ang = (inv[:, None] * pos[None, :]).astype(np.float32)
    cos, sin = np.cos(ang), np.sin(ang)
    return np.ascontiguousarray(np.concatenate([cos, cos, -sin, sin]).astype(np.float32))


def kernel(**inputs):
    import concourse.bacc as bacc
    from concourse.bass_utils import run_bass_kernel_spmd

    nc = bacc.Bacc("TRN2", target_bir_lowering=False, num_devices=1)
    arrays, ins, outs = {}, [], []
    for name in _INS:
        a = np.ascontiguousarray(inputs[name])
        if name in _FLAT:
            a = a[0]
        elif name == "x_sample":
            a = a[:, 0]
        arrays[f"in_{name}"] = a
        ins.append(nc.dram_tensor(f"in_{name}", a.shape, mybir.dt.from_np(a.dtype), kind="ExternalInput").ap())
    arrays["in_rope"] = rope_table()
    ins.append(nc.dram_tensor("in_rope", (P, T), F32, kind="ExternalInput").ap())
    for name, shape in _OUTS:
        outs.append(nc.dram_tensor(f"out_{name}", shape, F32, kind="ExternalOutput").ap())
    build(nc, ins, outs)
    r = run_bass_kernel_spmd(nc, [arrays], core_ids=[0])
    return tuple(r.results[0][f"out_{name}"].reshape(s) for (name, _), s in zip(_OUTS, _SHAPES))
```
